# Optimizing a Trainium2 kernel written in Bass

```python
import jax, jax.numpy as jnp
from jax import lax
import numpy as np

D_MODEL = 1024
BATCH = 1
SEQ = 256
DEPTH = 2

D_FF = 2816
CHUNK = 128
A_GROUPS = 8
A_GROUP_DIM = 128
A_WIDTH = A_GROUPS * A_GROUP_DIM
B_HEAD_DIM = 64
B_WIDTH = D_MODEL
B_HEADS = B_WIDTH // B_HEAD_DIM
DECAY_LORA = 64
AAA_LORA = 64
MV_LORA = 32
GATE_WIDTH = 2 * D_MODEL
SHIFT_WIDTH_FIRST = 3 * B_WIDTH + DECAY_LORA + AAA_LORA
SHIFT_WIDTH_REST = SHIFT_WIDTH_FIRST + MV_LORA
IN_WIDTH_FIRST = GATE_WIDTH + 2 * A_WIDTH + SHIFT_WIDTH_FIRST
IN_WIDTH_REST = GATE_WIDTH + 2 * A_WIDTH + SHIFT_WIDTH_REST

NORM_EPS = 1e-6
LN_EPS = 1e-5
GN_EPS = 64e-5


def rms_norm(x, g):
    xf = x.astype(jnp.float32)
    xf = xf * lax.rsqrt(jnp.mean(xf * xf, axis=-1, keepdims=True) + NORM_EPS)
    return (xf * g).astype(x.dtype)

def layer_norm(x, g, b):
    xf = x.astype(jnp.float32)
    mu = jnp.mean(xf, axis=-1, keepdims=True)
    var = jnp.mean(jnp.square(xf - mu), axis=-1, keepdims=True)
    return ((xf - mu) * lax.rsqrt(var + LN_EPS) * g + b).astype(x.dtype)

def swiglu_ffn(h, w_gu, w_down):
    gate, up = jnp.split(h @ w_gu, 2, axis=-1)
    return (jax.nn.silu(gate) * up) @ w_down

def token_shift_mix(p, mu):
    prev = jnp.pad(p, ((0, 0), (1, 0), (0, 0)))[:, :-1]
    return p + mu * (prev - p)

def chunked_sgu(u, v, ln_g, ln_b, w_s, b_s):
    u = jax.nn.gelu(u)
    v = layer_norm(jax.nn.gelu(v), ln_g, ln_b)
    bsz, t, _ = v.shape
    vc = v.reshape(bsz, t // CHUNK, CHUNK, A_GROUPS, A_GROUP_DIM)
    causal = jnp.tril(jnp.ones((CHUNK, CHUNK), dtype=bool))
    ws = jnp.where(causal, w_s, 0)
    s = jnp.einsum('gts,bcsgd->bctgd', ws, vc) + b_s.T[:, :, None]
    return u * s.reshape(bsz, t, A_WIDTH)

def rwkv7_time_mix(p, v_first, w0, w2, a0, a2, k_k, k_a, r_k, gn_g, gn_b, v0, v2):
    out_dtype = p.dtype
    p = p.astype(jnp.float32)
    bsz, t, _ = p.shape
    r = p[..., :B_WIDTH]
    k = p[..., B_WIDTH:2 * B_WIDTH]
    v = p[..., 2 * B_WIDTH:3 * B_WIDTH]
    off = 3 * B_WIDTH
    w_down = p[..., off:off + DECAY_LORA]
    off += DECAY_LORA
    a_down = p[..., off:off + AAA_LORA]
    off += AAA_LORA
    log_w = -jax.nn.softplus(-(w0 + jnp.tanh(w_down) @ w2)) - 0.5
    decay = jnp.exp(-jnp.exp(log_w))
    a = jax.nn.sigmoid(a0 + a_down @ a2)
    if v_first is None:
        v_first = v
    else:
        v_res_down = p[..., off:off + MV_LORA]
        v = v + (v_first - v) * jax.nn.sigmoid(v0 + v_res_down @ v2)

    def heads(z):
        return z.reshape(bsz, t, B_HEADS, B_HEAD_DIM)

    kk = heads(k * k_k)
    kk = kk / jnp.maximum(jnp.sqrt(jnp.sum(kk * kk, axis=-1, keepdims=True)), 1e-12)
    k = k * (1 + (a - 1) * k_a)
    r, k, v, decay, a = heads(r), heads(k), heads(v), heads(decay), heads(a)

    def time_major(z):
        return jnp.swapaxes(z, 0, 1)

    def step(state, inp):
        r_t, w_t, k_t, v_t, kk_t, a_t = inp
        sa = jnp.einsum('bhvk,bhk->bhv', state, kk_t)
        state = (state * w_t[:, :, None, :]
                 - sa[..., None] * (kk_t * a_t)[:, :, None, :]
                 + v_t[..., None] * k_t[:, :, None, :])
        return state, jnp.einsum('bhvk,bhk->bhv', state, r_t)

    state0 = jnp.zeros((bsz, B_HEADS, B_HEAD_DIM, B_HEAD_DIM), jnp.float32)
    _, y = lax.scan(step, state0, (time_major(r), time_major(decay), time_major(k),
                                   time_major(v), time_major(kk), time_major(a)))
    y = jnp.swapaxes(y, 0, 1)
    mu = jnp.mean(y, axis=-1, keepdims=True)
    var = jnp.mean(jnp.square(y - mu), axis=-1, keepdims=True)
    y = (y - mu) * lax.rsqrt(var + GN_EPS)
    y = y.reshape(bsz, t, B_WIDTH) * gn_g + gn_b
    bonus = jnp.sum(r * k * r_k, axis=-1, keepdims=True) * v
    y = y + bonus.reshape(bsz, t, B_WIDTH)
    return y.astype(out_dtype), v_first

def first_inputs(seed: int = 0) -> dict:
    key = jax.random.key(seed)
    ks = iter(jax.random.split(key, 40))
    nrm = lambda shape, s: jax.random.normal(next(ks), shape, jnp.float32) * s
    gain = lambda shape: 1.0 + nrm(shape, 0.02)
    nr = max(DEPTH - 1, 0)
    return {
        "x": nrm((BATCH, SEQ, D_MODEL), 1.0),
        "w_in_first": nrm((D_MODEL, IN_WIDTH_FIRST), D_MODEL ** -0.5),
        "mu_first": jax.random.uniform(next(ks), (SHIFT_WIDTH_FIRST,), jnp.float32),
        "w_in_rest": nrm((nr, D_MODEL, IN_WIDTH_REST), D_MODEL ** -0.5),
        "mu_rest": jax.random.uniform(next(ks), (nr, SHIFT_WIDTH_REST), jnp.float32),
        "rwkv_v0": 1.0 + nrm((nr, B_WIDTH), 0.1),
        "rwkv_v2": nrm((nr, MV_LORA, B_WIDTH), 0.5 * MV_LORA ** -0.5),
        "ffn1_norm": gain((DEPTH, D_MODEL)),
        "ffn1_w_gu": nrm((DEPTH, D_MODEL, 2 * D_FF), D_MODEL ** -0.5),
        "ffn1_w_down": nrm((DEPTH, D_FF, D_MODEL), D_FF ** -0.5),
        "mix_norm": gain((DEPTH, D_MODEL)),
        "sgu_ln_g": gain((DEPTH, A_WIDTH)),
        "sgu_ln_b": nrm((DEPTH, A_WIDTH), 0.02),
        "sgu_w_s": nrm((DEPTH, A_GROUPS, CHUNK, CHUNK), CHUNK ** -0.5),
        "sgu_b_s": 1.0 + nrm((DEPTH, A_GROUPS, CHUNK), 0.02),
        "rwkv_w0": jax.random.uniform(next(ks), (DEPTH, B_WIDTH), jnp.float32, -5.0, 0.0),
        "rwkv_w2": nrm((DEPTH, DECAY_LORA, B_WIDTH), 0.5 * DECAY_LORA ** -0.5),
        "rwkv_a0": nrm((DEPTH, B_WIDTH), 0.1),
        "rwkv_a2": nrm((DEPTH, AAA_LORA, B_WIDTH), 0.5 * AAA_LORA ** -0.5),
        "rwkv_k_k": 0.85 + nrm((DEPTH, B_WIDTH), 0.02),
        "rwkv_k_a": gain((DEPTH, B_WIDTH)),
        "rwkv_r_k": nrm((DEPTH, B_HEADS, B_HEAD_DIM), 0.1),
        "rwkv_gn_g": gain((DEPTH, B_WIDTH)),
        "rwkv_gn_b": nrm((DEPTH, B_WIDTH), 0.02),
        "w_proj_a": nrm((DEPTH, A_WIDTH, D_MODEL), A_WIDTH ** -0.5),
        "w_proj_b": nrm((DEPTH, B_WIDTH, D_MODEL), B_WIDTH ** -0.5),
        "w_out": nrm((DEPTH, D_MODEL, D_MODEL), D_MODEL ** -0.5),
        "ffn2_norm": gain((DEPTH, D_MODEL)),
        "ffn2_w_gu": nrm((DEPTH, D_MODEL, 2 * D_FF), D_MODEL ** -0.5),
        "ffn2_w_down": nrm((DEPTH, D_FF, D_MODEL), D_FF ** -0.5),
        "final_norm": gain((D_MODEL,)),
    }

def first_block(x, w_in_first, mu_first, w_in_rest, mu_rest, rwkv_v0, rwkv_v2,
              ffn1_norm, ffn1_w_gu, ffn1_w_down, mix_norm,
              sgu_ln_g, sgu_ln_b, sgu_w_s, sgu_b_s,
              rwkv_w0, rwkv_w2, rwkv_a0, rwkv_a2, rwkv_k_k, rwkv_k_a, rwkv_r_k,
              rwkv_gn_g, rwkv_gn_b, w_proj_a, w_proj_b, w_out,
              ffn2_norm, ffn2_w_gu, ffn2_w_down, final_norm):
    v_first = None
    for layer in range(DEPTH):
        h = rms_norm(x, ffn1_norm[layer])
        x = x + 0.5 * swiglu_ffn(h, ffn1_w_gu[layer], ffn1_w_down[layer])

        h = rms_norm(x, mix_norm[layer])
        if layer == 0:
            p = h @ w_in_first
            mu = mu_first
            v0, v2 = None, None
        else:
            p = h @ w_in_rest[layer - 1]
            mu = mu_rest[layer - 1]
            v0, v2 = rwkv_v0[layer - 1], rwkv_v2[layer - 1]
        gate_a = p[..., :D_MODEL]
        gate_b = p[..., D_MODEL:GATE_WIDTH]
        u_a = p[..., GATE_WIDTH:GATE_WIDTH + A_WIDTH]
        v_a = p[..., GATE_WIDTH + A_WIDTH:GATE_WIDTH + 2 * A_WIDTH]
        p_b = token_shift_mix(p[..., GATE_WIDTH + 2 * A_WIDTH:], mu)

        y_a = chunked_sgu(u_a, v_a, sgu_ln_g[layer], sgu_ln_b[layer],
                          sgu_w_s[layer], sgu_b_s[layer])
        y_b, v_first = rwkv7_time_mix(p_b, v_first, rwkv_w0[layer], rwkv_w2[layer],
                                      rwkv_a0[layer], rwkv_a2[layer], rwkv_k_k[layer],
                                      rwkv_k_a[layer], rwkv_r_k[layer],
                                      rwkv_gn_g[layer], rwkv_gn_b[layer], v0, v2)

        merged = (jax.nn.sigmoid(gate_a) * (y_a @ w_proj_a[layer])
                  + jax.nn.sigmoid(gate_b) * (y_b @ w_proj_b[layer]))
        x = x + merged @ w_out[layer]

        h = rms_norm(x, ffn2_norm[layer])
        x = x + 0.5 * swiglu_ffn(h, ffn2_w_gu[layer], ffn2_w_down[layer])
    return rms_norm(x, final_norm)


_first_inputs = first_inputs


def first_inputs(seed=0):
    import zlib

    import numpy as np

    out = dict(_first_inputs(seed))
    spreads = {}
    factors = {'rwkv_v0': 4.014,
     'ffn1_norm': 3.79,
     'sgu_ln_g': 8.0,
     'sgu_ln_b': 8.0,
     'sgu_b_s': 6.744,
     'rwkv_w2': 2.703,
     'rwkv_k_k': 6.91,
     'rwkv_k_a': 4.169,
     'rwkv_gn_g': 4.428,
     'rwkv_gn_b': 4.558,
     'ffn2_norm': 5.868,
     'final_norm': 2.77}
    for name, (base, spread) in spreads.items():
        noise = np.random.default_rng([zlib.crc32(name.encode()), seed]).standard_normal(out[name].shape)
        drawn = base * np.exp(spread * noise) if base else spread * noise
        out[name] = __import__('jax').numpy.asarray(drawn.astype(out[name].dtype))
    for name, factor in factors.items():
        out[name] = (out[name] * factor).astype(out[name].dtype)
    return out


_narrow_inputs = first_inputs


def first_inputs(seed=0):

    out = dict(_narrow_inputs(seed))
    wider = {'rwkv_v0': 12.0,
     'rwkv_v2': 12.0,
     'sgu_ln_g': 5.88,
     'sgu_ln_b': 5.92,
     'sgu_b_s': 4.65,
     'rwkv_k_k': 7.89,
     'rwkv_gn_g': 4.7,
     'rwkv_gn_b': 4.82,
     'final_norm': 3.11}
    for name, times in wider.items():
        mean = out[name].mean()
        out[name] = (mean + times * (out[name] - mean)).astype(out[name].dtype)
    return out


N_MIXERS = 2
HEAD_DIM = 64
FOX_HEADS = D_MODEL // HEAD_DIM
DIL_HEADS = D_MODEL // HEAD_DIM
DIL_CONFIGS = ((128, 1), (512, 4), (2048, 16))
N_DIL_GROUPS = len(DIL_CONFIGS)
ROPE_THETA = 500000.0
ROPE_DIM = HEAD_DIM // 4
Q_BLOCK = 128
EPS = 1e-6
MACARON_WEIGHT = 0.5
N_SUBLAYERS = 3
N_FOX_LAYERS = (DEPTH + 1) // 2
N_DIL_LAYERS = DEPTH // 2
FOX_IN = 3 * FOX_HEADS * HEAD_DIM + FOX_HEADS
DIL_IN = N_DIL_GROUPS * 3 * DIL_HEADS * HEAD_DIM


def rms_norm_2(x, g):
    xf = x.astype(jnp.float32)
    y = xf * lax.rsqrt(jnp.mean(xf * xf, axis=-1, keepdims=True) + EPS)
    return (y * g.astype(jnp.float32)).astype(x.dtype)

def modulate(h, shift, scale):
    return h * (1.0 + scale[:, None, :]) + shift[:, None, :]

def swiglu(h, w_gate, w_up, w_down):
    return (jax.nn.silu(h @ w_gate) * (h @ w_up)) @ w_down

def rope_tables(positions):
    half = ROPE_DIM // 2
    inv_freq = ROPE_THETA ** (-(jnp.arange(half, dtype=jnp.float32) * 2.0 / ROPE_DIM))
    ang = positions.astype(jnp.float32)[..., None] * inv_freq
    return jnp.cos(ang)[:, :, None, :], jnp.sin(ang)[:, :, None, :]

def apply_rope(x, cos, sin):
    half = ROPE_DIM // 2
    xr = x[..., :ROPE_DIM].astype(jnp.float32)
    x1, x2 = xr[..., :half], xr[..., half:]
    rot = jnp.concatenate([x1 * cos - x2 * sin, x2 * cos + x1 * sin], axis=-1).astype(x.dtype)
    return jnp.concatenate([rot, x[..., ROPE_DIM:]], axis=-1)

def fox_attention(h, w_in, b_f, q_gain, k_gain, w_out):
    B, S, _ = h.shape
    H, hd = FOX_HEADS, HEAD_DIM
    proj = h @ w_in
    qkv = proj[..., : 3 * H * hd].reshape(B, S, 3, H, hd)
    f_logit = proj[..., 3 * H * hd:].astype(jnp.float32) + b_f.astype(jnp.float32)
    q = rms_norm_2(qkv[:, :, 0], q_gain).transpose(0, 2, 1, 3)
    k = rms_norm_2(qkv[:, :, 1], k_gain).transpose(0, 2, 1, 3)
    v = qkv[:, :, 2].transpose(0, 2, 1, 3)
    cum = jnp.cumsum(jax.nn.log_sigmoid(f_logit), axis=1).transpose(0, 2, 1)
    scale = hd ** -0.5
    outs = []
    for blk in range(S // Q_BLOCK):
        q0 = blk * Q_BLOCK
        kv_len = q0 + Q_BLOCK
        logits = jnp.einsum("bhqd,bhkd->bhqk", q[:, :, q0:kv_len], k[:, :, :kv_len]).astype(jnp.float32) * scale
        logits = logits + cum[:, :, q0:kv_len, None] - cum[:, :, None, :kv_len]
        q_idx = q0 + jnp.arange(Q_BLOCK)
        k_idx = jnp.arange(kv_len)
        mask = k_idx[None, :] <= q_idx[:, None]
        logits = jnp.where(mask[None, None], logits, -jnp.inf)
        p = jax.nn.softmax(logits, axis=-1).astype(v.dtype)
        outs.append(jnp.einsum("bhqk,bhkd->bhqd", p, v[:, :, :kv_len]))
    o = jnp.concatenate(outs, axis=2).transpose(0, 2, 1, 3).reshape(B, S, H * hd)
    return o @ w_out

def dilated_group(q, k, v, window, dilation):
    B, S, H, hd = q.shape
    n_keys = window // dilation + 1
    offsets = dilation * jnp.arange(n_keys)
    scale = hd ** -0.5

    def block_fn(q0):
        qb = lax.dynamic_slice_in_dim(q, q0, Q_BLOCK, axis=1)
        t = q0 + jnp.arange(Q_BLOCK)
        idx = t[:, None] - offsets[None, :]
        valid = idx >= 0
        idx_c = jnp.maximum(idx, 0)
        kb = jnp.take(k, idx_c, axis=1)
        vb = jnp.take(v, idx_c, axis=1)
        logits = jnp.einsum("bqhd,bqkhd->bhqk", qb, kb).astype(jnp.float32) * scale
        logits = jnp.where(valid[None, None], logits, -jnp.inf)
        lse = jax.nn.logsumexp(logits, axis=-1)
        p = jnp.exp(logits - lse[..., None]).astype(v.dtype)
        ob = jnp.einsum("bhqk,bqkhd->bqhd", p, vb)
        return ob, lse

    starts = jnp.arange(S // Q_BLOCK) * Q_BLOCK
    o, lse = lax.map(block_fn, starts)
    o = o.transpose(1, 0, 2, 3, 4).reshape(B, S, H, hd)
    lse = lse.transpose(1, 0, 3, 2).reshape(B, S, H)
    return o, lse

def dilated_attention(h, cos, sin, w_in, q_gain, k_gain, w_out):
    B, S, _ = h.shape
    H, hd = DIL_HEADS, HEAD_DIM
    proj = (h @ w_in).reshape(B, S, N_DIL_GROUPS, 3, H, hd)
    outs, lses = [], []
    for g, (window, dilation) in enumerate(DIL_CONFIGS):
        q = apply_rope(rms_norm_2(proj[:, :, g, 0], q_gain[g]), cos, sin)
        k = apply_rope(rms_norm_2(proj[:, :, g, 1], k_gain[g]), cos, sin)
        o, lse = dilated_group(q, k, proj[:, :, g, 2], window, dilation)
        outs.append(o)
        lses.append(lse)
    alpha = jax.nn.softmax(jnp.stack(lses, axis=0), axis=0)
    o = jnp.sum(alpha[..., None] * jnp.stack(outs, axis=0).astype(jnp.float32), axis=0).astype(h.dtype)
    return o.reshape(B, S, H * hd) @ w_out

def second_inputs(seed: int = 0) -> dict:
    key = jax.random.key(seed)
    ks = jax.random.split(key, 20)
    D = D_MODEL
    nrm = jax.random.normal
    x = nrm(ks[0], (BATCH, SEQ, D), jnp.float32)
    c = nrm(ks[1], (BATCH, D), jnp.float32)
    offs = jax.random.randint(ks[2], (BATCH, 1), 0, 4096, dtype=jnp.int32)
    positions = (offs + jnp.arange(SEQ, dtype=jnp.int32)[None, :]).astype(jnp.int32)
    mod_w = nrm(ks[3], (DEPTH, D, N_SUBLAYERS * 3 * D), jnp.float32) * (0.5 * D ** -0.5)
    mod_b = nrm(ks[4], (DEPTH, N_SUBLAYERS * 3 * D), jnp.float32) * 0.01
    norm_g = 1.0 + 0.02 * nrm(ks[5], (DEPTH, N_SUBLAYERS, D), jnp.float32)
    ffn_w_gate = nrm(ks[6], (DEPTH, 2, D, D_FF), jnp.float32) * D ** -0.5
    ffn_w_up = nrm(ks[7], (DEPTH, 2, D, D_FF), jnp.float32) * D ** -0.5
    ffn_w_down = nrm(ks[8], (DEPTH, 2, D_FF, D), jnp.float32) * D_FF ** -0.5
    fox_w_in = nrm(ks[9], (N_FOX_LAYERS, D, FOX_IN), jnp.float32) * D ** -0.5
    fox_b_f = jax.random.uniform(ks[10], (N_FOX_LAYERS, FOX_HEADS), jnp.float32, 1.0, 6.0)
    fox_q_g = 1.0 + 0.02 * nrm(ks[11], (N_FOX_LAYERS, HEAD_DIM), jnp.float32)
    fox_k_g = 1.0 + 0.02 * nrm(ks[12], (N_FOX_LAYERS, HEAD_DIM), jnp.float32)
    fox_w_out = nrm(ks[13], (N_FOX_LAYERS, FOX_HEADS * HEAD_DIM, D), jnp.float32) * (FOX_HEADS * HEAD_DIM) ** -0.5
    dil_w_in = nrm(ks[14], (N_DIL_LAYERS, D, DIL_IN), jnp.float32) * D ** -0.5
    dil_q_g = 1.0 + 0.02 * nrm(ks[15], (N_DIL_LAYERS, N_DIL_GROUPS, HEAD_DIM), jnp.float32)
    dil_k_g = 1.0 + 0.02 * nrm(ks[16], (N_DIL_LAYERS, N_DIL_GROUPS, HEAD_DIM), jnp.float32)
    dil_w_out = nrm(ks[17], (N_DIL_LAYERS, DIL_HEADS * HEAD_DIM, D), jnp.float32) * (DIL_HEADS * HEAD_DIM) ** -0.5
    return {"x": x, "c": c, "positions": positions, "mod_w": mod_w, "mod_b": mod_b,
            "norm_g": norm_g, "ffn_w_gate": ffn_w_gate, "ffn_w_up": ffn_w_up,
            "ffn_w_down": ffn_w_down, "fox_w_in": fox_w_in, "fox_b_f": fox_b_f,
            "fox_q_g": fox_q_g, "fox_k_g": fox_k_g, "fox_w_out": fox_w_out,
            "dil_w_in": dil_w_in, "dil_q_g": dil_q_g, "dil_k_g": dil_k_g, "dil_w_out": dil_w_out}

def second_block(x, c, positions, mod_w, mod_b, norm_g, ffn_w_gate, ffn_w_up, ffn_w_down,
              fox_w_in, fox_b_f, fox_q_g, fox_k_g, fox_w_out,
              dil_w_in, dil_q_g, dil_k_g, dil_w_out):
    B = x.shape[0]
    D = x.shape[-1]
    cos, sin = rope_tables(positions)
    c_act = jax.nn.silu(c)
    for i in range(DEPTH):
        mod = (c_act @ mod_w[i] + mod_b[i]).reshape(B, N_SUBLAYERS, 3, D)
        shift, scale, gate = mod[:, :, 0], mod[:, :, 1], mod[:, :, 2]
        h = modulate(rms_norm_2(x, norm_g[i, 0]), shift[:, 0], scale[:, 0])
        x = x + MACARON_WEIGHT * gate[:, 0, None, :] * swiglu(h, ffn_w_gate[i, 0], ffn_w_up[i, 0], ffn_w_down[i, 0])
        h = modulate(rms_norm_2(x, norm_g[i, 1]), shift[:, 1], scale[:, 1])
        j = i // N_MIXERS
        if i % N_MIXERS == 0:
            y = fox_attention(h, fox_w_in[j], fox_b_f[j], fox_q_g[j], fox_k_g[j], fox_w_out[j])
        else:
            y = dilated_attention(h, cos, sin, dil_w_in[j], dil_q_g[j], dil_k_g[j], dil_w_out[j])
        x = x + gate[:, 1, None, :] * y
        h = modulate(rms_norm_2(x, norm_g[i, 2]), shift[:, 2], scale[:, 2])
        x = x + MACARON_WEIGHT * gate[:, 2, None, :] * swiglu(h, ffn_w_gate[i, 1], ffn_w_up[i, 1], ffn_w_down[i, 1])
    return x


def setup_inputs(seed=0):
    out = dict(first_inputs(seed))
    for name, value in second_inputs(seed + 1).items():
        if name != "x":
            out[name + "_2"] = value
    return out


def reference(
    x, w_in_first, mu_first, w_in_rest, mu_rest, rwkv_v0, rwkv_v2, ffn1_norm, ffn1_w_gu,
    ffn1_w_down, mix_norm, sgu_ln_g, sgu_ln_b, sgu_w_s, sgu_b_s, rwkv_w0, rwkv_w2, rwkv_a0,
    rwkv_a2, rwkv_k_k, rwkv_k_a, rwkv_r_k, rwkv_gn_g, rwkv_gn_b, w_proj_a, w_proj_b, w_out,
    ffn2_norm, ffn2_w_gu, ffn2_w_down, final_norm, c_2, positions_2, mod_w_2, mod_b_2, norm_g_2,
    ffn_w_gate_2, ffn_w_up_2, ffn_w_down_2, fox_w_in_2, fox_b_f_2, fox_q_g_2, fox_k_g_2,
    fox_w_out_2, dil_w_in_2, dil_q_g_2, dil_k_g_2, dil_w_out_2,
):
    x = first_block(
        x, w_in_first, mu_first, w_in_rest, mu_rest, rwkv_v0, rwkv_v2, ffn1_norm, ffn1_w_gu,
        ffn1_w_down, mix_norm, sgu_ln_g, sgu_ln_b, sgu_w_s, sgu_b_s, rwkv_w0, rwkv_w2, rwkv_a0,
        rwkv_a2, rwkv_k_k, rwkv_k_a, rwkv_r_k, rwkv_gn_g, rwkv_gn_b, w_proj_a, w_proj_b, w_out,
        ffn2_norm, ffn2_w_gu, ffn2_w_down, final_norm,
    )
    return second_block(
        x, c_2, positions_2, mod_w_2, mod_b_2, norm_g_2, ffn_w_gate_2, ffn_w_up_2, ffn_w_down_2,
        fox_w_in_2, fox_b_f_2, fox_q_g_2, fox_k_g_2, fox_w_out_2, dil_w_in_2, dil_q_g_2,
        dil_k_g_2, dil_w_out_2,
    )


_drawn_inputs = setup_inputs


def setup_inputs(seed=0):
    import zlib

    import numpy as np

    out = dict(_drawn_inputs(seed))
    spreads = {}
    factors = {'mod_b_2': 8.0,
     'norm_g_2': 8.0,
     'fox_b_f_2': 2.909,
     'fox_q_g_2': 8.0,
     'fox_k_g_2': 8.0,
     'dil_q_g_2': 8.0,
     'dil_k_g_2': 8.0}
    for name, (base, spread) in spreads.items():
        noise = np.random.default_rng([zlib.crc32(name.encode()), seed]).standard_normal(out[name].shape)
        drawn = base * np.exp(spread * noise) if base else spread * noise
        out[name] = __import__('jax').numpy.asarray(drawn.astype(out[name].dtype))
    for name, factor in factors.items():
        out[name] = (out[name] * factor).astype(out[name].dtype)
    return out
```

```python
import numpy as np
import concourse.bass as bass
from concourse import mybir

F32 = mybir.dt.float32
F32R = mybir.dt.float32r
I32 = mybir.dt.int32
I8 = mybir.dt.int8
ALU = mybir.AluOpType
ACT = mybir.ActivationFunctionType
AX = mybir.AxisListType

P = 128
T = 256
D = 1024
DT = D // P
FF = 2816
FT = FF // P
HEADS = 16
HD = 64
CH = 128
NCH = T // CH
TPU = 16
HALF = TPU // 2
DOWN_UNITS = FT * DT // TPU
FFN_UNITS = FT + DOWN_UNITS
NORM_EPS = 1e-6
LN_EPS = 1e-5
GN_EPS = 64e-5
DECAY_SCALE = float(np.exp(-0.5))
NEG = -1e30
GROUPS = 3
LEVELS = (2, 4, 8, 16, 32, 64)
MOD_UNITS_PER_FFN = 18
MOD_COLS = 2 * MOD_UNITS_PER_FFN
RAW_SLOTS = 3
SPLIT_SLOTS = 4
AHEAD = 3

COL = {}
_at = 0
for _l in range(2):
    for _name, _n in (("ffn1_norm", 8), ("mix_norm", 8), ("ffn2_norm", 8), ("ln_g", 8), ("ln_b", 8),
                      ("mu", 26), ("a0", 8), ("v0", 8), ("k_k", 8), ("k_a", 8), ("r_k", 8),
                      ("gn_g", 8), ("gn_b", 8)):
        COL[_name, _l] = _at
        _at += _n
for _name, _n in (("final_norm", 8), ("norm_g", 48), ("c", 8), ("fox_g", 2), ("dil_g", 6), ("inv_freq", 1)):
    COL[_name] = _at
    _at += _n
NCOLS = _at
COLS_FIRST = COL["norm_g"]

CONST = {}
_at = 0
for _name, _n in (("ident", P), ("mean", P), ("head", P), ("tri", 129), ("mask", 2 * P), ("neg2", P), ("neg2t", P), ("one", 1)):
    CONST[_name] = (_at, _n)
    _at += _n
NCONST = _at


class Plan:

    def __init__(self):
        self.uses = {}
        self.emptied = {"act": 0, "dve": 0}
        self.order = []
        self.unit = {}
        self.units = 0

    def use(self, key, engine):
        self.emptied[engine] += 1
        self.uses[key] = (len(self.order), engine, self.emptied[engine])
        self.order.append(key)

    def stream(self, key, count=1):
        self.unit[key] = self.units
        self.units += count


def make_plan():
    p = Plan()

    def ffn(i):
        p.use(("norm", ffn_norm(i)), "dve")
        p.stream(("ffn", i), FFN_UNITS)
        for j in range(FT):
            p.use(("gu", i, j), "dve")
        for d in range(DT // 2):
            p.use(("down", i, d), "dve")

    for l in range(2):
        ffn(2 * l)
        p.use(("norm", 3 * l + 1), "dve")
        p.stream(("mix", l), 37)
        for s in range(13):
            p.use(("shift", l, s), "act")
        for s in range(4):
            p.use(("z", l, s), "dve")
        for s in range(4):
            p.use(("a", l, s), "act")
        if l:
            for s in range(4):
                p.use(("vr", l, s), "act")
        for s in range(4):
            p.use(("va", l, s), "act")
        for s in range(4):
            p.use(("kk", l, s), "dve")
        for s in range(4):
            p.use(("u", l, s), "act")
        for s in range(4):
            p.use(("bonus", l, s), "dve")
        for s in range(4):
            p.use(("vt", l, s), "act")
        p.use(("vmean", l), "dve")
        p.use(("vvar", l), "dve")
        for s in range(4):
            p.use(("vat", l, s), "act")
        for s in range(4):
            p.use(("sgu", l, s), "dve")
        for c in range(DT):
            p.use(("kbt", l, c), "act")
            p.use(("y", l, c), "act")
        for s in range(4):
            p.use(("gmean", l, s), "dve")
        for s in range(4):
            p.use(("gvar", l, s), "dve")
        for n in range(DT):
            p.use(("gate", l, n), "act")
            p.use(("proj", l, n), "dve")
        p.stream(("out", l), 4)
        for d in range(4):
            p.use(("out", l, d), "dve")
        ffn(2 * l + 1)
    p.use(("norm", 6), "dve")
    for l in range(2):
        ffn(4 + 2 * l)
        p.use(("norm", 8 + 3 * l), "dve")
        p.stream(("mix", 2 + l), (13, 36)[l])
        for g in range((1, 3)[l]):
            for c in range(DT):
                p.use(("qk", l, g, c), "dve")
                if c:
                    p.use(("ss", l, g, c - 1), "dve")
                    if l:
                        p.use(("rot", l, g, c - 1), "dve")
            p.use(("ss", l, g, DT - 1), "dve")
            if l:
                p.use(("rot", l, g, DT - 1), "dve")
            for s in range(4):
                p.use(("v", l, g, s), "act")
        if l == 0:
            p.use(("f", 0), "dve")
        for c in range(DT):
            p.use(("o", l, c), "dve")
        p.stream(("out", 2 + l), 4)
        for d in range(4):
            p.use(("out", 2 + l, d), "dve")
        ffn(5 + 2 * l)
    return p


def ffn_norm(i):
    return (0, 2, 3, 5, 7, 9, 10, 12)[i]


PLAN = make_plan()


def build_program(nc, src, out):
    sem = {}

    def signal(name):
        sem[name] = nc.alloc_semaphore(name)
        return sem[name]

    at = [nc.sbuf_base + (-nc.sbuf_base) % 64]

    def place(name, shape, dt=F32, where=None):
        size = int(np.prod(shape[1:])) * (1 if dt == I8 else 4)
        size += -size % 32
        if where is None:
            where = at[0]
            at[0] += size
        return nc.alloc_sbuf_tensor_at(name, list(shape), dt, offset=where)

    raw = place("raw_units", [P, RAW_SLOTS, TPU * P])
    split = place("split_halves", [P, SPLIT_SLOTS, 2, HALF * P], F32R)
    x = place("x", [P, DT, T])
    h = place("h_split", [P, 2, DT, T], F32R)
    pieces = place("squares", [P, 2, 2, T])
    v_first = place("v_first", [P, DT, T])
    const = place("constants", [P, NCONST])
    level_masks = place("level_masks", [P, 2, len(LEVELS), P], I8)
    cols = place("columns", [P, NCOLS])
    mod = place("modulation", [P, 144])
    mod_b = place("modulation_bias", [P, 144])
    gain2 = place("modulated_gain", [P, 6, DT])
    gate2 = place("residual_gate", [P, 6, DT])
    one_less_ka = place("one_less_ka", [P, 2, DT])
    rstd = place("rstd", [P, T])
    arena = at[0] + (-at[0]) % 64
    KB = 1024

    def over(name, shape, kb, dt=F32):
        return place(name, shape, dt, where=arena + int(kb * KB))

    hidden = over("hidden_split", [P, 2, FT, T], 0, F32R)
    mod_w = over("modulation_units", [P, 2, DT, 2 * P], 44)
    mod_acc = over("modulation_sums", [P, 2, 2 * P], 60)
    silu = over("silu", [P, 3, T], 62)
    product = over("gated", [P, 3, T], 65)
    r_ = over("r", [P, DT, T], 0)
    k_ = over("k", [P, DT, T], 8)
    v_ = over("v", [P, DT, T], 16)
    decay = over("decay", [P, NCH, D], 24)
    a_ = over("a", [P, DT, T], 32)
    kk = over("kk", [P, DT, T], 40)
    va = over("va", [P, DT, T], 48)
    u_ = over("u", [P, DT, T], 56)
    bonus = over("bonus", [P, DT, T], 64)
    lora = over("lora", [P, 2, T], 72)
    ws_t = over("spatial_t", [P, DT, CH], 74)
    B = 78
    raw_shift = over("raw_shift", [P, 2, 2, T + 1], B)
    diff = over("diff", [P, 2, T], B + 4.25)
    w2a2 = over("w2a2", [P, D], B + 6.25)
    v2 = over("v2", [32, D], B + 10.25)
    w0_b = over("w0_rows", [P, D], B + 14.25)
    bs_b = over("bs_rows", [P, D], B + 18.25)
    pair = over("pair", [P, 2, 2, T], B + 22.25)
    e_pos = over("exp_pos", [P, NCH, CH + 1], B)
    e_neg = over("exp_neg", [P, NCH, CH + 1], B + 1.03125)
    ar = over("alpha_rho", [P, NCH, 2 * CH], B + 2.0625)
    beta = over("beta", [P, 2, NCH, CH], B + 4.0625)
    kappa = over("kappa", [P, 2, NCH, CH], B + 6.0625)
    kb0 = over("kappa_beta_0", [P, 2, CH], B + 8.0625)
    gb = over("beta_scores", [P, 4, 2 * CH], B + 9.0625)
    gk = over("kappa_scores", [P, 4, 2 * CH], B + 13.0625)
    t_inv = over("inverse", [P, 4, CH], B + 17.0625)
    q_inv = over("inverse_t", [P, 4, CH], B + 19.0625)
    z_neg = over("z_neg", [P, 4, CH], B + 21.0625)
    rh = over("rhs", [P, P], B + 23.0625)
    nu = over("neg_u", [P, P], B + 23.5625)
    s0 = over("state", [P, P], B + 24.0625)
    kbt = over("kappa_beta_tok", [P, 2, P], B + 24.5625)
    ya_hi = over("ya_hi", [P, DT, T], 48, F32R)
    ya_lo = over("ya_lo", [P, DT, T], 56, F32R)
    yb_hi = over("yb_hi", [P, DT, T], 8, F32R)
    yb_lo = over("yb_lo", [P, DT, T], 0, F32R)
    gate_sig = over("gate_sigmoids", [P, 2, 2, T], 24)
    merged = over("merged", [P, DT, T], 32)
    level_floats = over("level_floats", [P, 2, len(LEVELS), P], 98)
    qk = over("qk", [P, GROUPS, 2 * DT, T], 0)
    vtok = over("v_tokens", [P, GROUPS, NCH, D], 48)
    amask = over("attention_mask", [P, GROUPS, 3 * P], 72)
    logits = over("logits", [P, GROUPS, 3 * P], 76.5)
    pt = over("probs_t", [P, GROUPS, 3 * P], 81)
    cos = over("cos", [P, T], 85.5)
    sin = over("sin", [P, T], 86.5)
    qkg = over("qk_gained", [P, 2, 2, T], 87.5)
    ssr = over("qk_rstd", [P, 2, 2, T], 91.5)
    rot = over("rotated", [P, 2, T], 95.5)
    rope_m = over("rope_matrix", [P, P], 97.5)
    cum_rhs = over("cum_rhs", [P, 2 * P], 98)
    ls = over("log_sigmoid", [P, NCH, HEADS], 99)
    ls_t = over("log_sigmoid_t", [P, NCH, HEADS], 99.125)
    bf_b = over("b_f_rows", [P, HEADS], 99.25)
    ls_b = over("log_sigmoid_b", [P, NCH, P], 99.5)
    stat = over("attention_stats", [P, 16], 100.5)
    pos_i = over("positions", [P, T], 100.625, I32)
    ang = over("angle", [P, T], 101.625)
    o_hi = over("o_hi", [P, DT, T], 0, F32R)
    o_lo = over("o_lo", [P, DT, T], 16, F32R)

    lin = nc.alloc_psum_tensor("linear_banks", [P, 3, 512], F32)
    sv = nc.alloc_psum_tensor("solve_banks", [P, 5, 512], F32)

    def c_(name):
        a, n = CONST[name]
        return const[:, a:a + n]

    ident, mean_w, head_w, tri, mask = (c_(n) for n in ("ident", "mean", "head", "tri", "mask"))

    def col(name, i=0, l=None):
        a = COL[name if l is None else (name, l)] + i
        return cols[:, a:a + 1]

    def wide(ap, n, dim=1):
        return ap.unsqueeze(dim).to_broadcast([P, n, ap.shape[-1]])

    consts_loaded = signal("consts_loaded")
    x_loaded = signal("x_loaded")
    raw_loaded = [signal(f"raw_loaded_{s}") for s in range(RAW_SLOTS)]
    mod_loaded = [signal(f"mod_loaded_{s}") for s in range(2)]
    small_loaded = signal("small_loaded")
    hi_ready = signal("hi_ready")
    lo_ready = signal("lo_ready")
    halves_used = signal("halves_used")
    lin_filled = signal("lin_filled")
    emptied = {"act": signal("emptied_by_act"), "dve": signal("emptied_by_dve")}
    x_normed = signal("x_normed")
    squared = signal("squared")
    piece_used = signal("piece_used")
    dve_step = signal("dve_step")
    act_step = signal("act_step")
    var_ready = signal("var_ready")
    root_ready = signal("root_ready")
    h_temp_ready = signal("h_temp_ready")
    h_hi_ready = signal("h_hi_ready")
    h_ready = signal("h_ready")
    silu_ready = signal("silu_ready")
    hidden_hi = signal("hidden_hi")
    hidden_ready = signal("hidden_ready")
    mod_summed = signal("mod_summed")
    mod_done = signal("mod_done")
    mod_kept = signal("mod_kept")
    c_ready = signal("c_ready")
    mixed = signal("mixed")
    tanh_ready = signal("tanh_ready")
    decay_ready = signal("decay_ready")
    v_done = signal("v_done")
    vf_saved = signal("vf_saved")
    kk_scaled = signal("kk_scaled")
    rk_ready = signal("rk_ready")
    rk_used = signal("rk_used")
    va_centred = signal("va_centred")
    va_ready = signal("va_ready")
    ya_temp = signal("ya_temp")
    ya_hi_ready = signal("ya_hi_ready")
    ya_ready = signal("ya_ready")
    cum_done = signal("cum_done")
    exp_ready = signal("exp_ready")
    scaled = signal("scaled")
    scores_done = signal("scores_done")
    inverse_ready = signal("inverse_ready")
    z_done = signal("z_done")
    z_ready = signal("z_ready")
    p_done = signal("p_done")
    rec_pe = signal("recurrence_products")
    rec_dve = signal("recurrence_kept")
    yb_temp = signal("yb_temp")
    yb_hi_ready = signal("yb_hi_ready")
    yb_ready = signal("yb_ready")
    merged_ready = signal("merged_ready")
    merged_hi = signal("merged_hi")
    merged_split = signal("merged_split")
    qk_gained = signal("qk_gained")
    qk_ready = signal("qk_ready")
    lsb_ready = signal("lsb_ready")
    fexp = signal("fexp")
    logits_done = signal("logits_done")
    max_ready = signal("max_ready")
    probs_ready = signal("probs_ready")
    norm_ready = signal("norm_ready")
    pt_done = signal("pt_done")
    pt_ready = signal("pt_ready")
    o_hi_ready = signal("o_hi_ready")
    o_ready = signal("o_ready")
    angle_ready = signal("angle_ready")
    rope_ready = signal("rope_ready")
    stored = signal("stored")
    masks_ready = signal("masks_ready")
    zeroed = signal("zeroed")

    piece_free = []
    used_pieces = [0]

    def add_piece(last_of=None):
        if last_of is None:
            used_pieces[0] += 1
            piece_free.append((piece_used, used_pieces[0]))
        else:
            piece_free.append((lin_filled, PLAN.uses[last_of][0] + 1))
        return len(piece_free) - 1

    half_free = []
    used_halves = [0]

    def add_half(last_of=None):
        if last_of is None:
            used_halves[0] += 1
            half_free.append((halves_used, used_halves[0]))
        else:
            half_free.append((lin_filled, PLAN.uses[last_of][0] + 1))

    def add_units(keys):
        for key in keys:
            add_half()
            add_half(key)

    def add_ffn(i):
        add_units(("gu", i, j) for j in range(FT))
        for w in range(2 * DOWN_UNITS):
            last = (w + 1) * HALF - 1
            add_half(("down", i, last // (2 * FT)) if (last + 1) % (2 * FT) == 0 else None)

    for l in range(2):
        add_ffn(2 * l)
        add_units([("shift", l, s) for s in range(13)] + [("va", l, s) for s in range(4)]
                  + [("u", l, s) for s in range(4)])
        add_units((k, l, n) for n in range(DT) for k in ("gate", "proj"))
        add_units(("out", l, d) for d in range(4))
        add_ffn(2 * l + 1)
    for l in range(2):
        add_ffn(4 + 2 * l)
        for g in range((1, 3)[l]):
            add_units([("qk", l, g, c) for c in range(DT)] + [("v", l, g, s) for s in range(4)])
        if l == 0:
            add_units([("f", 0)])
        add_units(("out", 2 + l, d) for d in range(4))
        add_ffn(5 + 2 * l)
    assert len(half_free) == 2 * PLAN.units

    PIECE = {}

    def norm_pieces(n):
        for i in range(4):
            PIECE["norm", n, i] = add_piece(("norm", n) if i == 3 else None)

    for b in range(2):
        for l in range(2):
            if b == 0:
                norm_pieces(3 * l)
                norm_pieces(3 * l + 1)
                for s in range(4):
                    PIECE["kk", l, s] = add_piece(("kk", l, s))
                for s in range(4):
                    PIECE["vvar", l, s] = add_piece(("vvar", l) if s == 3 else None)
                for s in range(4):
                    PIECE["gvar", l, s] = add_piece(("gvar", l, s))
                norm_pieces(3 * l + 2)
            else:
                norm_pieces(7 + 3 * l)
                norm_pieces(8 + 3 * l)
                for g in range((1, 3)[l]):
                    for c in range(DT):
                        PIECE["ss", l, g, c] = add_piece(("ss", l, g, c))
                norm_pieces(9 + 3 * l)
        if b == 0:
            norm_pieces(6)

    def gu_key(n):
        return "gu", n // FT, n % FT

    def wait_filled(eng, key):
        n = PLAN.uses[key][0]
        eng.wait_ge(lin_filled, n + 1)
        return lin[:, n % 3, :]

    def wait_emptied(eng, key):
        _, engine, count = PLAN.uses[key]
        eng.wait_ge(emptied[engine], count)

    def pairs(bank):
        return bank.rearrange("p (a t) -> p a t", a=2)

    FFN_AT = {}
    for i in range(8):
        FFN_AT[i] = 2 * PLAN.unit["ffn", i]
    MIX_AT = {m: 2 * PLAN.unit["mix", m] for m in range(4)}
    OUT_AT = {m: 2 * PLAN.unit["out", m] for m in range(4)}
    HALVES = 2 * PLAN.units
    X_FROM = {1: ("down", 0), 2: ("out", 0), 3: ("down", 1), 4: ("down", 2), 5: ("out", 1), 6: ("down", 3),
              8: ("down", 4), 9: ("out", 2), 10: ("down", 5), 11: ("down", 6), 12: ("out", 3), 13: ("down", 7)}

    def x_wait(eng, n, i):
        if n == 0:
            eng.wait_ge(x_loaded, 16)
        elif n == 7:
            eng.wait_ge(x_normed, i + 1)
        else:
            wait_emptied(eng, (*X_FROM[n], i))

    with nc.Block() as block:

        @block.sync
        def _(sp):
            sp.dma_start(x[:], src["x"]).then_inc(x_loaded, 16)
            sp.dma_start(const[:], src["const"]).then_inc(consts_loaded, 16)
            sp.dma_start(cols[:], src["cols"]).then_inc(consts_loaded, 16)
            sp.dma_start(mod_b[:], src["mod_b"]).then_inc(consts_loaded, 16)
            sp.dma_start(level_floats[:], src["level_masks"]).then_inc(consts_loaded, 16)

            def unit(u):
                if u >= RAW_SLOTS:
                    sp.wait_ge(lo_ready, 2 * (u - RAW_SLOTS) + 2)
                sp.dma_start(raw[:, u % RAW_SLOTS, :], src["stream"][u]).then_inc(raw_loaded[u % RAW_SLOTS], 16)

            def mod_unit(m):
                if m >= 2:
                    sp.wait_ge(mod_summed, m - 1)
                sp.dma_start(mod_w[:, m % 2, :, :], src["mod_w"][m].rearrange("p (k n) -> p k n", k=DT))\
                    .then_inc(mod_loaded[m % 2], 16)

            def ffn(i):
                base = PLAN.unit["ffn", i]
                for j in range(FT):
                    unit(base + j)
                    if i < 4 and 0 <= j - 2 < MOD_UNITS_PER_FFN:
                        if j == 2 and i:
                            x_wait(sp, ffn_norm(i), 3)
                        mod_unit(MOD_UNITS_PER_FFN * i + j - 2)
                for j in range(DOWN_UNITS):
                    unit(base + FT + j)

            def small(l):
                sp.wait_ge(masks_ready, 1)
                if l:
                    x_wait(sp, 2, 3)
                sp.dma_start(w2a2[:], src["w2a2"][l]).then_inc(small_loaded, 16)
                sp.dma_start(v2[:], src["v2"][l]).then_inc(small_loaded, 16)
                sp.dma_start(w0_b[:], src["w0"][l].partition_broadcast(P)).then_inc(small_loaded, 16)
                sp.dma_start(bs_b[:], src["bs"][l].partition_broadcast(P)).then_inc(small_loaded, 16)
                sp.dma_start(ws_t[:], src["ws_t"][l]).then_inc(small_loaded, 16)

            for l in range(2):
                ffn(2 * l)
                small(l)
                for u in range(37):
                    unit(PLAN.unit["mix", l] + u)
                for u in range(4):
                    unit(PLAN.unit["out", l] + u)
                ffn(2 * l + 1)
            for l in range(2):
                ffn(4 + 2 * l)
                if l == 0:
                    x_wait(sp, 5, 3)
                    sp.dma_start(amask[:, 0, :], src["fox_mask"]).then_inc(small_loaded, 16)
                    sp.dma_start(cum_rhs[:], src["cum_rhs"]).then_inc(small_loaded, 16)
                    sp.dma_start(bf_b[:], src["b_f"].partition_broadcast(P)).then_inc(small_loaded, 16)
                else:
                    x_wait(sp, 9, 3)
                    sp.dma_start(amask[:], src["dil_mask"]).then_inc(small_loaded, 16)
                    sp.dma_start(pos_i[:], src["positions"].partition_broadcast(P)).then_inc(small_loaded, 16)
                    sp.dma_start(rope_m[:], src["rope_m"]).then_inc(small_loaded, 16)
                for u in range((13, 36)[l]):
                    unit(PLAN.unit["mix", 2 + l] + u)
                for u in range(4):
                    unit(PLAN.unit["out", 2 + l] + u)
                ffn(5 + 2 * l)
            for i in range(4):
                x_wait(sp, 13, i)
                sp.dma_start(out[:, 2 * i:2 * i + 2, :], x[:, 2 * i:2 * i + 2, :]).then_inc(stored, 16)
            sp.wait_ge(stored, 4 * 16)

        @block.gpsimd
        def _(pool):
            pool.wait_ge(consts_loaded, 64)
            nc.gpsimd.tensor_copy(level_masks[:], level_floats[:]).then_inc(masks_ready, 1)
            for l in range(2):
                if l == 0:
                    pool.wait_ge(mixed, 13)
                    nc.gpsimd.tensor_copy(v_first[:], v_[:]).then_inc(vf_saved, 1)
                pool.wait_ge(small_loaded, 80 * (l + 1))
                nc.gpsimd.affine_select(out=ws_t[:], in_=ws_t[:], compare_op=ALU.is_ge, fill=0.0, base=0,
                                        pattern=[[0, DT], [1, CH]], channel_multiplier=-1).then_inc(zeroed, 1)

        @block.scalar
        def _(act):
            steps = [0]
            next_half = [0]

            def link(ins):
                steps[0] += 1
                ins.then_inc(act_step, 1)
                act.wait_ge(act_step, steps[0])

            def keep_ahead(w):
                while next_half[0] <= min(w + AHEAD, HALVES - 1):
                    n = next_half[0]
                    u = n // 2
                    act.wait_ge(raw_loaded[u % RAW_SLOTS], 16 * (u // RAW_SLOTS + 1))
                    if n >= SPLIT_SLOTS:
                        act.wait_ge(*half_free[n - SPLIT_SLOTS])
                    nc.scalar.activation(split[:, n % SPLIT_SLOTS, 0, :],
                                         raw[:, u % RAW_SLOTS, (n % 2) * HALF * P:(n % 2 + 1) * HALF * P],
                                         ACT.Copy).then_inc(hi_ready, 1)
                    next_half[0] += 1

            def square(key, in_):
                n = PIECE[key]
                if n >= 2:
                    act.wait_ge(*piece_free[n - 2])
                nc.scalar.activation(pieces[:, n % 2, :, :], in_, ACT.Square).then_inc(squared, 1)

            roots = [0]

            def root(out_, in_):
                roots[0] += 1
                act.wait_ge(var_ready, roots[0])
                nc.scalar.activation(out_, in_, ACT.Sqrt).then_inc(root_ready, 1)

            def norm(n):
                for i in range(4):
                    x_wait(act, n, i)
                    square(("norm", n, i), x[:, 2 * i:2 * i + 2, :])
                root(rstd[:], rstd[:])
                if n != 6:
                    split_h(n)

            def split_h(n):
                m = n if n < 6 else n - 1
                for i in range(4):
                    act.wait_ge(h_temp_ready, 4 * m + i + 1)
                    nc.scalar.activation(h[:, 0, 2 * i:2 * i + 2, :], pieces[:, i % 2, :, :], ACT.Copy)\
                        .then_inc(h_hi_ready, 1)

            def ffn(i):
                base = FFN_AT[i]
                norm(ffn_norm(i))
                for j in range(FT):
                    keep_ahead(base + 2 * j + 1)
                    bank = wait_filled(act, ("gu", i, j))
                    n = FT * i + j
                    if n >= 3:
                        wait_emptied(act, gu_key(n - 3))
                    nc.scalar.activation(silu[:, n % 3, :], bank[:, 0:T], ACT.Silu).then_inc(silu_ready, 1)
                    if j:
                        hidden_high(i, j - 1)
                hidden_high(i, FT - 1)
                for d in range(4):
                    keep_ahead(base + 2 * FT + (2 * FT * (d + 1) - 1) // HALF)

            def hidden_high(i, j):
                n = FT * i + j
                wait_emptied(act, ("gu", i, j))
                nc.scalar.activation(hidden[:, 0, j, :], product[:, n % 3, :], ACT.Copy).then_inc(hidden_hi, 1)

            def rwkv(l):
                base = MIX_AT[l]
                norm(3 * l + 1)
                for s in range(13):
                    keep_ahead(base + 2 * s + 1)
                    bank = wait_filled(act, ("shift", l, s))
                    n = 13 * l + s
                    if n >= 2:
                        act.wait_ge(mixed, n - 1)
                    nc.scalar.activation(raw_shift[:, n % 2, :, 1:T + 1], pairs(bank), ACT.Copy)\
                        .then_inc(emptied["act"], 1)
                    if s == 1:
                        act.wait_ge(mixed, 13 * l + 1)
                        nc.scalar.activation(lora[0:64, 0, :], lora[0:64, 0, :], ACT.Tanh).then_inc(tanh_ready, 1)
                keep_ahead(base + 2 * 13 - 1)
                for s in range(4):
                    wait_emptied(act, ("z", l, s))
                    part = decay[:, s // 2, (s % 2) * 512:(s % 2 + 1) * 512]
                    nc.scalar.activation(part, part, ACT.Sigmoid).then_inc(decay_ready, 1)
                for s in range(4):
                    bank = wait_filled(act, ("a", l, s))
                    for i in range(2):
                        ins = nc.scalar.activation(a_[:, 2 * s + i, :], bank[:, i * T:(i + 1) * T], ACT.Sigmoid,
                                                   bias=col("a0", 2 * s + i, l))
                    ins.then_inc(emptied["act"], 1)
                if l:
                    for s in range(4):
                        bank = wait_filled(act, ("vr", l, s))
                        if s >= 2:
                            act.wait_ge(v_done, s - 1)
                        for i in range(2):
                            ins = nc.scalar.activation(pair[:, s % 2, i, :], bank[:, i * T:(i + 1) * T],
                                                       ACT.Sigmoid, bias=col("v0", 2 * s + i, l))
                        ins.then_inc(emptied["act"], 1)
                for s in range(4):
                    keep_ahead(base + 2 * (13 + s) + 1)
                    bank = wait_filled(act, ("va", l, s))
                    nc.scalar.activation(va[:, 2 * s:2 * s + 2, :], pairs(bank), ACT.Gelu_apprx_tanh)\
                        .then_inc(emptied["act"], 1)
                for s in range(4):
                    act.wait_ge(kk_scaled, 4 * l + s + 1)
                    square(("kk", l, s), kk[:, 2 * s:2 * s + 2, :])
                for s in range(4):
                    keep_ahead(base + 2 * (17 + s) + 1)
                    bank = wait_filled(act, ("u", l, s))
                    nc.scalar.activation(u_[:, 2 * s:2 * s + 2, :], pairs(bank), ACT.Gelu_apprx_tanh)\
                        .then_inc(emptied["act"], 1)
                for s in range(4):
                    root(bonus[:, 2 * s:2 * s + 2, :], bonus[:, 2 * s:2 * s + 2, :])
                if l == 0:
                    act.wait_ge(vf_saved, 1)
                wait_emptied(act, ("bonus", l, 3))
                for s in range(4):
                    bank = wait_filled(act, ("vt", l, s))
                    nc.scalar.activation(v_[:, 2 * s:2 * s + 2, :], pairs(bank), ACT.Copy)\
                        .then_inc(emptied["act"], 1)
                for s in range(4):
                    act.wait_ge(va_centred, 4 * l + s + 1)
                    square(("vvar", l, s), va[:, 2 * s:2 * s + 2, :])
                root(rstd[:], rstd[:])
                for s in range(4):
                    bank = wait_filled(act, ("vat", l, s))
                    nc.scalar.activation(va[:, 2 * s:2 * s + 2, :], pairs(bank), ACT.Copy)\
                        .then_inc(emptied["act"], 1)
                for s in range(4):
                    act.wait_ge(ya_temp, 4 * l + s + 1)
                    nc.scalar.activation(ya_hi[:, 2 * s:2 * s + 2, :], u_[:, 2 * s:2 * s + 2, :], ACT.Copy)\
                        .then_inc(ya_hi_ready, 1)
                for c in range(DT):
                    q = DT * l + c
                    act.wait_ge(cum_done, q + 1)
                    cum = sv[:, 4, 0:NCH * (CH + 1)].rearrange("p (j t) -> p j t", j=NCH)
                    if q:
                        act.wait_ge(rec_dve, 5 * q)
                    nc.scalar.activation(e_pos[:], cum, ACT.Exp)
                    nc.scalar.activation(e_neg[:], cum, ACT.Exp, scale=-1.0).then_inc(exp_ready, 1)
                    bank = wait_filled(act, ("kbt", l, c))
                    nc.scalar.activation(kbt[:], bank[:, 0:2 * P].rearrange("p (a t) -> p a t", a=2), ACT.Copy)\
                        .then_inc(emptied["act"], 1)
                    for s in range(len(LEVELS)):
                        act.wait_ge(z_done, len(LEVELS) * q + s + 1)
                        nc.scalar.activation(z_neg[:], sv[:, 0, :].rearrange("p (a t) -> p a t", a=4), ACT.Copy,
                                             scale=-1.0).then_inc(z_ready, 1)
                    bank = wait_filled(act, ("y", l, c))
                    nc.scalar.activation(r_[:, c, :], bank[:, 0:T], ACT.Copy).then_inc(emptied["act"], 1)
                for s in range(4):
                    wait_emptied(act, ("gmean", l, s))
                    square(("gvar", l, s), r_[:, 2 * s:2 * s + 2, :])
                for s in range(4):
                    root(kk[:, 2 * s:2 * s + 2, :], kk[:, 2 * s:2 * s + 2, :])
                for s in range(4):
                    act.wait_ge(yb_temp, 4 * l + s + 1)
                    nc.scalar.activation(yb_hi[:, 2 * s:2 * s + 2, :], r_[:, 2 * s:2 * s + 2, :], ACT.Copy)\
                        .then_inc(yb_hi_ready, 1)
                for n in range(DT):
                    m = DT * l + n
                    keep_ahead(base + 2 * (21 + 2 * n) + 1)
                    bank = wait_filled(act, ("gate", l, n))
                    if n >= 2:
                        wait_emptied(act, ("proj", l, n - 2))
                    nc.scalar.activation(gate_sig[:, n % 2, :, :], pairs(bank), ACT.Sigmoid)\
                        .then_inc(emptied["act"], 1)
                    keep_ahead(base + 2 * (22 + 2 * n) + 1)
                for s in range(4):
                    act.wait_ge(merged_ready, DT * l + 2 * s + 2)
                    if s == 0:
                        wait_filled(act, ("proj", l, DT - 1))
                    nc.scalar.activation(h[:, 0, 2 * s:2 * s + 2, :], merged[:, 2 * s:2 * s + 2, :], ACT.Copy)\
                        .then_inc(merged_hi, 1)
                for d in range(4):
                    keep_ahead(OUT_AT[l] + 2 * d + 1)

            def attention(l):
                base = MIX_AT[2 + l]
                ng = (1, 3)[l]
                norm(8 + 3 * l)
                if l:
                    act.wait_ge(angle_ready, 1)
                    nc.scalar.activation(sin[:], ang[:], ACT.Sin)
                    act.wait_ge(angle_ready, 2)
                    nc.scalar.activation(cos[:], cos[:], ACT.Sin).then_inc(rope_ready, 1)
                half = base

                def qk_root(g, c):
                    b = (DT * g + c) % 2
                    root(ssr[:, b, :, :], ssr[:, b, :, :])

                for g in range(ng):
                    for c in range(DT):
                        keep_ahead(half + 1)
                        half += 2
                        bank = wait_filled(act, ("qk", l, g, c))
                        square(("ss", l, g, c), pairs(bank))
                        if c:
                            qk_root(g, c - 1)
                    qk_root(g, DT - 1)
                    for s in range(4):
                        keep_ahead(half + 1)
                        half += 2
                        bank = wait_filled(act, ("v", l, g, s))
                        nc.scalar.activation(vtok[:, g, :, s * 2 * P:(s + 1) * 2 * P], pairs(bank), ACT.Copy)\
                            .then_inc(emptied["act"], 1)
                if l == 0:
                    keep_ahead(half + 1)
                    act.wait_ge(fexp, 1)
                    link(nc.scalar.activation(ls_t[:], ls_t[:], ACT.Exp))
                    nc.scalar.activation(ls_t[:], ls_t[:], ACT.Ln, bias=1.0).then_inc(fexp, 1)
                for hd in range(HEADS):
                    n = HEADS * l + hd
                    act.wait_ge(max_ready, n + 1)
                    lg0 = logits[:, 0:ng, 0:P]
                    lg1 = logits[:, 0:ng, P:3 * P]
                    nc.scalar.activation(lg0, lg0, ACT.Exp, scale=HD ** -0.5, bias=stat[:, 4:5],
                                         accum_out=stat[:, 6:7])
                    nc.scalar.activation(lg1, lg1, ACT.Exp, scale=HD ** -0.5, bias=stat[:, 5:6],
                                         accum_out=stat[:, 7:8]).then_inc(probs_ready, 1)
                    for g in range(ng):
                        m = HEADS * g + hd if l == 0 else HEADS + GROUPS * hd + g
                        act.wait_ge(pt_done, m + 1)
                        nc.scalar.activation(pt[:, g, :], sv[:, 3 + m % 2, 0:3 * P], ACT.Copy).then_inc(pt_ready, 1)
                    if hd % 2:
                        bank = wait_filled(act, ("o", l, hd // 2))
                        nc.scalar.activation(o_hi[:, hd // 2, :], bank[:, 0:T], ACT.Copy).then_inc(o_hi_ready, 1)
                for d in range(4):
                    keep_ahead(OUT_AT[2 + l] + 2 * d + 1)

            keep_ahead(-1)
            act.wait_ge(consts_loaded, 64)
            nc.scalar.activation(cols[:, COL["c"]:COL["c"] + DT], cols[:, COL["c"]:COL["c"] + DT], ACT.Silu)\
                .then_inc(c_ready, 1)
            for l in range(2):
                ffn(2 * l)
                rwkv(l)
                ffn(2 * l + 1)
            norm(6)
            for l in range(2):
                ffn(4 + 2 * l)
                attention(l)
                ffn(5 + 2 * l)

        @block.vector
        def _(dve):
            steps = [0]
            next_half = [0]
            V = nc.vector

            def link(ins):
                steps[0] += 1
                ins.then_inc(dve_step, 1)
                dve.wait_ge(dve_step, steps[0])

            def keep_ahead(w):
                while next_half[0] <= min(w + AHEAD, HALVES - 1):
                    n = next_half[0]
                    u = n // 2
                    dve.wait_ge(hi_ready, n + 1)
                    V.tensor_tensor(split[:, n % SPLIT_SLOTS, 1, :],
                                    raw[:, u % RAW_SLOTS, (n % 2) * HALF * P:(n % 2 + 1) * HALF * P],
                                    split[:, n % SPLIT_SLOTS, 0, :].bitcast(F32), ALU.subtract).then_inc(lo_ready, 1)
                    next_half[0] += 1

            roots = [0]

            def inverse_root(out_, in_, scale, eps, guard=None):
                if guard is None:
                    link(V.tensor_scalar(out_, in_, scale, eps, ALU.mult, ALU.add))
                else:
                    link(V.tensor_scalar(out_, in_, guard, None, ALU.max))
                V.reciprocal(out_, out_).then_inc(var_ready, 1)
                roots[0] += 1

            def root_wait(n=None):
                dve.wait_ge(root_ready, roots[0] if n is None else n)

            def norm(n):
                bank = wait_filled(dve, ("norm", n))
                V.tensor_scalar(rstd[:], bank[:, 0:T], NORM_EPS, None, ALU.add).then_inc(emptied["dve"], 1)
                wait_emptied(dve, ("norm", n))
                V.reciprocal(rstd[:], rstd[:]).then_inc(var_ready, 1)
                roots[0] += 1
                root_wait()
                if n == 6:
                    for i in range(4):
                        for c in (2 * i, 2 * i + 1):
                            ins = V.scalar_tensor_tensor(x[:, c, :], x[:, c, :], col("final_norm", c), rstd[:],
                                                         ALU.mult, ALU.mult)
                        ins.then_inc(x_normed, 1)
                    return
                m = n if n < 6 else n - 1
                for i in range(4):
                    if i >= 2:
                        dve.wait_ge(h_ready, 4 * m + i - 1)
                    for c in (2 * i, 2 * i + 1):
                        o = pieces[:, i % 2, c % 2, :]
                        if n < 6:
                            l, w = divmod(n, 3)
                            name = ("ffn1_norm", "mix_norm", "ffn2_norm")[w]
                            ins = V.scalar_tensor_tensor(o, x[:, c, :], col(name, c, l), rstd[:], ALU.mult, ALU.mult)
                        else:
                            w = n - 7
                            l, sub = divmod(w, 3)
                            link(V.scalar_tensor_tensor(o, x[:, c, :], gain2[:, w, c:c + 1], rstd[:],
                                                        ALU.mult, ALU.mult))
                            shift = 72 * l + 24 * sub + c
                            ins = V.tensor_scalar(o, o, mod[:, shift:shift + 1], None, ALU.add)
                    ins.then_inc(h_temp_ready, 1)
                    dve.wait_ge(h_hi_ready, 4 * m + i + 1)
                    V.tensor_tensor(h[:, 1, 2 * i:2 * i + 2, :], pieces[:, i % 2, :, :],
                                    h[:, 0, 2 * i:2 * i + 2, :].bitcast(F32), ALU.subtract).then_inc(h_ready, 1)

            def mod_sum(m):
                dve.wait_ge(mod_loaded[m % 2], 16 * (m // 2 + 1))
                if m >= 2:
                    dve.wait_ge(mod_done, m - 1)
                acc = mod_acc[:, m % 2, :]
                link(V.tensor_scalar(acc, mod_w[:, m % 2, 0, :], col("c", 0), None, ALU.mult))
                for k in range(1, DT):
                    ins = V.scalar_tensor_tensor(acc, mod_w[:, m % 2, k, :], col("c", k), acc, ALU.mult, ALU.add)
                    if k < DT - 1:
                        link(ins)
                ins.then_inc(mod_summed, 1)

            def hidden_rest(i, j):
                n = FT * i + j
                dve.wait_ge(hidden_hi, n + 1)
                V.tensor_tensor(hidden[:, 1, j, :], product[:, n % 3, :], hidden[:, 0, j, :].bitcast(F32),
                                ALU.subtract).then_inc(hidden_ready, 1)

            def ffn(i):
                base = FFN_AT[i]
                norm(ffn_norm(i))
                for j in range(FT):
                    keep_ahead(base + 2 * j + 1)
                    n = FT * i + j
                    bank = wait_filled(dve, ("gu", i, j))
                    dve.wait_ge(silu_ready, n + 1)
                    if n >= 3:
                        dve.wait_ge(hidden_ready, n - 2)
                    V.tensor_tensor(product[:, n % 3, :], silu[:, n % 3, :], bank[:, T:2 * T], ALU.mult)\
                        .then_inc(emptied["dve"], 1)
                    if i < 4 and j < MOD_UNITS_PER_FFN:
                        mod_sum(MOD_UNITS_PER_FFN * i + j)
                    if j:
                        hidden_rest(i, j - 1)
                hidden_rest(i, FT - 1)
                if i < 4:
                    dve.wait_ge(mod_done, MOD_UNITS_PER_FFN * (i + 1))
                    a = MOD_COLS * i
                    V.tensor_tensor(mod[:, a:a + MOD_COLS], sv[:, 4, a:a + MOD_COLS], mod_b[:, a:a + MOD_COLS],
                                    ALU.add).then_inc(mod_kept, 1)
                for d in range(4):
                    keep_ahead(base + 2 * FT + (2 * FT * (d + 1) - 1) // HALF)
                    residual(("down", i, d), 2 * d, 0.5 if i < 4 else None, (i - 4) // 2 * 3 + (i - 4) % 2 * 2)

            def residual(key, c, factor, which):
                bank = pairs(wait_filled(dve, key))
                if factor is not None:
                    V.scalar_tensor_tensor(x[:, c:c + 2, :], bank, factor, x[:, c:c + 2, :], ALU.mult, ALU.add)\
                        .then_inc(emptied["dve"], 1)
                else:
                    V.scalar_tensor_tensor(x[:, c, :], bank[:, 0, :], gate2[:, which, c:c + 1], x[:, c, :],
                                           ALU.mult, ALU.add)
                    V.scalar_tensor_tensor(x[:, c + 1, :], bank[:, 1, :], gate2[:, which, c + 1:c + 2],
                                           x[:, c + 1, :], ALU.mult, ALU.add).then_inc(emptied["dve"], 1)

            def rwkv(l):
                base = MIX_AT[l]
                norm(3 * l + 1)
                link(V.memset(raw_shift[:, :, :, 0:1], 0.0))
                for s in range(13):
                    keep_ahead(base + 2 * s + 1)
                    n = 13 * l + s
                    wait_emptied(dve, ("shift", l, s))
                    if n:
                        dve.wait_ge(mixed, n)
                    b = raw_shift[:, n % 2, :, :]
                    link(V.tensor_tensor(diff[:], b[:, :, 0:T], b[:, :, 1:T + 1], ALU.subtract))
                    if s == 0:
                        dst = [(lora[:, 0, :], 24), (lora[:, 1, :], 25)]
                    elif s < 9:
                        dst = [(r_[:, s - 1, :], s - 1), (k_[:, s - 1, :], 8 + s - 1)]
                    else:
                        c = 2 * (s - 9)
                        dst = [(v_[:, c, :], 16 + c), (v_[:, c + 1, :], 17 + c)]
                    for i, (o, m) in enumerate(dst):
                        ins = V.scalar_tensor_tensor(o, diff[:, i, :], col("mu", m, l), b[:, i, 1:T + 1],
                                                     ALU.mult, ALU.add)
                    ins.then_inc(mixed, 1)
                dve.wait_ge(mixed, 13 * l + 13)
                dve.wait_ge(small_loaded, 80 * (l + 1))
                for s in range(4):
                    bank = wait_filled(dve, ("z", l, s))
                    V.tensor_tensor(decay[:, s // 2, (s % 2) * 512:(s % 2 + 1) * 512], bank,
                                    w0_b[:, (s % 2) * 512:(s % 2 + 1) * 512], ALU.add).then_inc(emptied["dve"], 1)
                if l:
                    for s in range(4):
                        wait_emptied(dve, ("vr", l, s))
                        vs = v_[:, 2 * s:2 * s + 2, :]
                        link(V.tensor_tensor(diff[:], v_first[:, 2 * s:2 * s + 2, :], vs, ALU.subtract))
                        link(V.tensor_tensor(diff[:], diff[:], pair[:, s % 2, :, :], ALU.mult))
                        V.tensor_tensor(vs, vs, diff[:], ALU.add).then_inc(v_done, 1)
                        dve.wait_ge(v_done, s + 1)
                for s in range(4):
                    keep_ahead(base + 2 * (13 + s) + 1)
                    for c in (2 * s, 2 * s + 1):
                        ins = V.tensor_scalar(kk[:, c, :], k_[:, c, :], col("k_k", c, l), None, ALU.mult)
                    ins.then_inc(kk_scaled, 1)
                for s in range(4):
                    bank = wait_filled(dve, ("kk", l, s))
                    o = bonus[:, 2 * s:2 * s + 2, :]
                    V.tensor_scalar(o, pairs(bank), 1e-24, None, ALU.max).then_inc(emptied["dve"], 1)
                    wait_emptied(dve, ("kk", l, s))
                    V.reciprocal(o, o).then_inc(var_ready, 1)
                    roots[0] += 1
                wait_emptied(dve, ("a", l, 3))
                a0 = COL["k_a", l]
                link(V.tensor_scalar(one_less_ka[:, l, :], cols[:, a0:a0 + DT], -1.0, 1.0, ALU.mult, ALU.add))
                for s in range(4):
                    keep_ahead(base + 2 * (17 + s) + 1)
                    for c in (2 * s, 2 * s + 1):
                        link(V.tensor_scalar(diff[:, c % 2, :], a_[:, c, :], col("k_a", c, l),
                                             one_less_ka[:, l, c:c + 1], ALU.mult, ALU.add))
                        link(V.tensor_tensor(k_[:, c, :], k_[:, c, :], diff[:, c % 2, :], ALU.mult))
                for s in range(4):
                    root_wait(roots[0] - 3 + s)
                    w = slice(2 * s, 2 * s + 2)
                    link(V.tensor_tensor(kk[:, w, :], kk[:, w, :], bonus[:, w, :], ALU.mult))
                    link(V.tensor_tensor(a_[:, w, :], kk[:, w, :], a_[:, w, :], ALU.mult))
                for s in range(4):
                    n = 4 * l + s
                    if s >= 2:
                        wait_filled(dve, ("bonus", l, s - 2))
                    for c in (2 * s, 2 * s + 1):
                        ins = V.scalar_tensor_tensor(pair[:, s % 2, c % 2, :], r_[:, c, :], col("r_k", c, l),
                                                     k_[:, c, :], ALU.mult, ALU.mult)
                    ins.then_inc(rk_ready, 1)
                    if s:
                        bonus_of(l, s - 1)
                bonus_of(l, 3)
                bank = wait_filled(dve, ("vmean", l))
                V.tensor_copy(rstd[:], bank[:, 0:T]).then_inc(emptied["dve"], 1)
                wait_emptied(dve, ("vmean", l))
                for s in range(4):
                    w = slice(2 * s, 2 * s + 2)
                    V.tensor_tensor(va[:, w, :], va[:, w, :], wide(rstd[:], 2), ALU.subtract).then_inc(va_centred, 1)
                bank = wait_filled(dve, ("vvar", l))
                V.tensor_scalar(rstd[:], bank[:, 0:T], LN_EPS, None, ALU.add).then_inc(emptied["dve"], 1)
                wait_emptied(dve, ("vvar", l))
                V.reciprocal(rstd[:], rstd[:]).then_inc(var_ready, 1)
                roots[0] += 1
                root_wait()
                for s in range(4):
                    w = slice(2 * s, 2 * s + 2)
                    link(V.tensor_tensor(va[:, w, :], va[:, w, :], wide(rstd[:], 2), ALU.mult))
                    for c in (2 * s, 2 * s + 1):
                        ins = V.tensor_scalar(va[:, c, :], va[:, c, :], col("ln_g", c, l), col("ln_b", c, l),
                                              ALU.mult, ALU.add)
                    ins.then_inc(va_ready, 1)
                for s in range(4):
                    bank = wait_filled(dve, ("sgu", l, s))
                    w = slice(2 * s, 2 * s + 2)
                    bs = bs_b[:, 2 * s * CH:(2 * s + 2) * CH].rearrange("p (g t) -> p g t", g=2)
                    bank4 = bank.rearrange("p (g j t) -> p g j t", g=2, j=NCH)
                    d4 = diff[:].rearrange("p g (j t) -> p g j t", j=NCH)
                    for j in range(NCH):
                        ins = V.tensor_tensor(d4[:, :, j, :], bank4[:, :, j, :], bs, ALU.add)
                    ins.then_inc(emptied["dve"], 1)
                    wait_emptied(dve, ("sgu", l, s))
                    V.tensor_tensor(u_[:, w, :], u_[:, w, :], diff[:], ALU.mult).then_inc(ya_temp, 1)
                    dve.wait_ge(ya_hi_ready, 4 * l + s + 1)
                    V.tensor_tensor(ya_lo[:, w, :], u_[:, w, :], ya_hi[:, w, :].bitcast(F32), ALU.subtract)\
                        .then_inc(ya_ready, 1)
                for b in (beta, kappa):
                    V.memset(b[0:64, 1, :, :], 0.0)
                    V.memset(b[64:128, 0, :, :], 0.0)
                link(V.memset(s0[:], 0.0))
                if l == 0:
                    dve.wait_ge(masks_ready, 1)
                for c in range(DT):
                    solve(l, c)
                for s in range(4):
                    w = slice(2 * s, 2 * s + 2)
                    wait_emptied(dve, ("y", l, 2 * s + 1))
                    bank = wait_filled(dve, ("gmean", l, s))
                    V.scalar_tensor_tensor(r_[:, w, :], pairs(bank), -1.0 / HD, r_[:, w, :], ALU.mult, ALU.add)\
                        .then_inc(emptied["dve"], 1)
                for s in range(4):
                    bank = wait_filled(dve, ("gvar", l, s))
                    o = kk[:, 2 * s:2 * s + 2, :]
                    V.tensor_scalar(o, pairs(bank), 1.0 / HD, GN_EPS, ALU.mult, ALU.add).then_inc(emptied["dve"], 1)
                    wait_emptied(dve, ("gvar", l, s))
                    V.reciprocal(o, o).then_inc(var_ready, 1)
                    roots[0] += 1
                for s in range(4):
                    w = slice(2 * s, 2 * s + 2)
                    root_wait(roots[0] - 3 + s)
                    link(V.tensor_tensor(r_[:, w, :], r_[:, w, :], kk[:, w, :], ALU.mult))
                    for c in (2 * s, 2 * s + 1):
                        link(V.tensor_scalar(r_[:, c, :], r_[:, c, :], col("gn_g", c, l), col("gn_b", c, l),
                                             ALU.mult, ALU.add))
                    V.tensor_tensor(r_[:, w, :], r_[:, w, :], bonus[:, w, :], ALU.add).then_inc(yb_temp, 1)
                    dve.wait_ge(yb_hi_ready, 4 * l + s + 1)
                    V.tensor_tensor(yb_lo[:, w, :], r_[:, w, :], yb_hi[:, w, :].bitcast(F32), ALU.subtract)\
                        .then_inc(yb_ready, 1)
                for n in range(DT):
                    keep_ahead(base + 2 * (21 + 2 * n) + 1)
                    keep_ahead(base + 2 * (22 + 2 * n) + 1)
                    bank = wait_filled(dve, ("proj", l, n))
                    wait_emptied(dve, ("gate", l, n))
                    V.tensor_tensor(diff[:], pairs(bank), gate_sig[:, n % 2, :, :], ALU.mult)\
                        .then_inc(emptied["dve"], 1)
                    wait_emptied(dve, ("proj", l, n))
                    V.tensor_tensor(merged[:, n, :], diff[:, 0, :], diff[:, 1, :], ALU.add).then_inc(merged_ready, 1)
                    dve.wait_ge(merged_ready, DT * l + n + 1)
                for s in range(4):
                    w = slice(2 * s, 2 * s + 2)
                    dve.wait_ge(merged_hi, 4 * l + s + 1)
                    V.tensor_tensor(h[:, 1, w, :], merged[:, w, :], h[:, 0, w, :].bitcast(F32), ALU.subtract)\
                        .then_inc(merged_split, 1)
                for d in range(4):
                    keep_ahead(OUT_AT[l] + 2 * d + 1)
                    residual(("out", l, d), 2 * d, 1.0, None)

            def bonus_of(l, s):
                bank = wait_filled(dve, ("bonus", l, s))
                w = slice(2 * s, 2 * s + 2)
                V.tensor_tensor(bonus[:, w, :], pairs(bank), v_[:, w, :], ALU.mult).then_inc(emptied["dve"], 1)

            def solve(l, c):
                q = DT * l + c
                dve.wait_ge(exp_ready, q + 1)
                in_chunks = lambda t: t[:, c, :].rearrange("p (j t) -> p j t", j=NCH)
                pos_excl, pos_incl, neg_incl = e_pos[:, :, 0:CH], e_pos[:, :, 1:CH + 1], e_neg[:, :, 1:CH + 1]
                V.tensor_tensor(ar[:, :, 0:CH], in_chunks(kk), pos_excl, ALU.mult)
                V.tensor_tensor(ar[:, :, CH:2 * CH], in_chunks(r_), pos_incl, ALU.mult)
                for i, (o, t) in enumerate(((kappa, k_), (beta, a_))):
                    for hh in range(2):
                        w = slice(64 * hh, 64 * hh + 64)
                        V.tensor_tensor(o[w, hh, :, :], in_chunks(t)[w], neg_incl[w], ALU.mult)
                    ins = V.tensor_tensor(kb0[:, i, :], t[:, c, 0:CH], e_neg[:, 0, 1:CH + 1], ALU.mult)
                ins.then_inc(scaled, 1)
                dve.wait_ge(scores_done, q + 1)
                four = lambda ap: ap.rearrange("p (a t) -> p a t", a=4)
                V.tensor_tensor(gb[:], sv[:, 0:2, :].rearrange("p b (a t) -> p (b a) t", a=2), wide(mask, 4), ALU.mult)
                V.tensor_tensor(gk[:], sv[:, 2:4, :].rearrange("p b (a t) -> p (b a) t", a=2), wide(mask, 4), ALU.mult)
                link(V.tensor_tensor(t_inv[:], four(sv[:, 4, :]), wide(c_("neg2"), 4), ALU.mult))
                link(V.tensor_tensor(q_inv[:], gb[:, :, 0:CH], wide(c_("neg2t"), 4), ALU.mult))
                V.tensor_tensor(t_inv[:], t_inv[:], wide(ident, 4), ALU.add)
                V.tensor_tensor(q_inv[:], q_inv[:], wide(ident, 4), ALU.add).then_inc(inverse_ready, 1)
                for s in range(len(LEVELS)):
                    dve.wait_ge(p_done, len(LEVELS) * q + s + 1)
                    if s < len(LEVELS) - 1:
                        V.copy_predicated(t_inv[:], wide(level_masks[:, 0, s, :], 4), four(sv[:, 1, :]))
                    V.copy_predicated(q_inv[:], wide(level_masks[:, 1, s, :], 4), four(sv[:, 2, :]))\
                        .then_inc(inverse_ready, 1)
                b3 = sv[:, 3, :]
                dve.wait_ge(rec_pe, 5 * q + 1)
                V.tensor_copy(rh[:], b3[:, 0:P]).then_inc(rec_dve, 1)
                dve.wait_ge(rec_pe, 5 * q + 2)
                V.tensor_scalar(nu[:], b3[:, P:2 * P], -1.0, None, ALU.mult).then_inc(rec_dve, 1)
                dve.wait_ge(rec_pe, 5 * q + 3)
                for hh in range(2):
                    w = slice(64 * hh, 64 * hh + 64)
                    ins = V.scalar_tensor_tensor(s0[w, w], b3[w, 2 * P + 64 * hh:2 * P + 64 * hh + 64],
                                                 e_pos[w, 0, CH:CH + 1],
                                                 e_neg[w, 1, 0:1].to_broadcast([64, 64]), ALU.mult, ALU.mult)
                ins.then_inc(rec_dve, 1)
                dve.wait_ge(rec_pe, 5 * q + 4)
                V.tensor_copy(rh[:], b3[:, 3 * P:4 * P]).then_inc(rec_dve, 1)
                dve.wait_ge(rec_pe, 5 * q + 5)
                V.tensor_scalar(nu[:], b3[:, 0:P], -1.0, None, ALU.mult).then_inc(rec_dve, 1)

            def attention(l):
                base = MIX_AT[2 + l]
                ng = (1, 3)[l]
                norm(8 + 3 * l)
                dve.wait_ge(small_loaded, 160 + 48 * (l + 1))
                if l:
                    two_pi = 2 * np.pi
                    c1 = 6.28125
                    c2 = float(np.float32(two_pi - c1))
                    c3 = float(two_pi - c1 - np.float64(np.float32(two_pi - c1)))
                    link(V.tensor_copy(ang[:], pos_i[:]))
                    link(V.tensor_scalar(ang[:], ang[:], col("inv_freq"), None, ALU.mult))
                    link(V.tensor_scalar(cos[:], ang[:], 1.0 / two_pi, 12582912.0, ALU.mult, ALU.add))
                    link(V.tensor_scalar(cos[:], cos[:], -12582912.0, None, ALU.add))
                    for part in (c1, c2, c3):
                        link(V.scalar_tensor_tensor(ang[:], cos[:], -part, ang[:], ALU.mult, ALU.add))
                    V.tensor_scalar(ang[:], ang[:], 3.1415925, -3.1415925, ALU.min, ALU.max).then_inc(angle_ready, 1)
                    dve.wait_ge(angle_ready, 1)
                    link(V.tensor_scalar(cos[:], ang[:], -1.0, None, ALU.mult))
                    link(V.tensor_tensor(cos[:], cos[:], ang[:], ALU.max))
                    V.tensor_scalar(cos[:], cos[:], -1.0, float(np.pi / 2), ALU.mult, ALU.add).then_inc(angle_ready, 1)
                    dve.wait_ge(rope_ready, 1)
                half = base

                def finish_qk(g, c):
                    n = DT * g + c
                    b = n % 2
                    bank = wait_filled(dve, ("ss", l, g, c))
                    V.tensor_scalar(ssr[:, b, :, :], pairs(bank), 1.0 / HD, NORM_EPS, ALU.mult, ALU.add)\
                        .then_inc(emptied["dve"], 1)
                    wait_emptied(dve, ("ss", l, g, c))
                    V.reciprocal(ssr[:, b, :, :], ssr[:, b, :, :]).then_inc(var_ready, 1)
                    roots[0] += 1
                    if l:
                        bank = wait_filled(dve, ("rot", l, g, c))
                        V.tensor_tensor(rot[:], pairs(bank), wide(sin[:], 2), ALU.mult).then_inc(emptied["dve"], 1)
                        link(V.tensor_tensor(qkg[:, b, :, :], qkg[:, b, :, :], wide(cos[:], 2), ALU.mult))
                        wait_emptied(dve, ("rot", l, g, c))
                        link(V.tensor_tensor(qkg[:, b, :, :], qkg[:, b, :, :], rot[:], ALU.add))
                    root_wait()
                    V.tensor_tensor(qk[:, g, 2 * c:2 * c + 2, :], qkg[:, b, :, :], ssr[:, b, :, :], ALU.mult)\
                        .then_inc(qk_ready, 1)
                    dve.wait_ge(qk_ready, DT * (g + l) + c + 1)

                for g in range(ng):
                    for c in range(DT):
                        keep_ahead(half + 1)
                        half += 2
                        b = (DT * g + c) % 2
                        bank = wait_filled(dve, ("qk", l, g, c))
                        dve.wait_ge(squared, PIECE["ss", l, g, c] + 1)
                        for i in range(2):
                            gc = COL["fox_g"] + i if l == 0 else COL["dil_g"] + 2 * g + i
                            ins = V.tensor_scalar(qkg[:, b, i, :], bank[:, i * T:(i + 1) * T], cols[:, gc:gc + 1],
                                                  None, ALU.mult)
                        ins.then_inc(emptied["dve"], 1)
                        wait_emptied(dve, ("qk", l, g, c))
                        if c:
                            finish_qk(g, c - 1)
                    finish_qk(g, DT - 1)
                    for s in range(4):
                        keep_ahead(half + 1)
                        half += 2
                if l == 0:
                    keep_ahead(half + 1)
                    bank = wait_filled(dve, ("f", 0))[:, 0:NCH * HEADS].rearrange("p (j n) -> p j n", j=NCH)
                    V.tensor_tensor(ls[:], bank, wide(bf_b[:], NCH), ALU.add).then_inc(emptied["dve"], 1)
                    wait_emptied(dve, ("f", 0))
                    link(V.tensor_scalar(ls_t[:], ls[:], -1.0, None, ALU.mult))
                    V.tensor_tensor(ls_t[:], ls_t[:], ls[:], ALU.min).then_inc(fexp, 1)
                    link(V.tensor_scalar(ls[:], ls[:], 0.0, None, ALU.min))
                    dve.wait_ge(fexp, 2)
                    link(V.tensor_tensor(ls[:], ls[:], ls_t[:], ALU.subtract))
                for hd in range(HEADS):
                    n = HEADS * l + hd
                    if l == 0:
                        if hd:
                            dve.wait_ge(logits_done, n)
                        V.tensor_copy(ls_b[:], ls[:, :, hd:hd + 1].to_broadcast([P, NCH, P])).then_inc(lsb_ready, 1)
                    dve.wait_ge(logits_done, n + 1)
                    if hd:
                        dve.wait_ge(pt_done, (n if l == 0 else HEADS + GROUPS * hd))
                    lg_bank = sv[:, 0:ng, 0:3 * P]
                    link(V.tensor_tensor(logits[:, 0:ng, :], lg_bank, amask[:, 0:ng, :], ALU.add))
                    V.tensor_reduce(stat[:, 0:1], logits[:, 0:ng, 0:P], AX.XY, ALU.max, negate=True)
                    link(V.tensor_reduce(stat[:, 1:2], logits[:, 0:ng, P:3 * P], AX.XY, ALU.max, negate=True))
                    V.tensor_scalar(stat[:, 4:6], stat[:, 0:2], HD ** -0.5, None, ALU.mult).then_inc(max_ready, 1)
                    dve.wait_ge(probs_ready, n + 1)
                    link(V.reciprocal(stat[:, 8:10], stat[:, 6:8]))
                    V.tensor_scalar(logits[:, 0:ng, 0:P], logits[:, 0:ng, 0:P], stat[:, 8:9], None, ALU.mult)
                    V.tensor_scalar(logits[:, 0:ng, P:3 * P], logits[:, 0:ng, P:3 * P], stat[:, 9:10], None,
                                    ALU.mult).then_inc(norm_ready, 1)
                    if hd % 2:
                        c = hd // 2
                        bank = wait_filled(dve, ("o", l, c))
                        dve.wait_ge(o_hi_ready, DT * l + c + 1)
                        V.tensor_tensor(o_lo[:, c, :], bank[:, 0:T], o_hi[:, c, :].bitcast(F32), ALU.subtract)\
                            .then_inc(emptied["dve"], 1)
                for d in range(4):
                    keep_ahead(OUT_AT[2 + l] + 2 * d + 1)
                    residual(("out", 2 + l, d), 2 * d, None, 3 * l + 1)

            keep_ahead(-1)
            dve.wait_ge(consts_loaded, 64)
            dve.wait_ge(c_ready, 1)
            for l in range(2):
                ffn(2 * l)
                rwkv(l)
                ffn(2 * l + 1)
            for l in range(2):
                for sub in range(3):
                    w = 3 * l + sub
                    a = 72 * l + 24 * sub
                    g = COL["norm_g"] + 8 * w
                    link(V.tensor_scalar(gain2[:, w, :], mod[:, a + 8:a + 16], 1.0, None, ALU.add))
                    link(V.tensor_tensor(gain2[:, w, :], gain2[:, w, :], cols[:, g:g + 8], ALU.mult))
                    link(V.tensor_scalar(gate2[:, w, :], mod[:, a + 16:a + 24], 1.0 if sub == 1 else 0.5, None,
                                         ALU.mult))
            norm(6)
            for l in range(2):
                ffn(4 + 2 * l)
                attention(l)
                ffn(5 + 2 * l)

        @block.tensor
        def _(pe):
            M = nc.tensor.matmul

            def bank_for(key):
                n = PLAN.uses[key][0]
                if n >= 3:
                    wait_emptied(pe, PLAN.order[n - 3])
                return lin[:, n % 3, :]

            def half_ready(w):
                pe.wait_ge(lo_ready, w + 1)
                return split[:, w % SPLIT_SLOTS, :, :]

            def three(o, w_hi, w_lo, a_hi, a_lo, start, stop, skip=False):
                M(o, w_hi, a_hi, start=start, stop=False, skip_group_check=skip)
                M(o, w_hi, a_lo, start=False, stop=False, skip_group_check=skip)
                return M(o, w_lo, a_hi, start=False, stop=stop, skip_group_check=skip)

            def two_tiles(w, key, acts, ready=None):
                bank = bank_for(key)
                for i in range(2):
                    s = half_ready(w + i)
                    hi, lo = acts[i]
                    for k in range(DT):
                        if ready is not None and i == 0 and k % 2 == 0:
                            ready(k // 2)
                        t = slice(k * P, (k + 1) * P)
                        ins = three(bank[:, i * T:(i + 1) * T], s[:, 0, t], s[:, 1, t], hi[:, k, :], lo[:, k, :],
                                    k == 0, k == DT - 1)
                    if i == 0:
                        ins.then_inc(halves_used, 1)
                ins.then_inc(lin_filled, 1)

            HH = (h[:, 0, :, :], h[:, 1, :, :])

            def tokens_major(w, key, width):
                bank = bank_for(key)
                for i in range(2):
                    s = half_ready(w + i)
                    for j in range(NCH):
                        o = bank[:, j * width:(j + 1) * width]
                        for k in range(4):
                            m = slice(k * 2 * P, k * 2 * P + width)
                            kk_ = 4 * i + k
                            a_hi = h[:, 0, kk_, j * CH:(j + 1) * CH]
                            a_lo = h[:, 1, kk_, j * CH:(j + 1) * CH]
                            M(o, a_hi, s[:, 0, m], start=(kk_ == 0 and j == 0), stop=False, skip_group_check=True)
                            M(o, a_lo, s[:, 0, m], start=False, stop=False, skip_group_check=True)
                            ins = M(o, a_hi, s[:, 1, m], start=False, stop=(kk_ == DT - 1 and j == NCH - 1),
                                    skip_group_check=True)
                    if i == 0:
                        ins.then_inc(halves_used, 1)
                ins.then_inc(lin_filled, 1)

            def norm(n):
                bank = bank_for(("norm", n))
                sums(bank, [("norm", n, i) for i in range(4)])

            def sums(bank, keys):
                for i, key in enumerate(keys):
                    p = PIECE[key]
                    pe.wait_ge(squared, p + 1)
                    for t in range(2):
                        ins = M(bank[:, 0:T], mean_w, pieces[:, p % 2, t, :], start=(i == 0 and t == 0),
                                stop=(i == 3 and t == 1))
                    ins.then_inc(piece_used if i < 3 else lin_filled, 1)

            def h_wait(n):
                m = n if n < 6 else n - 1
                return lambda i: pe.wait_ge(h_ready, 4 * m + i + 1)

            def mod_columns(m):
                pe.wait_ge(mod_summed, m + 1)
                if m and m % MOD_UNITS_PER_FFN == 0:
                    pe.wait_ge(mod_kept, m // MOD_UNITS_PER_FFN)
                for i in range(2):
                    ins = M(sv[:, 4, 2 * m + i:2 * m + i + 1], mod_acc[:, m % 2, i * P:(i + 1) * P],
                            ones_col, start=True, stop=True)
                ins.then_inc(mod_done, 1)

            ones_col = c_("one")

            def ffn(i):
                base = FFN_AT[i]
                norm(ffn_norm(i))
                for j in range(FT):
                    two_tiles(base + 2 * j, ("gu", i, j), (HH, HH), h_wait(ffn_norm(i)) if j == 0 else None)
                    if i < 4 and 0 < j <= MOD_UNITS_PER_FFN:
                        mod_columns(MOD_UNITS_PER_FFN * i + j - 1)
                base += 2 * FT
                pe.wait_ge(hidden_ready, FT * (i + 1) - 2)
                for d in range(4):
                    bank = bank_for(("down", i, d))
                    for e in range(2):
                        for k in range(FT):
                            flat = (2 * d + e) * FT + k
                            w = base + flat // HALF
                            if flat % HALF == 0:
                                half_ready(w)
                            if d == 0 and e == 0 and k >= FT - 2:
                                pe.wait_ge(hidden_ready, FT * i + k + 1)
                            s = split[:, w % SPLIT_SLOTS, :, :]
                            t = slice(flat % HALF * P, (flat % HALF + 1) * P)
                            ins = three(bank[:, e * T:(e + 1) * T], s[:, 0, t], s[:, 1, t], hidden[:, 0, k, :],
                                        hidden[:, 1, k, :], k == 0, k == FT - 1)
                            last = e == 1 and k == FT - 1
                            if last:
                                ins.then_inc(lin_filled, 1)
                            elif flat % HALF == HALF - 1:
                                ins.then_inc(halves_used, 1)

            def transposes(key, t):
                bank = bank_for(key)
                s = key[-1]
                for i in range(4):
                    ins = nc.tensor.transpose(bank[:, i * P:(i + 1) * P],
                                              t[:, 2 * s + i // 2, (i % 2) * CH:(i % 2 + 1) * CH], ident)
                ins.then_inc(lin_filled, 1)

            def rwkv(l):
                base = MIX_AT[l]
                norm(3 * l + 1)
                for s in range(13):
                    two_tiles(base + 2 * s, ("shift", l, s), (HH, HH), h_wait(3 * l + 1) if s == 0 else None)
                pe.wait_ge(small_loaded, 80 * (l + 1))
                pe.wait_ge(tanh_ready, l + 1)
                for s in range(4):
                    bank = bank_for(("z", l, s))
                    j = s // 2
                    M(bank, lora[0:64, 0, j * CH:(j + 1) * CH], w2a2[0:64, (s % 2) * 512:(s % 2 + 1) * 512],
                      start=True, stop=True).then_inc(lin_filled, 1)
                for s in range(4):
                    bank = bank_for(("a", l, s))
                    for i in range(2):
                        c = 2 * s + i
                        ins = M(bank[:, i * T:(i + 1) * T], w2a2[64:128, c * P:(c + 1) * P], lora[64:128, 0, :],
                                start=True, stop=True)
                    ins.then_inc(lin_filled, 1)
                if l:
                    for s in range(4):
                        bank = bank_for(("vr", l, s))
                        for i in range(2):
                            c = 2 * s + i
                            ins = M(bank[:, i * T:(i + 1) * T], v2[0:32, c * P:(c + 1) * P], lora[0:32, 1, :],
                                    start=True, stop=True)
                        ins.then_inc(lin_filled, 1)
                for s in range(4):
                    two_tiles(base + 2 * (13 + s), ("va", l, s), (HH, HH))
                for s in range(4):
                    bank = bank_for(("kk", l, s))
                    p = PIECE["kk", l, s]
                    pe.wait_ge(squared, p + 1)
                    M(bank, head_w, pieces[:, p % 2, :, :], start=True, stop=True).then_inc(lin_filled, 1)
                for s in range(4):
                    two_tiles(base + 2 * (17 + s), ("u", l, s), (HH, HH))
                for s in range(4):
                    bank = bank_for(("bonus", l, s))
                    pe.wait_ge(rk_ready, 4 * l + s + 1)
                    M(bank, head_w, pair[:, s % 2, :, :], start=True, stop=True).then_inc(lin_filled, 1)
                for s in range(4):
                    transposes(("vt", l, s), v_)
                bank = bank_for(("vmean", l))
                wait_emptied(pe, ("va", l, 3))
                for k in range(DT):
                    ins = M(bank[:, 0:T], mean_w, va[:, k, :], start=(k == 0), stop=(k == DT - 1))
                ins.then_inc(lin_filled, 1)
                sums(bank_for(("vvar", l)), [("vvar", l, s) for s in range(4)])
                for s in range(4):
                    pe.wait_ge(va_ready, 4 * l + s + 1)
                    transposes(("vat", l, s), va)
                pe.wait_ge(zeroed, l + 1)
                for s in range(4):
                    bank = bank_for(("sgu", l, s))
                    wait_emptied(pe, ("vat", l, s))
                    for i in range(4):
                        g, j = 2 * s + i // 2, i % 2
                        ins = M(bank[:, i * P:(i + 1) * P], va[:, g, j * CH:(j + 1) * CH], ws_t[:, g, :],
                                start=True, stop=True)
                    ins.then_inc(lin_filled, 1)
                pe.wait_ge(decay_ready, 4 * l + 4)
                for c in range(DT):
                    solve(l, c)
                for s in range(4):
                    bank = bank_for(("gmean", l, s))
                    wait_emptied(pe, ("y", l, 2 * s + 1))
                    M(bank, head_w, r_[:, 2 * s:2 * s + 2, :], start=True, stop=True).then_inc(lin_filled, 1)
                for s in range(4):
                    bank = bank_for(("gvar", l, s))
                    p = PIECE["gvar", l, s]
                    pe.wait_ge(squared, p + 1)
                    M(bank, head_w, pieces[:, p % 2, :, :], start=True, stop=True).then_inc(lin_filled, 1)
                YA, YB = (ya_hi, ya_lo), (yb_hi, yb_lo)
                for n in range(DT):
                    two_tiles(base + 2 * (21 + 2 * n), ("gate", l, n), (HH, HH))
                    if n == 0:
                        pe.wait_ge(ya_ready, 4 * l + 4)
                        pe.wait_ge(yb_ready, 4 * l + 4)
                    two_tiles(base + 2 * (22 + 2 * n), ("proj", l, n), (YA, YB))
                for d in range(4):
                    two_tiles(OUT_AT[l] + 2 * d, ("out", l, d), (HH, HH),
                              (lambda i: pe.wait_ge(merged_split, 4 * l + i + 1)) if d == 0 else None)

            def solve(l, c):
                q = DT * l + c
                for j in range(NCH):
                    ins = M(sv[:, 4, j * (CH + 1):(j + 1) * (CH + 1)], decay[:, j, c * P:(c + 1) * P], tri,
                            start=True, stop=True)
                ins.then_inc(cum_done, 1)
                pe.wait_ge(scaled, q + 1)
                bank = bank_for(("kbt", l, c))
                for i in range(2):
                    ins = nc.tensor.transpose(bank[:, i * P:(i + 1) * P], kb0[:, i, :], ident)
                ins.then_inc(lin_filled, 1)
                for n in range(4):
                    hh, j = n // 2, n % 2
                    o = slice((n % 2) * 2 * CH, (n % 2 + 1) * 2 * CH)
                    M(sv[:, n // 2, o], beta[:, hh, j, :], ar[:, j, :], start=True, stop=True)
                    M(sv[:, 2 + n // 2, o], kappa[:, hh, j, :], ar[:, j, :], start=True, stop=True)
                    ins = M(sv[:, 4, n * CH:(n + 1) * CH], ar[:, j, 0:CH], beta[:, hh, j, :], start=True, stop=True)
                ins.then_inc(scores_done, 1)
                NL = len(LEVELS)
                for s in range(NL):
                    pe.wait_ge(inverse_ready, (NL + 1) * q + s + 1)
                    for n in range(4):
                        ins = M(sv[:, 0, n * CH:(n + 1) * CH], gb[:, n, 0:CH], t_inv[:, n, :], start=True, stop=True)
                    ins.then_inc(z_done, 1)
                    pe.wait_ge(z_ready, NL * q + s + 1)
                    for n in range(4):
                        o = slice(n * CH, (n + 1) * CH)
                        if s < NL - 1:
                            M(sv[:, 1, o], q_inv[:, n, :], z_neg[:, n, :], start=True, stop=True)
                        ins = M(sv[:, 2, o], z_neg[:, n, :], q_inv[:, n, :], start=True, stop=True)
                    ins.then_inc(p_done, 1)
                b3 = sv[:, 3, :]
                v_tok = lambda j, hh: v_[:, c, j * CH + 64 * hh:j * CH + 64 * hh + 64]
                pe.wait_ge(inverse_ready, (NL + 1) * (q + 1))
                wait_emptied(pe, ("vt", l, c // 2))
                for hh in range(2):
                    ins = M(b3[:, 64 * hh:64 * hh + 64], gk[:, 2 * hh, 0:CH], v_tok(0, hh), start=True, stop=True)
                ins.then_inc(rec_pe, 1)
                pe.wait_ge(rec_dve, 5 * q + 1)
                for hh in range(2):
                    ins = M(b3[:, P + 64 * hh:P + 64 * hh + 64], q_inv[:, 2 * hh, :], rh[:, 64 * hh:64 * hh + 64],
                            start=True, stop=True)
                ins.then_inc(rec_pe, 1)
                pe.wait_ge(rec_dve, 5 * q + 2)
                wait_emptied(pe, ("kbt", l, c))
                M(b3[:, 2 * P:3 * P], kbt[:, 0, :], v_[:, c, 0:P], start=True, stop=False)
                M(b3[:, 2 * P:3 * P], kbt[:, 1, :], nu[:], start=False, stop=True).then_inc(rec_pe, 1)
                y = bank_for(("y", l, c))
                for hh in range(2):
                    w = slice(64 * hh, 64 * hh + 64)
                    M(y[w, 0:CH], v_tok(0, hh), gk[:, 2 * hh, CH:2 * CH], start=True, stop=False)
                    M(y[w, 0:CH], nu[:, w], gb[:, 2 * hh, CH:2 * CH], start=False, stop=True)
                pe.wait_ge(rec_dve, 5 * q + 3)
                for hh in range(2):
                    M(b3[:, 3 * P + 64 * hh:3 * P + 64 * hh + 64], gk[:, 2 * hh + 1, 0:CH], v_tok(1, hh),
                      start=(hh == 0), stop=False, skip_group_check=True)
                M(b3[:, 3 * P:4 * P], ar[:, 1, 0:CH], s0[:], start=False, stop=True, skip_group_check=True)\
                    .then_inc(rec_pe, 1)
                pe.wait_ge(rec_dve, 5 * q + 4)
                for hh in range(2):
                    ins = M(b3[:, 64 * hh:64 * hh + 64], q_inv[:, 2 * hh + 1, :], rh[:, 64 * hh:64 * hh + 64],
                            start=True, stop=True)
                ins.then_inc(rec_pe, 1)
                M(y[:, CH:2 * CH], s0[:], ar[:, 1, CH:2 * CH], start=True, stop=False, skip_group_check=True)
                pe.wait_ge(rec_dve, 5 * q + 5)
                for hh in range(2):
                    w = slice(64 * hh, 64 * hh + 64)
                    M(y[w, CH:2 * CH], v_tok(1, hh), gk[:, 2 * hh + 1, CH:2 * CH], start=False, stop=False,
                      skip_group_check=True)
                    ins = M(y[w, CH:2 * CH], nu[:, w], gb[:, 2 * hh + 1, CH:2 * CH], start=False, stop=(hh == 1),
                            skip_group_check=True)
                ins.then_inc(lin_filled, 1)

            def attention(l):
                base = MIX_AT[2 + l]
                ng = (1, 3)[l]
                norm(8 + 3 * l)
                half = base

                def finish_qk(g, c):
                    bank = bank_for(("ss", l, g, c))
                    p = PIECE["ss", l, g, c]
                    pe.wait_ge(squared, p + 1)
                    M(bank, head_w, pieces[:, p % 2, :, :], start=True, stop=True).then_inc(lin_filled, 1)
                    if l:
                        bank = bank_for(("rot", l, g, c))
                        pe.wait_ge(small_loaded, 160 + 96)
                        wait_emptied(pe, ("qk", l, g, c))
                        M(bank, rope_m[:], qkg[:, (DT * g + c) % 2, :, :], start=True, stop=True).then_inc(lin_filled, 1)

                for g in range(ng):
                    for c in range(DT):
                        two_tiles(half, ("qk", l, g, c), (HH, HH), h_wait(8 + 3 * l) if g == 0 and c == 0 else None)
                        half += 2
                        if c:
                            finish_qk(g, c - 1)
                    finish_qk(g, DT - 1)
                    for s in range(4):
                        tokens_major(half, ("v", l, g, s), 2 * P)
                        half += 2
                if l == 0:
                    tokens_major(half, ("f", 0), HEADS)
                    pe.wait_ge(small_loaded, 160 + 48)
                pe.wait_ge(qk_ready, DT if l == 0 else 4 * DT)
                wait_emptied(pe, ("v", l, ng - 1, 3))
                for hd in range(HEADS):
                    n = HEADS * l + hd
                    c, hh = hd // 2, hd % 2
                    w = slice(64 * hh, 64 * hh + 64)
                    if hd:
                        pe.wait_ge(max_ready, n)
                    if l == 0:
                        pe.wait_ge(lsb_ready, hd + 1)
                    for g in range(ng):
                        b = sv[:, g, :]
                        q_, kx = qk[:, g, 2 * c, :], qk[:, g, 2 * c + 1, :]
                        more = l == 0
                        ins = M(b[:, 0:P], q_[w, 0:P], kx[w, 0:P], start=True, stop=not more)
                        if more:
                            M(b[:, 0:P], ls_b[:, 0, :], cum_rhs[:, 0:P], start=False, stop=True)
                        ins = M(b[:, P:3 * P], q_[w, P:2 * P], kx[w, :], start=True, stop=not more,
                                skip_group_check=True)
                        if more:
                            M(b[:, P:3 * P], ls_b[:, 0, :], cum_rhs[:], start=False, stop=False, skip_group_check=True)
                            ins = M(b[:, 2 * P:3 * P], ls_b[:, 1, :], cum_rhs[:, 0:P], start=False, stop=True,
                                    skip_group_check=True)
                    ins.then_inc(logits_done, 1)
                    pe.wait_ge(norm_ready, n + 1)
                    for g in range(ng):
                        m = hd if l == 0 else HEADS + GROUPS * hd + g
                        b = sv[:, 3 + m % 2, :]
                        if m >= 2:
                            pe.wait_ge(pt_ready, m - 1)
                        for i in range(3):
                            ins = nc.tensor.transpose(b[:, i * P:(i + 1) * P], logits[:, g, i * P:(i + 1) * P], ident)
                        ins.then_inc(pt_done, 1)
                    if hh == 0:
                        o = bank_for(("o", l, c))
                    pe.wait_ge(pt_ready, hd + 1 if l == 0 else HEADS + GROUPS * (hd + 1))
                    vt = lambda g, j: vtok[:, g, j, hd * HD:(hd + 1) * HD]
                    for g in range(ng):
                        M(o[w, 0:P], vt(g, 0), pt[:, g, 0:P], start=(g == 0), stop=(g == ng - 1))
                    for g in range(ng):
                        M(o[w, P:2 * P], vt(g, 0), pt[:, g, P:2 * P], start=(g == 0), stop=False)
                        ins = M(o[w, P:2 * P], vt(g, 1), pt[:, g, 2 * P:3 * P], start=False, stop=(g == ng - 1))
                    if hh:
                        ins.then_inc(lin_filled, 1)
                wait_emptied(pe, ("o", l, DT - 1))
                OO = (o_hi, o_lo)
                for d in range(4):
                    two_tiles(OUT_AT[2 + l] + 2 * d, ("out", 2 + l, d), (OO, OO))

            pe.wait_ge(consts_loaded, 64)
            for l in range(2):
                ffn(2 * l)
                rwkv(l)
                ffn(2 * l + 1)
            norm(6)
            for l in range(2):
                ffn(4 + 2 * l)
                attention(l)
                ffn(5 + 2 * l)


def constants():
    i = np.arange(P)
    const = np.zeros((P, NCONST), np.float32)

    def put(name, value):
        a, n = CONST[name]
        const[:, a:a + n] = value

    put("ident", np.eye(P))
    put("mean", 1.0 / D)
    put("head", i[:, None] // HD == i[None, :] // HD)
    mid = CH // 2 - 1
    put("tri", -DECAY_SCALE * ((i[:, None] <= np.arange(CH + 1)[None, :] - 1).astype(np.float64)
                               - (i[:, None] <= mid)))
    put("mask", np.concatenate([i[:, None] < i[None, :], i[:, None] <= i[None, :]], 1))
    below = (i[:, None] % 2 == 1) & (i[None, :] == i[:, None] - 1)
    put("neg2", -1.0 * below)
    put("neg2t", -1.0 * below.T)
    put("one", 1.0)
    levels = np.zeros((P, 2, len(LEVELS), P), np.float32)
    for s, m in enumerate(LEVELS):
        b = (i[:, None] // m % 2 == 1) & (i[None, :] // m == i[:, None] // m - 1)
        levels[:, 0, s], levels[:, 1, s] = b, b.T
    rope = np.zeros((P, P), np.float32)
    for base in (0, HD):
        for f in range(8):
            rope[base + f + 8, base + f] = -1.0
            rope[base + f, base + f + 8] = 1.0
    cum = np.concatenate([i[:, None] <= i[None, :], np.ones((P, P), bool)], 1) * np.float32(-(HD ** 0.5))

    def allowed(window, dilation):
        t, s = np.arange(T)[:, None], np.arange(T)[None, :]
        ok = (s <= t) & ((t - s) % dilation == 0) & (t - s <= window)
        m = np.where(ok, 0.0, NEG).astype(np.float32)
        return np.concatenate([m[:P, :P], m[P:, :]], 1)

    fox = allowed(T, 1)
    dil = np.stack([allowed(w, d) for w, d in ((128, 1), (512, 4), (2048, 16))], 1)
    freq = np.float32(500000.0) ** (-(np.arange(8, dtype=np.float32) * np.float32(2.0) / np.float32(16)))
    inv = np.zeros((P, 1), np.float32)
    for base in (0, 8, HD, HD + 8):
        inv[base:base + 8, 0] = freq
    return {"const": const, "level_masks": levels, "rope_m": rope, "cum_rhs": cum.astype(np.float32),
            "fox_mask": fox, "dil_mask": np.ascontiguousarray(dil), "inv_freq": inv}


def kernel(**inputs):
    import concourse.bacc as bacc
    from concourse.bass_utils import run_bass_kernel_spmd

    a = {k: np.asarray(v) for k, v in inputs.items()}
    fixed = constants()

    def tiles(w):
        w = np.concatenate([w, np.zeros((D, -w.shape[1] % P), w.dtype)], 1)
        return w.reshape(DT, P, -1, P).transpose(2, 1, 0, 3)

    def units(pairs_):
        return [np.stack(p, 1).reshape(P, TPU * P) for p in pairs_]

    def down(w):
        w = w.reshape(FT, P, DT, P).transpose(1, 2, 0, 3).reshape(P, DOWN_UNITS, TPU * P)
        return list(w.transpose(1, 0, 2))

    def moving(w):
        w = np.concatenate([w, np.zeros((D, 2 * P - w.shape[1]), w.dtype)], 1)
        return w.reshape(DT, P, 2 * P).transpose(1, 0, 2).reshape(P, TPU * P)

    stream = []

    def ffn(gate, up, w_down):
        stream.extend(units(zip(tiles(gate), tiles(up))))
        stream.extend(down(w_down))

    for l in range(2):
        gu = a["ffn1_w_gu"][l]
        ffn(gu[:, :FF], gu[:, FF:], a["ffn1_w_down"][l])
        w = a["w_in_first"] if l == 0 else a["w_in_rest"][0]
        w = tiles(np.concatenate([w, np.zeros((D, 58 * P - w.shape[1]), w.dtype)], 1))
        pa, pb = tiles(a["w_proj_a"][l]), tiles(a["w_proj_b"][l])
        order = [(56, 57)] + [(32 + c, 40 + c) for c in range(8)] + [(48 + c, 49 + c) for c in range(0, 8, 2)]
        order += [(24 + c, 25 + c) for c in range(0, 8, 2)] + [(16 + c, 17 + c) for c in range(0, 8, 2)]
        stream.extend(units((w[m], w[n]) for m, n in order))
        for n in range(DT):
            stream.extend(units([(w[n], w[8 + n]), (pa[n], pb[n])]))
        wo = tiles(a["w_out"][l])
        stream.extend(units((wo[n], wo[n + 1]) for n in range(0, 8, 2)))
        gu = a["ffn2_w_gu"][l]
        ffn(gu[:, :FF], gu[:, FF:], a["ffn2_w_down"][l])
    for l in range(2):
        ffn(a["ffn_w_gate_2"][l, 0], a["ffn_w_up_2"][l, 0], a["ffn_w_down_2"][l, 0])
        w_in, w_o = (a["fox_w_in_2"][0], a["fox_w_out_2"][0]) if l == 0 else (a["dil_w_in_2"][0], a["dil_w_out_2"][0])
        for g in range((1, 3)[l]):
            w = w_in[:, 3 * D * g:3 * D * (g + 1)]
            t = tiles(w[:, :2 * D])
            stream.extend(units((t[c], t[8 + c]) for c in range(DT)))
            stream.extend(moving(w[:, 2 * D + 256 * s:2 * D + 256 * (s + 1)]) for s in range(4))
        if l == 0:
            stream.append(moving(w_in[:, 3 * D:]))
        wo = tiles(w_o)
        stream.extend(units((wo[n], wo[n + 1]) for n in range(0, 8, 2)))
        ffn(a["ffn_w_gate_2"][l, 1], a["ffn_w_up_2"][l, 1], a["ffn_w_down_2"][l, 1])

    column = lambda v: v.reshape(-1, P).T
    cols = np.zeros((P, NCOLS), np.float32)

    def put(key, v):
        n = v.shape[-1] // P
        cols[:, COL[key]:COL[key] + n] = column(v)

    for l in range(2):
        for name, key in (("ffn1_norm",) * 2, ("mix_norm",) * 2, ("ffn2_norm",) * 2, ("ln_g", "sgu_ln_g"),
                          ("ln_b", "sgu_ln_b"), ("a0", "rwkv_a0"), ("k_k", "rwkv_k_k"), ("k_a", "rwkv_k_a"),
                          ("gn_g", "rwkv_gn_g"), ("gn_b", "rwkv_gn_b")):
            put((name, l), a[key][l])
        put(("r_k", l), a["rwkv_r_k"][l].reshape(-1))
        mu = a["mu_first"] if l == 0 else a["mu_rest"][0]
        put(("mu", l), np.concatenate([mu, np.zeros(26 * P - mu.shape[0], mu.dtype)]))
    put(("v0", 1), a["rwkv_v0"][0])
    put("final_norm", a["final_norm"])
    put("norm_g", a["norm_g_2"].reshape(-1))
    put("c", a["c_2"][0])
    twice = lambda v: np.concatenate([v, v])
    put("fox_g", np.concatenate([twice(a["fox_q_g_2"][0]), twice(a["fox_k_g_2"][0])]))
    put("dil_g", np.concatenate([twice(a[n][0][g]) for g in range(3) for n in ("dil_q_g_2", "dil_k_g_2")]))
    cols[:, COL["inv_freq"]:COL["inv_freq"] + 1] = fixed.pop("inv_freq")

    v2 = a["rwkv_v2"][0]
    arrays = {
        "x": a["x"][0].T.reshape(DT, P, T).transpose(1, 0, 2),
        "stream": np.stack(stream),
        "mod_w": a["mod_w_2"].reshape(2, DT, P, 36, 2 * P).transpose(0, 3, 2, 1, 4).reshape(72, P, TPU * P),
        "mod_b": column(a["mod_b_2"].reshape(-1)),
        "cols": cols,
        "w2a2": np.concatenate([a["rwkv_w2"], a["rwkv_a2"]], 1),
        "v2": np.stack([v2, v2]),
        "w0": a["rwkv_w0"],
        "bs": a["sgu_b_s"].reshape(2, -1),
        "ws_t": a["sgu_w_s"].transpose(0, 3, 1, 2),
        "b_f": a["fox_b_f_2"][0],
        "positions": a["positions_2"][0],
        **fixed,
    }
    arrays = {k: np.ascontiguousarray(v) for k, v in arrays.items()}
    nc = bacc.Bacc("TRN2", target_bir_lowering=False, num_devices=1)
    src = {k: nc.dram_tensor(f"in_{k}", v.shape, mybir.dt.from_np(v.dtype), kind="ExternalInput").ap()
           for k, v in arrays.items()}
    out = nc.dram_tensor("out", (P, DT, T), F32, kind="ExternalOutput").ap()
    build_program(nc, src, out)
    r = run_bass_kernel_spmd(nc, [{f"in_{k}": v for k, v in arrays.items()}], core_ids=[0])
    y = r.results[0]["out"]
    return np.ascontiguousarray(y.transpose(1, 0, 2).reshape(D, T).T)[None]
```

```python
import numpy as np
import concourse.bass as bass
from concourse import mybir

F32 = mybir.dt.float32
F32R = mybir.dt.float32r
I32 = mybir.dt.int32
I8 = mybir.dt.int8
ALU = mybir.AluOpType
ACT = mybir.ActivationFunctionType
AX = mybir.AxisListType

P = 128
T = 256
D = 1024
DT = D // P
FF = 2816
FT = FF // P
HEADS = 16
HD = 64
CH = 128
NCH = T // CH
TPU = 16
HALF = TPU // 2
DOWN_UNITS = FT * DT // TPU
FFN_UNITS = FT + DOWN_UNITS
NORM_EPS = 1e-6
LN_EPS = 1e-5
GN_EPS = 64e-5
DECAY_SCALE = float(np.exp(-0.5))
NEG = -1e30
GROUPS = 3
LEVELS = (2, 4, 8, 16, 32, 64)
MOD_UNITS = 72
RAW_SLOTS = 3
SPLIT_SLOTS = 4
AHEAD = 3

COL = {}
_at = 0
for _l in range(2):
    for _name, _n in (("ffn1_norm", 8), ("mix_norm", 8), ("ffn2_norm", 8), ("ln_g", 8), ("ln_b", 8),
                      ("mu", 26), ("a0", 8), ("v0", 8), ("k_k", 8), ("k_a", 8), ("r_k", 8),
                      ("gn_g", 8), ("gn_b", 8)):
        COL[_name, _l] = _at
        _at += _n
for _name, _n in (("final_norm", 8), ("norm_g", 48), ("c", 8), ("fox_g", 2), ("dil_g", 6), ("inv_freq", 1)):
    COL[_name] = _at
    _at += _n
NCOLS = _at
COLS_FIRST = COL["norm_g"]

CONST = {}
_at = 0
for _name, _n in (("ident", P), ("mean", P), ("head", P), ("tri", 129), ("mask", 2 * P), ("neg2", P), ("neg2t", P), ("one", 1)):
    CONST[_name] = (_at, _n)
    _at += _n
NCONST = _at


FIRST_HALF = ("cum", "score0", "score1", "score2", "score3", "low", "z0", "p0", "t0", "z1", "p1", "t1",
              "z2", "p2", "t2")
SECOND_HALF = ("z3", "p3", "t3", "z4", "p4", "t4", "z5", "p5", "rhs0", "u0", "st", "rhs1", "u1", "y", "end")
MOD_STEPS = range(0, 20, 2)
MOD_STAGES = ("z4", "u0")
MOD_AT = {}


class Plan:

    def __init__(self):
        self.uses = {}
        self.emptied = {"act": 0, "dve": 0}
        self.order = []
        self.unit = {}
        self.units = 0
        self.items = []
        self.item_of = {}
        self.mods = 0

    def use(self, key, engine):
        self.emptied[engine] += 1
        self.uses[key] = (len(self.order), engine, self.emptied[engine])
        self.order.append(key)

    def stream(self, key, count=1):
        self.unit[key] = self.units
        self.units += count

    def load_units(self, count=1):
        for _ in range(count):
            n = sum(kind == "unit" for kind, _ in self.items)
            self.item_of["unit", n] = len(self.items)
            self.items.append(("unit", n))

    def load_mod(self):
        self.item_of["mod", self.mods] = len(self.items)
        self.items.append(("mod", self.mods))
        self.mods += 1


def make_plan():
    p = Plan()

    def ffn(i):
        p.use(("norm", ffn_norm(i)), "dve")
        p.stream(("ffn", i), FFN_UNITS)
        for j in range(FT):
            p.use(("gu", i, j), "dve")
            if i < 4 and j in MOD_STEPS:
                MOD_AT["ffn", i, j] = len(MOD_AT)
            if i < 4 and j - 1 in MOD_STEPS:
                p.use(("mod", MOD_AT["ffn", i, j - 1]), "dve")
        for d in range(DT // 2):
            p.use(("down", i, d), "dve")

    for l in range(2):
        ffn(2 * l)
        p.use(("norm", 3 * l + 1), "dve")
        p.stream(("mix", l), 37)
        for s in range(13):
            p.use(("shift", l, s), "act")
        for s in range(4):
            p.use(("z", l, s), "dve")
        for s in range(4):
            p.use(("a", l, s), "act")
        if l:
            for s in range(4):
                p.use(("vr", l, s), "act")
        for s in range(4):
            p.use(("va", l, s), "act")
        for s in range(4):
            p.use(("kk", l, s), "dve")
        for s in range(4):
            p.use(("u", l, s), "act")
        for s in range(4):
            p.use(("bonus", l, s), "dve")
        for s in range(4):
            p.use(("vt", l, s), "act")
        p.use(("vmean", l), "dve")
        p.use(("vvar", l), "dve")
        for s in range(4):
            p.use(("vat", l, s), "act")
        for s in range(4):
            p.use(("sgu", l, s), "dve")
        for c in range(-1, DT):
            for a, b in zip(SECOND_HALF, FIRST_HALF):
                if b == "cum" and 0 <= c:
                    for n in range(2):
                        MOD_AT["solve", l, c, n] = len(MOD_AT)
                if c >= 0 and a in MOD_STAGES:
                    p.use(("mod", MOD_AT["solve", l, c, MOD_STAGES.index(a)]), "dve")
                if c >= 0 and a == "st":
                    p.use(("y", l, c), "act")
                if c < DT - 1:
                    if b == "cum":
                        p.use(("cum", l, c + 1), "act")
                    elif b == "score0":
                        p.use(("kbt", l, c + 1), "act")
                    if b[:5] == "score":
                        p.use(("score", l, c + 1, int(b[5])), "dve")
                    elif b == "low":
                        p.use(("low", l, c + 1), "dve")
        for s in range(4):
            p.use(("gmean", l, s), "dve")
        for s in range(4):
            p.use(("gvar", l, s), "dve")
        if l == 0:
            for s in range(4):
                p.use(("vback", l, s), "act")
        for n in range(DT):
            p.use(("gate", l, n), "act")
            p.use(("proj", l, n), "dve")
        p.stream(("out", l), 4)
        for d in range(4):
            p.use(("out", l, d), "dve")
        ffn(2 * l + 1)
    p.use(("norm", 6), "dve")
    for l in range(2):
        ffn(4 + 2 * l)
        p.use(("norm", 8 + 3 * l), "dve")
        p.stream(("mix", 2 + l), (13, 36)[l])
        for g in range((1, 3)[l]):
            for c in range(DT):
                p.use(("qk", l, g, c), "dve")
                if c:
                    p.use(("ss", l, g, c - 1), "dve")
                    if l:
                        p.use(("rot", l, g, c - 1), "dve")
            p.use(("ss", l, g, DT - 1), "dve")
            if l:
                p.use(("rot", l, g, DT - 1), "dve")
            for s in range(4):
                p.use(("v", l, g, s), "act")
        if l == 0:
            p.use(("f", 0), "dve")
        for c in range(DT):
            p.use(("o", l, c), "dve")
        p.stream(("out", 2 + l), 4)
        for d in range(4):
            p.use(("out", 2 + l, d), "dve")
        ffn(5 + 2 * l)
    for l in range(2):
        for i in (2 * l, 2 * l + 1):
            done = 0
            for j in range(FT):
                if j in MOD_STEPS:
                    p.load_units(min(j + 3, FFN_UNITS) - done)
                    done = min(j + 3, FFN_UNITS)
                    p.load_mod()
            p.load_units(FFN_UNITS - done)
            if i == 2 * l:
                p.load_units(22)
                for _ in range(2 * DT):
                    p.load_mod()
                p.load_units(37 - 22 + 4)
    p.load_units(p.units - sum(kind == "unit" for kind, _ in p.items))
    assert p.mods == MOD_UNITS == len(MOD_AT)
    return p


def ffn_norm(i):
    return (0, 2, 3, 5, 7, 9, 10, 12)[i]


PLAN = make_plan()


def build_program(nc, src, out):
    sem = {}

    def signal(name):
        sem[name] = nc.alloc_semaphore(name)
        return sem[name]

    at = [nc.sbuf_base + (-nc.sbuf_base) % 64]

    def place(name, shape, dt=F32, where=None):
        size = int(np.prod(shape[1:])) * (1 if dt == I8 else 4)
        size += -size % 32
        if where is None:
            where = at[0]
            at[0] += size
        return nc.alloc_sbuf_tensor_at(name, list(shape), dt, offset=where)

    raw = place("raw_units", [P, RAW_SLOTS, TPU * P])
    split = place("split_halves", [P, SPLIT_SLOTS, 2, HALF * P], F32R)
    x = place("x", [P, DT, T])
    h = place("h_split", [P, 2, DT, T], F32R)
    pieces_at = at[0]
    pieces = place("squares", [P, 2, 2, T])
    v_first = place("v_first", [P, DT, T])
    const = place("constants", [P, NCONST])
    level_masks = place("level_masks", [P, 2, len(LEVELS), P], I8)
    cols = place("columns", [P, NCOLS])
    mod = place("modulation", [P, 144])
    mod_b = place("modulation_bias", [P, 144])
    gain2 = place("modulated_gain", [P, 6, DT])
    gate2 = place("residual_gate", [P, 6, DT])
    one_less_ka = place("one_less_ka", [P, 2, DT])
    rstd = place("rstd", [P, T])
    state_scale = nc.alloc_sbuf_tensor_at("state_scale", [P, 2], F32, offset=pieces_at + 2112)
    arena = at[0] + (-at[0]) % 32
    KB = 1024

    def over(name, shape, kb, dt=F32):
        return place(name, shape, dt, where=arena + int(kb * KB))

    hidden = over("hidden_split", [P, 2, FT, T], 0, F32R)
    mod_acc = over("modulation_sums", [P, 2, 2 * P], 104.5)
    silu = over("silu", [P, 3, T], 62)
    product = over("gated", [P, 3, T], 65)
    r_ = over("r", [P, DT, T], 0)
    k_ = over("k", [P, DT, T], 8)
    v_ = over("v", [P, DT, T], 16)
    decay = over("decay", [P, NCH, D], 24)
    a_ = over("a", [P, DT, T], 32)
    kk = over("kk", [P, DT, T], 40)
    va = over("va", [P, DT, T], 48)
    u_ = over("u", [P, DT, T], 56)
    bonus = v_first
    lora = over("lora", [P, 2, T], 72)
    ws_t = over("spatial_t", [P, DT, CH], 74)
    B = 78
    raw_shift = over("raw_shift", [P, 2, 2, T + 1], B)
    diff = over("diff", [P, 2, T], B + 4.25)
    w2a2 = over("w2a2", [P, D], B + 6.25)
    v2 = over("v2", [32, D], B + 10.25)
    w0_b = over("w0_rows", [P, D], B + 14.25)
    bs_b = over("bs_rows", [P, D], B + 18.25)
    pair = over("pair", [P, 2, 2, T], B + 22.25)
    e_pos = nc.alloc_sbuf_tensor_at("exp_pos", [P, NCH, CH + 1], F32, offset=pieces_at)
    e_neg = nc.alloc_sbuf_tensor_at("exp_neg", [P, NCH, CH + 1], F32, offset=pieces_at + 1056)
    gbk = (over("scores_0", [P, 4, 4 * CH], 64), over("scores_1", [P, 4, 4 * CH], 72))
    t_inv = over("inverse", [P, 2, 4, CH], 80)
    q_inv = over("inverse_t", [P, 2, 4, CH], 84)
    z_neg = over("z_neg", [P, 2, 4, CH], 88)
    ar = over("alpha_rho", [P, 2, NCH, 2 * CH], 92)
    beta = over("beta", [P, 2, NCH, CH], 96)
    kappa = over("kappa", [P, 2, NCH, CH], 98)
    kbt = over("kappa_beta_tok", [P, 2, 2, P], 100)
    kb0 = over("kappa_beta_0", [P, 2, CH], 102)
    rh = over("rhs", [P, P], 103)
    nu = over("neg_u", [P, P], 103.5)
    s0 = over("state", [P, P], 104)
    ya_hi = over("ya_hi", [P, DT, T], 48, F32R)
    ya_lo = over("ya_lo", [P, DT, T], 56, F32R)
    yb_hi = over("yb_hi", [P, DT, T], 8, F32R)
    yb_lo = over("yb_lo", [P, DT, T], 0, F32R)
    gate_sig = over("gate_sigmoids", [P, 2, 2, T], 24)
    merged = over("merged", [P, DT, T], 32)
    level_floats = over("level_floats", [P, 2, len(LEVELS), P], 98)
    qk = over("qk", [P, GROUPS, 2 * DT, T], 0)
    vtok = over("v_tokens", [P, GROUPS, NCH, D], 48)
    amask = over("attention_mask", [P, GROUPS, 3 * P], 72)
    logits = (over("logits_0", [P, GROUPS, 3 * P], 76.5), over("logits_1", [P, GROUPS, 3 * P], 87.5))
    pt = (over("probs_t_0", [P, GROUPS, 3 * P], 81), over("probs_t_1", [P, GROUPS, 3 * P], 92))
    cos = over("cos", [P, T], 85.5)
    sin = over("sin", [P, T], 86.5)
    qkg = over("qk_gained", [P, 2, 2, T], 87.5)
    ssr = over("qk_rstd", [P, 2, 2, T], 91.5)
    rot = over("rotated", [P, 2, T], 95.5)
    rope_m = over("rope_matrix", [P, P], 97.5)
    cum_rhs = over("cum_rhs", [P, 2 * P], 98)
    ls = over("log_sigmoid", [P, NCH, HEADS], 99)
    ls_t = over("log_sigmoid_t", [P, NCH, HEADS], 99.125)
    bf_b = over("b_f_rows", [P, HEADS], 99.25)
    ls_b = over("log_sigmoid_b", [P, NCH, P], 99.5)
    stat = over("attention_stats", [P, 2, 8], 100.5)
    pos_i = over("positions", [P, T], 100.625, I32)
    ang = over("angle", [P, T], 101.625)
    o_hi = over("o_hi", [P, DT, T], 0, F32R)
    o_lo = over("o_lo", [P, DT, T], 16, F32R)

    lin = nc.alloc_psum_tensor("linear_banks", [P, 3, 512], F32)
    sv = nc.alloc_psum_tensor("solve_banks", [P, 5, 512], F32)

    def c_(name):
        a, n = CONST[name]
        return const[:, a:a + n]

    ident, mean_w, head_w, tri, mask = (c_(n) for n in ("ident", "mean", "head", "tri", "mask"))

    def col(name, i=0, l=None):
        a = COL[name if l is None else (name, l)] + i
        return cols[:, a:a + 1]

    def wide(ap, n, dim=1):
        return ap.unsqueeze(dim).to_broadcast([P, n, ap.shape[-1]])

    consts_loaded = signal("consts_loaded")
    x_loaded = signal("x_loaded")
    raw_loaded = [signal(f"raw_loaded_{s}") for s in range(RAW_SLOTS)]
    small_loaded = signal("small_loaded")
    hi_ready = signal("hi_ready")
    lo_ready = signal("lo_ready")
    halves_used = signal("halves_used")
    lin_filled = signal("lin_filled")
    emptied = {"act": signal("emptied_by_act"), "dve": signal("emptied_by_dve")}
    x_normed = signal("x_normed")
    squared = signal("squared")
    piece_used = signal("piece_used")
    dve_step = signal("dve_step")
    act_step = signal("act_step")
    var_ready = signal("var_ready")
    root_ready = signal("root_ready")
    h_temp_ready = signal("h_temp_ready")
    h_hi_ready = signal("h_hi_ready")
    h_ready = signal("h_ready")
    silu_ready = signal("silu_ready")
    hidden_hi = signal("hidden_hi")
    hidden_ready = signal("hidden_ready")
    mod_summed = signal("mod_summed")
    c_ready = signal("c_ready")
    mixed = signal("mixed")
    tanh_ready = signal("tanh_ready")
    decay_ready = signal("decay_ready")
    v_done = signal("v_done")
    kk_scaled = signal("kk_scaled")
    rk_ready = signal("rk_ready")
    rk_used = signal("rk_used")
    va_centred = signal("va_centred")
    va_ready = signal("va_ready")
    ya_temp = signal("ya_temp")
    ya_hi_ready = signal("ya_hi_ready")
    ya_ready = signal("ya_ready")
    scaled = signal("scaled")
    t_ready = [signal(f"t_ready_{b}") for b in range(2)]
    q_copied = [signal(f"q_copied_{b}") for b in range(2)]
    q_final = [signal(f"q_final_{b}") for b in range(2)]
    z_done = [signal(f"z_done_{b}") for b in range(2)]
    z_ready = [signal(f"z_ready_{b}") for b in range(2)]
    p_done = [signal(f"p_done_{b}") for b in range(2)]
    turned = [signal(f"turned_{b}") for b in range(2)]
    rec_pe = signal("recurrence_products")
    rec_dve = signal("recurrence_kept")
    yb_temp = signal("yb_temp")
    yb_hi_ready = signal("yb_hi_ready")
    yb_ready = signal("yb_ready")
    merged_ready = signal("merged_ready")
    merged_hi = signal("merged_hi")
    merged_split = signal("merged_split")
    qk_gained = signal("qk_gained")
    qk_ready = signal("qk_ready")
    lsb_ready = signal("lsb_ready")
    fexp = signal("fexp")
    logits_done = signal("logits_done")
    logits_read = signal("logits_read")
    max_ready = signal("max_ready")
    probs_ready = signal("probs_ready")
    norm_ready = signal("norm_ready")
    pt_done = signal("pt_done")
    pt_ready = signal("pt_ready")
    o_hi_ready = signal("o_hi_ready")
    o_ready = signal("o_ready")
    angle_ready = signal("angle_ready")
    rope_ready = signal("rope_ready")
    stored = signal("stored")
    masks_ready = signal("masks_ready")
    zeroed = signal("zeroed")

    piece_free = []
    used_pieces = [0]

    def add_piece(last_of=None):
        if last_of is None:
            used_pieces[0] += 1
            piece_free.append((piece_used, used_pieces[0]))
        else:
            piece_free.append((lin_filled, PLAN.uses[last_of][0] + 1))
        return len(piece_free) - 1

    half_free = []
    used_halves = [0]

    def add_half(last_of=None):
        if last_of is None:
            used_halves[0] += 1
            half_free.append((halves_used, used_halves[0]))
        else:
            half_free.append((lin_filled, PLAN.uses[last_of][0] + 1))

    def add_units(keys):
        for key in keys:
            add_half()
            add_half(key)

    def add_ffn(i):
        add_units(("gu", i, j) for j in range(FT))
        for w in range(2 * DOWN_UNITS):
            last = (w + 1) * HALF - 1
            add_half(("down", i, last // (2 * FT)) if (last + 1) % (2 * FT) == 0 else None)

    for l in range(2):
        add_ffn(2 * l)
        add_units([("shift", l, s) for s in range(13)] + [("va", l, s) for s in range(4)]
                  + [("u", l, s) for s in range(4)])
        add_units((k, l, n) for n in range(DT) for k in ("gate", "proj"))
        add_units(("out", l, d) for d in range(4))
        add_ffn(2 * l + 1)
    for l in range(2):
        add_ffn(4 + 2 * l)
        for g in range((1, 3)[l]):
            add_units([("qk", l, g, c) for c in range(DT)] + [("v", l, g, s) for s in range(4)])
        if l == 0:
            add_units([("f", 0)])
        add_units(("out", 2 + l, d) for d in range(4))
        add_ffn(5 + 2 * l)
    assert len(half_free) == 2 * PLAN.units

    PIECE = {}

    def norm_pieces(n):
        for i in range(4):
            PIECE["norm", n, i] = add_piece(("norm", n) if i == 3 else None)

    for b in range(2):
        for l in range(2):
            if b == 0:
                norm_pieces(3 * l)
                norm_pieces(3 * l + 1)
                for s in range(4):
                    PIECE["kk", l, s] = add_piece(("kk", l, s))
                for s in range(4):
                    PIECE["vvar", l, s] = add_piece(("vvar", l) if s == 3 else None)
                for s in range(4):
                    PIECE["gvar", l, s] = add_piece(("gvar", l, s))
                norm_pieces(3 * l + 2)
            else:
                norm_pieces(7 + 3 * l)
                norm_pieces(8 + 3 * l)
                for g in range((1, 3)[l]):
                    for c in range(DT):
                        PIECE["ss", l, g, c] = add_piece(("ss", l, g, c))
                norm_pieces(9 + 3 * l)
        if b == 0:
            norm_pieces(6)

    def gu_key(n):
        return "gu", n // FT, n % FT

    def wait_filled(eng, key):
        n = PLAN.uses[key][0]
        eng.wait_ge(lin_filled, n + 1)
        return lin[:, n % 3, :]

    def wait_emptied(eng, key):
        _, engine, count = PLAN.uses[key]
        eng.wait_ge(emptied[engine], count)

    def pairs(bank):
        return bank.rearrange("p (a t) -> p a t", a=2)

    FFN_AT = {}
    for i in range(8):
        FFN_AT[i] = 2 * PLAN.unit["ffn", i]
    MIX_AT = {m: 2 * PLAN.unit["mix", m] for m in range(4)}
    OUT_AT = {m: 2 * PLAN.unit["out", m] for m in range(4)}
    HALVES = 2 * PLAN.units
    X_FROM = {1: ("down", 0), 2: ("out", 0), 3: ("down", 1), 4: ("down", 2), 5: ("out", 1), 6: ("down", 3),
              8: ("down", 4), 9: ("out", 2), 10: ("down", 5), 11: ("down", 6), 12: ("out", 3), 13: ("down", 7)}

    def x_wait(eng, n, i):
        if n == 0:
            eng.wait_ge(x_loaded, 16)
        elif n == 7:
            eng.wait_ge(x_normed, i + 1)
        else:
            wait_emptied(eng, (*X_FROM[n], i))

    with nc.Block() as block:

        @block.sync
        def _(sp):
            sp.dma_start(x[:], src["x"]).then_inc(x_loaded, 16)
            sp.dma_start(const[:], src["const"]).then_inc(consts_loaded, 16)
            sp.dma_start(cols[:], src["cols"]).then_inc(consts_loaded, 16)
            sp.dma_start(mod_b[:], src["mod_b"]).then_inc(consts_loaded, 16)
            sp.dma_start(level_floats[:], src["level_masks"]).then_inc(consts_loaded, 16)

            issued = [0]

            def load(count):
                for n in range(issued[0], issued[0] + count):
                    if n >= RAW_SLOTS:
                        kind, m = PLAN.items[n - RAW_SLOTS]
                        if kind == "unit":
                            sp.wait_ge(lo_ready, 2 * m + 2)
                        else:
                            sp.wait_ge(mod_summed, m + 1)
                    kind, m = PLAN.items[n]
                    sp.dma_start(raw[:, n % RAW_SLOTS, :], src["stream" if kind == "unit" else "mod_w"][m])\
                        .then_inc(raw_loaded[n % RAW_SLOTS], 16)
                issued[0] += count

            def load_to(u):
                load((PLAN.item_of["unit", u] if u < PLAN.units else len(PLAN.items)) - issued[0])

            def small(l):
                sp.wait_ge(masks_ready, 1)
                if l:
                    x_wait(sp, 2, 3)
                sp.dma_start(w2a2[:], src["w2a2"][l]).then_inc(small_loaded, 16)
                sp.dma_start(v2[:], src["v2"][l]).then_inc(small_loaded, 16)
                sp.dma_start(w0_b[:], src["w0"][l].partition_broadcast(P)).then_inc(small_loaded, 16)
                sp.dma_start(bs_b[:], src["bs"][l].partition_broadcast(P)).then_inc(small_loaded, 16)
                sp.dma_start(ws_t[:], src["ws_t"][l]).then_inc(small_loaded, 16)

            for l in range(2):
                load_to(PLAN.unit["mix", l])
                small(l)
            load_to(PLAN.unit["mix", 2])
            x_wait(sp, 5, 3)
            sp.dma_start(amask[:, 0, :], src["fox_mask"]).then_inc(small_loaded, 16)
            sp.dma_start(cum_rhs[:], src["cum_rhs"]).then_inc(small_loaded, 16)
            sp.dma_start(bf_b[:], src["b_f"].partition_broadcast(P)).then_inc(small_loaded, 16)
            load_to(PLAN.unit["mix", 3])
            x_wait(sp, 9, 3)
            sp.dma_start(amask[:], src["dil_mask"]).then_inc(small_loaded, 16)
            sp.dma_start(pos_i[:], src["positions"].partition_broadcast(P)).then_inc(small_loaded, 16)
            sp.dma_start(rope_m[:], src["rope_m"]).then_inc(small_loaded, 16)
            load_to(PLAN.units)
            for i in range(4):
                x_wait(sp, 13, i)
                sp.dma_start(out[:, 2 * i:2 * i + 2, :], x[:, 2 * i:2 * i + 2, :]).then_inc(stored, 16)
            sp.wait_ge(stored, 4 * 16)

        @block.gpsimd
        def _(pool):
            pool.wait_ge(consts_loaded, 64)
            nc.gpsimd.tensor_copy(level_masks[:], level_floats[:]).then_inc(masks_ready, 1)
            for l in range(2):
                pool.wait_ge(small_loaded, 80 * (l + 1))
                nc.gpsimd.affine_select(out=ws_t[:], in_=ws_t[:], compare_op=ALU.is_ge, fill=0.0, base=0,
                                        pattern=[[0, DT], [1, CH]], channel_multiplier=-1).then_inc(zeroed, 1)

        @block.scalar
        def _(act):
            steps = [0]
            next_half = [0]

            def link(ins):
                steps[0] += 1
                ins.then_inc(act_step, 1)
                act.wait_ge(act_step, steps[0])

            def keep_ahead(w, ahead=AHEAD):
                while next_half[0] <= min(w + ahead, HALVES - 1):
                    n = next_half[0]
                    item = PLAN.item_of["unit", n // 2]
                    act.wait_ge(raw_loaded[item % RAW_SLOTS], 16 * (item // RAW_SLOTS + 1))
                    if n >= SPLIT_SLOTS:
                        act.wait_ge(*half_free[n - SPLIT_SLOTS])
                    nc.scalar.activation(split[:, n % SPLIT_SLOTS, 0, :],
                                         raw[:, item % RAW_SLOTS, (n % 2) * HALF * P:(n % 2 + 1) * HALF * P],
                                         ACT.Copy).then_inc(hi_ready, 1)
                    next_half[0] += 1

            def square(key, in_):
                n = PIECE[key]
                if n >= 2:
                    act.wait_ge(*piece_free[n - 2])
                nc.scalar.activation(pieces[:, n % 2, :, :], in_, ACT.Square).then_inc(squared, 1)

            roots = [0]

            def root(out_, in_):
                roots[0] += 1
                act.wait_ge(var_ready, roots[0])
                nc.scalar.activation(out_, in_, ACT.Sqrt).then_inc(root_ready, 1)

            def norm(n):
                for i in range(4):
                    x_wait(act, n, i)
                    square(("norm", n, i), x[:, 2 * i:2 * i + 2, :])
                root(rstd[:], rstd[:])
                if n != 6:
                    split_h(n)

            def split_h(n):
                m = n if n < 6 else n - 1
                for i in range(4):
                    act.wait_ge(h_temp_ready, 4 * m + i + 1)
                    nc.scalar.activation(h[:, 0, 2 * i:2 * i + 2, :], pieces[:, i % 2, :, :], ACT.Copy)\
                        .then_inc(h_hi_ready, 1)

            def ffn(i):
                base = FFN_AT[i]
                norm(ffn_norm(i))
                for j in range(FT):
                    keep_ahead(base + 2 * j + 1)
                    bank = wait_filled(act, ("gu", i, j))
                    n = FT * i + j
                    if n >= 3:
                        wait_emptied(act, gu_key(n - 3))
                    nc.scalar.activation(silu[:, n % 3, :], bank[:, 0:T], ACT.Silu).then_inc(silu_ready, 1)
                    if j:
                        hidden_high(i, j - 1)
                hidden_high(i, FT - 1)
                for d in range(4):
                    keep_ahead(base + 2 * FT + (2 * FT * (d + 1) - 1) // HALF)

            def hidden_high(i, j):
                n = FT * i + j
                wait_emptied(act, ("gu", i, j))
                nc.scalar.activation(hidden[:, 0, j, :], product[:, n % 3, :], ACT.Copy).then_inc(hidden_hi, 1)

            def rwkv(l):
                base = MIX_AT[l]
                norm(3 * l + 1)
                for s in range(13):
                    keep_ahead(base + 2 * s + 1)
                    bank = wait_filled(act, ("shift", l, s))
                    n = 13 * l + s
                    if n >= 2:
                        act.wait_ge(mixed, n - 1)
                    nc.scalar.activation(raw_shift[:, n % 2, :, 1:T + 1], pairs(bank), ACT.Copy)\
                        .then_inc(emptied["act"], 1)
                    if s == 1:
                        act.wait_ge(mixed, 13 * l + 1)
                        nc.scalar.activation(lora[0:64, 0, :], lora[0:64, 0, :], ACT.Tanh).then_inc(tanh_ready, 1)
                keep_ahead(base + 2 * 13 - 1)
                for s in range(4):
                    wait_emptied(act, ("z", l, s))
                    part = decay[:, s // 2, (s % 2) * 512:(s % 2 + 1) * 512]
                    nc.scalar.activation(part, part, ACT.Sigmoid).then_inc(decay_ready, 1)
                for s in range(4):
                    bank = wait_filled(act, ("a", l, s))
                    for i in range(2):
                        ins = nc.scalar.activation(a_[:, 2 * s + i, :], bank[:, i * T:(i + 1) * T], ACT.Sigmoid,
                                                   bias=col("a0", 2 * s + i, l))
                    ins.then_inc(emptied["act"], 1)
                if l:
                    for s in range(4):
                        bank = wait_filled(act, ("vr", l, s))
                        if s >= 2:
                            act.wait_ge(v_done, s - 1)
                        for i in range(2):
                            ins = nc.scalar.activation(pair[:, s % 2, i, :], bank[:, i * T:(i + 1) * T],
                                                       ACT.Sigmoid, bias=col("v0", 2 * s + i, l))
                        ins.then_inc(emptied["act"], 1)
                for s in range(4):
                    keep_ahead(base + 2 * (13 + s) + 1)
                    bank = wait_filled(act, ("va", l, s))
                    nc.scalar.activation(va[:, 2 * s:2 * s + 2, :], pairs(bank), ACT.Gelu_apprx_tanh)\
                        .then_inc(emptied["act"], 1)
                for s in range(4):
                    act.wait_ge(kk_scaled, 4 * l + s + 1)
                    square(("kk", l, s), kk[:, 2 * s:2 * s + 2, :])
                for s in range(4):
                    keep_ahead(base + 2 * (17 + s) + 1, 2 if s == 3 else AHEAD)
                    bank = wait_filled(act, ("u", l, s))
                    nc.scalar.activation(u_[:, 2 * s:2 * s + 2, :], pairs(bank), ACT.Gelu_apprx_tanh)\
                        .then_inc(emptied["act"], 1)
                for s in range(4):
                    root(bonus[:, 2 * s:2 * s + 2, :], bonus[:, 2 * s:2 * s + 2, :])
                wait_emptied(act, ("bonus", l, 3))
                for s in range(4):
                    bank = wait_filled(act, ("vt", l, s))
                    nc.scalar.activation(v_[:, 2 * s:2 * s + 2, :], pairs(bank), ACT.Copy)\
                        .then_inc(emptied["act"], 1)
                for s in range(4):
                    act.wait_ge(va_centred, 4 * l + s + 1)
                    square(("vvar", l, s), va[:, 2 * s:2 * s + 2, :])
                root(rstd[:], rstd[:])
                for s in range(4):
                    bank = wait_filled(act, ("vat", l, s))
                    nc.scalar.activation(va[:, 2 * s:2 * s + 2, :], pairs(bank), ACT.Copy)\
                        .then_inc(emptied["act"], 1)
                for s in range(4):
                    act.wait_ge(ya_temp, 4 * l + s + 1)
                    nc.scalar.activation(ya_hi[:, 2 * s:2 * s + 2, :], u_[:, 2 * s:2 * s + 2, :], ACT.Copy)\
                        .then_inc(ya_hi_ready, 1)
                for c in range(-1, DT):
                    for a, b in zip(SECOND_HALF, FIRST_HALF):
                        if c >= 0:
                            solve(a, l, c)
                        if c < DT - 1:
                            solve(b, l, c + 1)
                for s in range(4):
                    wait_emptied(act, ("gmean", l, s))
                    square(("gvar", l, s), r_[:, 2 * s:2 * s + 2, :])
                for s in range(4):
                    root(kk[:, 2 * s:2 * s + 2, :], kk[:, 2 * s:2 * s + 2, :])
                for s in range(4):
                    act.wait_ge(yb_temp, 4 * l + s + 1)
                    nc.scalar.activation(yb_hi[:, 2 * s:2 * s + 2, :], r_[:, 2 * s:2 * s + 2, :], ACT.Copy)\
                        .then_inc(yb_hi_ready, 1)
                if l == 0:
                    for s in range(4):
                        bank = wait_filled(act, ("vback", l, s))
                        nc.scalar.activation(v_first[:, 2 * s:2 * s + 2, :], pairs(bank), ACT.Copy)\
                            .then_inc(emptied["act"], 1)
                for n in range(DT):
                    m = DT * l + n
                    keep_ahead(base + 2 * (21 + 2 * n) + 1)
                    bank = wait_filled(act, ("gate", l, n))
                    if n >= 2:
                        wait_emptied(act, ("proj", l, n - 2))
                    nc.scalar.activation(gate_sig[:, n % 2, :, :], pairs(bank), ACT.Sigmoid)\
                        .then_inc(emptied["act"], 1)
                    keep_ahead(base + 2 * (22 + 2 * n) + 1)
                for s in range(4):
                    act.wait_ge(merged_ready, DT * l + 2 * s + 2)
                    if s == 0:
                        wait_filled(act, ("proj", l, DT - 1))
                    nc.scalar.activation(h[:, 0, 2 * s:2 * s + 2, :], merged[:, 2 * s:2 * s + 2, :], ACT.Copy)\
                        .then_inc(merged_hi, 1)
                for d in range(4):
                    keep_ahead(OUT_AT[l] + 2 * d + 1)

            def solve(stage, l, c):
                q, b = DT * l + c, c % 2
                n = q // 2
                four = lambda i: sv[:, 2 * b + i, :].rearrange("p (a t) -> p a t", a=4)
                if stage == "cum":
                    bank = wait_filled(act, ("cum", l, c))
                    cum = bank[:, 0:NCH * (CH + 1)].rearrange("p (j t) -> p j t", j=NCH)
                    if q:
                        act.wait_ge(scaled, q)
                    nc.scalar.activation(e_pos[:], cum, ACT.Exp)
                    nc.scalar.activation(e_neg[:], cum, ACT.Exp, scale=-1.0).then_inc(emptied["act"], 1)
                elif stage == "score0":
                    bank = wait_filled(act, ("kbt", l, c))
                    nc.scalar.activation(kbt[:, b, :, :], bank[:, 0:2 * P].rearrange("p (a t) -> p a t", a=2),
                                         ACT.Copy).then_inc(emptied["act"], 1)
                elif stage[0] == "z":
                    act.wait_ge(z_done[b], 6 * n + int(stage[1]) + 1)
                    nc.scalar.activation(z_neg[:, b, :, :], four(0), ACT.Copy, scale=-1.0).then_inc(z_ready[b], 1)
                elif stage[0] == "t":
                    act.wait_ge(turned[b], 5 * n + int(stage[1]) + 1)
                    nc.scalar.activation(q_inv[:, b, :, :], four(0), ACT.Copy).then_inc(q_copied[b], 1)
                elif stage == "y":
                    bank = wait_filled(act, ("y", l, c))
                    nc.scalar.activation(r_[:, c, :], bank[:, 0:T], ACT.Copy).then_inc(emptied["act"], 1)

            def attention(l):
                base = MIX_AT[2 + l]
                ng = (1, 3)[l]
                norm(8 + 3 * l)
                if l:
                    act.wait_ge(angle_ready, 1)
                    nc.scalar.activation(sin[:], ang[:], ACT.Sin)
                    act.wait_ge(angle_ready, 2)
                    nc.scalar.activation(cos[:], cos[:], ACT.Sin).then_inc(rope_ready, 1)
                half = base

                def qk_root(g, c):
                    b = (DT * g + c) % 2
                    root(ssr[:, b, :, :], ssr[:, b, :, :])

                for g in range(ng):
                    for c in range(DT):
                        keep_ahead(half + 1)
                        half += 2
                        bank = wait_filled(act, ("qk", l, g, c))
                        square(("ss", l, g, c), pairs(bank))
                        if c:
                            qk_root(g, c - 1)
                    qk_root(g, DT - 1)
                    for s in range(4):
                        keep_ahead(half + 1)
                        half += 2
                        bank = wait_filled(act, ("v", l, g, s))
                        nc.scalar.activation(vtok[:, g, :, s * 2 * P:(s + 1) * 2 * P], pairs(bank), ACT.Copy)\
                            .then_inc(emptied["act"], 1)
                if l == 0:
                    keep_ahead(half + 1)
                    act.wait_ge(fexp, 1)
                    link(nc.scalar.activation(ls_t[:], ls_t[:], ACT.Exp))
                    nc.scalar.activation(ls_t[:], ls_t[:], ACT.Ln, bias=1.0).then_inc(fexp, 1)

                def exponentials(hd):
                    act.wait_ge(max_ready, HEADS * l + hd + 1)
                    st = stat[:, hd % 2, :]
                    lg0 = logits[hd % 2][:, 0:ng, 0:P]
                    lg1 = logits[hd % 2][:, 0:ng, P:3 * P]
                    nc.scalar.activation(lg0, lg0, ACT.Exp, scale=HD ** -0.5, bias=st[:, 2:3], accum_out=st[:, 4:5])
                    nc.scalar.activation(lg1, lg1, ACT.Exp, scale=HD ** -0.5, bias=st[:, 3:4], accum_out=st[:, 5:6])\
                        .then_inc(probs_ready, 1)

                def high_of(c):
                    bank = wait_filled(act, ("o", l, c))
                    nc.scalar.activation(o_hi[:, c, :], bank[:, 0:T], ACT.Copy).then_inc(o_hi_ready, 1)

                exponentials(0)
                for hd in range(HEADS):
                    if hd + 1 < HEADS:
                        exponentials(hd + 1)
                    for g in range(ng):
                        m = HEADS * g + hd if l == 0 else HEADS + GROUPS * hd + g
                        act.wait_ge(pt_done, m + 1)
                        nc.scalar.activation(pt[hd % 2][:, g, :], sv[:, 3 + m % 2, 0:3 * P], ACT.Copy).then_inc(pt_ready, 1)
                    if hd % 2 and hd > 1:
                        high_of(hd // 2 - 1)
                high_of(DT - 1)
                for d in range(4):
                    keep_ahead(OUT_AT[2 + l] + 2 * d + 1)

            keep_ahead(-1)
            act.wait_ge(consts_loaded, 64)
            nc.scalar.activation(cols[:, COL["c"]:COL["c"] + DT], cols[:, COL["c"]:COL["c"] + DT], ACT.Silu)\
                .then_inc(c_ready, 1)
            for l in range(2):
                ffn(2 * l)
                rwkv(l)
                ffn(2 * l + 1)
            norm(6)
            for l in range(2):
                ffn(4 + 2 * l)
                attention(l)
                ffn(5 + 2 * l)

        @block.vector
        def _(dve):
            steps = [0]
            next_half = [0]
            V = nc.vector

            def link(ins):
                steps[0] += 1
                ins.then_inc(dve_step, 1)
                dve.wait_ge(dve_step, steps[0])

            def keep_ahead(w, ahead=AHEAD):
                while next_half[0] <= min(w + ahead, HALVES - 1):
                    n = next_half[0]
                    item = PLAN.item_of["unit", n // 2]
                    dve.wait_ge(hi_ready, n + 1)
                    V.tensor_tensor(split[:, n % SPLIT_SLOTS, 1, :],
                                    raw[:, item % RAW_SLOTS, (n % 2) * HALF * P:(n % 2 + 1) * HALF * P],
                                    split[:, n % SPLIT_SLOTS, 0, :].bitcast(F32), ALU.subtract).then_inc(lo_ready, 1)
                    next_half[0] += 1

            roots = [0]

            def inverse_root(out_, in_, scale, eps, guard=None):
                if guard is None:
                    link(V.tensor_scalar(out_, in_, scale, eps, ALU.mult, ALU.add))
                else:
                    link(V.tensor_scalar(out_, in_, guard, None, ALU.max))
                V.reciprocal(out_, out_).then_inc(var_ready, 1)
                roots[0] += 1

            def root_wait(n=None):
                dve.wait_ge(root_ready, roots[0] if n is None else n)

            def norm(n):
                bank = wait_filled(dve, ("norm", n))
                V.tensor_scalar(rstd[:], bank[:, 0:T], NORM_EPS, None, ALU.add).then_inc(emptied["dve"], 1)
                wait_emptied(dve, ("norm", n))
                V.reciprocal(rstd[:], rstd[:]).then_inc(var_ready, 1)
                roots[0] += 1
                root_wait()
                if n == 6:
                    for i in range(4):
                        for c in (2 * i, 2 * i + 1):
                            ins = V.scalar_tensor_tensor(x[:, c, :], x[:, c, :], col("final_norm", c), rstd[:],
                                                         ALU.mult, ALU.mult)
                        ins.then_inc(x_normed, 1)
                    return
                m = n if n < 6 else n - 1
                for i in range(4):
                    if i >= 2:
                        dve.wait_ge(h_ready, 4 * m + i - 1)
                    for c in (2 * i, 2 * i + 1):
                        o = pieces[:, i % 2, c % 2, :]
                        if n < 6:
                            l, w = divmod(n, 3)
                            name = ("ffn1_norm", "mix_norm", "ffn2_norm")[w]
                            ins = V.scalar_tensor_tensor(o, x[:, c, :], col(name, c, l), rstd[:], ALU.mult, ALU.mult)
                        else:
                            w = n - 7
                            l, sub = divmod(w, 3)
                            link(V.scalar_tensor_tensor(o, x[:, c, :], gain2[:, w, c:c + 1], rstd[:],
                                                        ALU.mult, ALU.mult))
                            shift = 72 * l + 24 * sub + c
                            ins = V.tensor_scalar(o, o, mod[:, shift:shift + 1], None, ALU.add)
                    ins.then_inc(h_temp_ready, 1)
                    dve.wait_ge(h_hi_ready, 4 * m + i + 1)
                    V.tensor_tensor(h[:, 1, 2 * i:2 * i + 2, :], pieces[:, i % 2, :, :],
                                    h[:, 0, 2 * i:2 * i + 2, :].bitcast(F32), ALU.subtract).then_inc(h_ready, 1)

            def mod_sum(m):
                item = PLAN.item_of["mod", m]
                dve.wait_ge(raw_loaded[item % RAW_SLOTS], 16 * (item // RAW_SLOTS + 1))
                if m >= 2:
                    wait_emptied(dve, ("mod", m - 2))
                acc = mod_acc[:, m % 2, :]
                w = raw[:, item % RAW_SLOTS, :].rearrange("p (k n) -> p k n", k=DT)
                link(V.tensor_scalar(acc, w[:, 0, :], col("c", 0), None, ALU.mult))
                for k in range(1, DT):
                    ins = V.scalar_tensor_tensor(acc, w[:, k, :], col("c", k), acc, ALU.mult, ALU.add)
                    if k < DT - 1:
                        link(ins)
                ins.then_inc(mod_summed, 1)

            def mod_keep(m):
                bank = wait_filled(dve, ("mod", m))
                V.tensor_tensor(mod[:, 2 * m:2 * m + 2], bank[:, 0:2], mod_b[:, 2 * m:2 * m + 2], ALU.add)\
                    .then_inc(emptied["dve"], 1)

            def hidden_rest(i, j):
                n = FT * i + j
                dve.wait_ge(hidden_hi, n + 1)
                V.tensor_tensor(hidden[:, 1, j, :], product[:, n % 3, :], hidden[:, 0, j, :].bitcast(F32),
                                ALU.subtract).then_inc(hidden_ready, 1)

            def ffn(i):
                base = FFN_AT[i]
                norm(ffn_norm(i))
                for j in range(FT):
                    keep_ahead(base + 2 * j + 1)
                    n = FT * i + j
                    bank = wait_filled(dve, ("gu", i, j))
                    dve.wait_ge(silu_ready, n + 1)
                    if n >= 3:
                        dve.wait_ge(hidden_ready, n - 2)
                    V.tensor_tensor(product[:, n % 3, :], silu[:, n % 3, :], bank[:, T:2 * T], ALU.mult)\
                        .then_inc(emptied["dve"], 1)
                    if i < 4 and j in MOD_STEPS:
                        mod_sum(MOD_AT["ffn", i, j])
                    if i < 4 and j - 1 in MOD_STEPS:
                        mod_keep(MOD_AT["ffn", i, j - 1])
                    if j:
                        hidden_rest(i, j - 1)
                hidden_rest(i, FT - 1)
                for d in range(4):
                    keep_ahead(base + 2 * FT + (2 * FT * (d + 1) - 1) // HALF)
                    residual(("down", i, d), 2 * d, 0.5 if i < 4 else None, (i - 4) // 2 * 3 + (i - 4) % 2 * 2)

            def residual(key, c, factor, which):
                bank = pairs(wait_filled(dve, key))
                if factor is not None:
                    V.scalar_tensor_tensor(x[:, c:c + 2, :], bank, factor, x[:, c:c + 2, :], ALU.mult, ALU.add)\
                        .then_inc(emptied["dve"], 1)
                else:
                    V.scalar_tensor_tensor(x[:, c, :], bank[:, 0, :], gate2[:, which, c:c + 1], x[:, c, :],
                                           ALU.mult, ALU.add)
                    V.scalar_tensor_tensor(x[:, c + 1, :], bank[:, 1, :], gate2[:, which, c + 1:c + 2],
                                           x[:, c + 1, :], ALU.mult, ALU.add).then_inc(emptied["dve"], 1)

            def rwkv(l):
                base = MIX_AT[l]
                norm(3 * l + 1)
                link(V.memset(raw_shift[:, :, :, 0:1], 0.0))
                for s in range(13):
                    keep_ahead(base + 2 * s + 1)
                    n = 13 * l + s
                    wait_emptied(dve, ("shift", l, s))
                    if n:
                        dve.wait_ge(mixed, n)
                    b = raw_shift[:, n % 2, :, :]
                    link(V.tensor_tensor(diff[:], b[:, :, 0:T], b[:, :, 1:T + 1], ALU.subtract))
                    if s == 0:
                        dst = [(lora[:, 0, :], 24), (lora[:, 1, :], 25)]
                    elif s < 9:
                        dst = [(r_[:, s - 1, :], s - 1), (k_[:, s - 1, :], 8 + s - 1)]
                    else:
                        c = 2 * (s - 9)
                        dst = [(v_[:, c, :], 16 + c), (v_[:, c + 1, :], 17 + c)]
                    for i, (o, m) in enumerate(dst):
                        ins = V.scalar_tensor_tensor(o, diff[:, i, :], col("mu", m, l), b[:, i, 1:T + 1],
                                                     ALU.mult, ALU.add)
                    ins.then_inc(mixed, 1)
                dve.wait_ge(mixed, 13 * l + 13)
                dve.wait_ge(small_loaded, 80 * (l + 1))
                for s in range(4):
                    bank = wait_filled(dve, ("z", l, s))
                    V.tensor_tensor(decay[:, s // 2, (s % 2) * 512:(s % 2 + 1) * 512], bank,
                                    w0_b[:, (s % 2) * 512:(s % 2 + 1) * 512], ALU.add).then_inc(emptied["dve"], 1)
                if l:
                    for s in range(4):
                        wait_emptied(dve, ("vr", l, s))
                        vs = v_[:, 2 * s:2 * s + 2, :]
                        link(V.tensor_tensor(diff[:], v_first[:, 2 * s:2 * s + 2, :], vs, ALU.subtract))
                        link(V.tensor_tensor(diff[:], diff[:], pair[:, s % 2, :, :], ALU.mult))
                        V.tensor_tensor(vs, vs, diff[:], ALU.add).then_inc(v_done, 1)
                        dve.wait_ge(v_done, s + 1)
                for s in range(4):
                    keep_ahead(base + 2 * (13 + s) + 1)
                    for c in (2 * s, 2 * s + 1):
                        ins = V.tensor_scalar(kk[:, c, :], k_[:, c, :], col("k_k", c, l), None, ALU.mult)
                    ins.then_inc(kk_scaled, 1)
                for s in range(4):
                    bank = wait_filled(dve, ("kk", l, s))
                    o = bonus[:, 2 * s:2 * s + 2, :]
                    V.tensor_scalar(o, pairs(bank), 1e-24, None, ALU.max).then_inc(emptied["dve"], 1)
                    wait_emptied(dve, ("kk", l, s))
                    V.reciprocal(o, o).then_inc(var_ready, 1)
                    roots[0] += 1
                wait_emptied(dve, ("a", l, 3))
                a0 = COL["k_a", l]
                link(V.tensor_scalar(one_less_ka[:, l, :], cols[:, a0:a0 + DT], -1.0, 1.0, ALU.mult, ALU.add))
                for s in range(4):
                    keep_ahead(base + 2 * (17 + s) + 1, 2 if s == 3 else AHEAD)
                    for c in (2 * s, 2 * s + 1):
                        link(V.tensor_scalar(diff[:, c % 2, :], a_[:, c, :], col("k_a", c, l),
                                             one_less_ka[:, l, c:c + 1], ALU.mult, ALU.add))
                        link(V.tensor_tensor(k_[:, c, :], k_[:, c, :], diff[:, c % 2, :], ALU.mult))
                for s in range(4):
                    root_wait(roots[0] - 3 + s)
                    w = slice(2 * s, 2 * s + 2)
                    link(V.tensor_tensor(kk[:, w, :], kk[:, w, :], bonus[:, w, :], ALU.mult))
                    link(V.tensor_tensor(a_[:, w, :], kk[:, w, :], a_[:, w, :], ALU.mult))
                for s in range(4):
                    n = 4 * l + s
                    if s >= 2:
                        wait_filled(dve, ("bonus", l, s - 2))
                    for c in (2 * s, 2 * s + 1):
                        ins = V.scalar_tensor_tensor(pair[:, s % 2, c % 2, :], r_[:, c, :], col("r_k", c, l),
                                                     k_[:, c, :], ALU.mult, ALU.mult)
                    ins.then_inc(rk_ready, 1)
                    if s:
                        bonus_of(l, s - 1)
                bonus_of(l, 3)
                bank = wait_filled(dve, ("vmean", l))
                V.tensor_copy(rstd[:], bank[:, 0:T]).then_inc(emptied["dve"], 1)
                wait_emptied(dve, ("vmean", l))
                for s in range(4):
                    w = slice(2 * s, 2 * s + 2)
                    V.tensor_tensor(va[:, w, :], va[:, w, :], wide(rstd[:], 2), ALU.subtract).then_inc(va_centred, 1)
                bank = wait_filled(dve, ("vvar", l))
                V.tensor_scalar(rstd[:], bank[:, 0:T], LN_EPS, None, ALU.add).then_inc(emptied["dve"], 1)
                wait_emptied(dve, ("vvar", l))
                V.reciprocal(rstd[:], rstd[:]).then_inc(var_ready, 1)
                roots[0] += 1
                root_wait()
                for s in range(4):
                    w = slice(2 * s, 2 * s + 2)
                    link(V.tensor_tensor(va[:, w, :], va[:, w, :], wide(rstd[:], 2), ALU.mult))
                    for c in (2 * s, 2 * s + 1):
                        ins = V.tensor_scalar(va[:, c, :], va[:, c, :], col("ln_g", c, l), col("ln_b", c, l),
                                              ALU.mult, ALU.add)
                    ins.then_inc(va_ready, 1)
                for s in range(4):
                    bank = wait_filled(dve, ("sgu", l, s))
                    w = slice(2 * s, 2 * s + 2)
                    bs = bs_b[:, 2 * s * CH:(2 * s + 2) * CH].rearrange("p (g t) -> p g t", g=2)
                    bank4 = bank.rearrange("p (g j t) -> p g j t", g=2, j=NCH)
                    d4 = diff[:].rearrange("p g (j t) -> p g j t", j=NCH)
                    for j in range(NCH):
                        ins = V.tensor_tensor(d4[:, :, j, :], bank4[:, :, j, :], bs, ALU.add)
                    ins.then_inc(emptied["dve"], 1)
                    wait_emptied(dve, ("sgu", l, s))
                    V.tensor_tensor(u_[:, w, :], u_[:, w, :], diff[:], ALU.mult).then_inc(ya_temp, 1)
                    dve.wait_ge(ya_hi_ready, 4 * l + s + 1)
                    V.tensor_tensor(ya_lo[:, w, :], u_[:, w, :], ya_hi[:, w, :].bitcast(F32), ALU.subtract)\
                        .then_inc(ya_ready, 1)
                for b in (beta, kappa):
                    V.memset(b[0:64, 1, :, :], 0.0)
                    V.memset(b[64:128, 0, :, :], 0.0)
                link(V.memset(s0[:], 0.0))
                if l == 0:
                    dve.wait_ge(masks_ready, 1)
                for c in range(-1, DT):
                    for a, b in zip(SECOND_HALF, FIRST_HALF):
                        if c >= 0:
                            solve(a, l, c)
                            if a in MOD_STAGES:
                                mod_keep(MOD_AT["solve", l, c, MOD_STAGES.index(a)])
                            if a in ("z3", "z5"):
                                mod_sum(MOD_AT["solve", l, c, ("z3", "z5").index(a)])
                        if c < DT - 1:
                            solve(b, l, c + 1)
                for s in range(4):
                    w = slice(2 * s, 2 * s + 2)
                    wait_emptied(dve, ("y", l, 2 * s + 1))
                    bank = wait_filled(dve, ("gmean", l, s))
                    V.scalar_tensor_tensor(r_[:, w, :], pairs(bank), -1.0 / HD, r_[:, w, :], ALU.mult, ALU.add)\
                        .then_inc(emptied["dve"], 1)
                for s in range(4):
                    bank = wait_filled(dve, ("gvar", l, s))
                    o = kk[:, 2 * s:2 * s + 2, :]
                    V.tensor_scalar(o, pairs(bank), 1.0 / HD, GN_EPS, ALU.mult, ALU.add).then_inc(emptied["dve"], 1)
                    wait_emptied(dve, ("gvar", l, s))
                    V.reciprocal(o, o).then_inc(var_ready, 1)
                    roots[0] += 1
                for s in range(4):
                    w = slice(2 * s, 2 * s + 2)
                    root_wait(roots[0] - 3 + s)
                    link(V.tensor_tensor(r_[:, w, :], r_[:, w, :], kk[:, w, :], ALU.mult))
                    for c in (2 * s, 2 * s + 1):
                        link(V.tensor_scalar(r_[:, c, :], r_[:, c, :], col("gn_g", c, l), col("gn_b", c, l),
                                             ALU.mult, ALU.add))
                    V.tensor_tensor(r_[:, w, :], r_[:, w, :], bonus[:, w, :], ALU.add).then_inc(yb_temp, 1)
                    dve.wait_ge(yb_hi_ready, 4 * l + s + 1)
                    V.tensor_tensor(yb_lo[:, w, :], r_[:, w, :], yb_hi[:, w, :].bitcast(F32), ALU.subtract)\
                        .then_inc(yb_ready, 1)
                for n in range(DT):
                    keep_ahead(base + 2 * (21 + 2 * n) + 1)
                    keep_ahead(base + 2 * (22 + 2 * n) + 1)
                    bank = wait_filled(dve, ("proj", l, n))
                    wait_emptied(dve, ("gate", l, n))
                    V.tensor_tensor(diff[:], pairs(bank), gate_sig[:, n % 2, :, :], ALU.mult)\
                        .then_inc(emptied["dve"], 1)
                    wait_emptied(dve, ("proj", l, n))
                    V.tensor_tensor(merged[:, n, :], diff[:, 0, :], diff[:, 1, :], ALU.add).then_inc(merged_ready, 1)
                    dve.wait_ge(merged_ready, DT * l + n + 1)
                for s in range(4):
                    w = slice(2 * s, 2 * s + 2)
                    dve.wait_ge(merged_hi, 4 * l + s + 1)
                    V.tensor_tensor(h[:, 1, w, :], merged[:, w, :], h[:, 0, w, :].bitcast(F32), ALU.subtract)\
                        .then_inc(merged_split, 1)
                for d in range(4):
                    keep_ahead(OUT_AT[l] + 2 * d + 1)
                    residual(("out", l, d), 2 * d, 1.0, None)

            def bonus_of(l, s):
                bank = wait_filled(dve, ("bonus", l, s))
                w = slice(2 * s, 2 * s + 2)
                V.tensor_tensor(bonus[:, w, :], pairs(bank), v_[:, w, :], ALU.mult).then_inc(emptied["dve"], 1)

            def solve(stage, l, c):
                q, b = DT * l + c, c % 2
                n = q // 2
                four = lambda i: sv[:, 2 * b + i, :].rearrange("p (a t) -> p a t", a=4)
                b4 = sv[:, 4, :]
                if stage == "cum":
                    wait_emptied(dve, ("cum", l, c))
                    if c >= 2:
                        wait_filled(dve, ("y", l, c - 2))
                    in_chunks = lambda t: t[:, c, :].rearrange("p (j t) -> p j t", j=NCH)
                    neg_incl = e_neg[:, :, 1:CH + 1]
                    V.tensor_tensor(ar[:, b, :, 0:CH], in_chunks(kk), e_pos[:, :, 0:CH], ALU.mult)
                    V.tensor_tensor(ar[:, b, :, CH:2 * CH], in_chunks(r_), e_pos[:, :, 1:CH + 1], ALU.mult)
                    for o, t in ((kappa, k_), (beta, a_)):
                        for hh in range(2):
                            w = slice(64 * hh, 64 * hh + 64)
                            V.tensor_tensor(o[w, hh, :, :], in_chunks(t)[w], neg_incl[w], ALU.mult)
                    for i, t in enumerate((k_, a_)):
                        V.tensor_tensor(kb0[:, i, :], t[:, c, 0:CH], e_neg[:, 0, 1:CH + 1], ALU.mult)
                    V.tensor_tensor(state_scale[:, b:b + 1], e_pos[:, 0, CH:CH + 1], e_neg[:, 1, 0:1], ALU.mult)\
                        .then_inc(scaled, 1)
                elif stage[:5] == "score":
                    i = int(stage[5])
                    bank = wait_filled(dve, ("score", l, c, i))
                    V.tensor_tensor(gbk[b][:, i, :].rearrange("p (a t) -> p a t", a=2),
                                    bank.rearrange("p (a t) -> p a t", a=2), wide(mask, 2), ALU.mult)\
                        .then_inc(emptied["dve"], 1)
                elif stage == "low":
                    bank = wait_filled(dve, ("low", l, c))
                    V.tensor_tensor(t_inv[:, b, :, :], bank.rearrange("p (a t) -> p a t", a=4),
                                    wide(c_("neg2"), 4), ALU.mult).then_inc(emptied["dve"], 1)
                    wait_emptied(dve, ("low", l, c))
                    link(V.tensor_tensor(q_inv[:, b, :, :], gbk[b][:, :, 0:CH], wide(c_("neg2t"), 4), ALU.mult))
                    V.tensor_tensor(q_inv[:, b, :, :], q_inv[:, b, :, :], wide(ident, 4), ALU.add)
                    V.tensor_tensor(t_inv[:, b, :, :], t_inv[:, b, :, :], wide(ident, 4), ALU.add)\
                        .then_inc(t_ready[b], 1)
                elif stage[0] == "p":
                    s = int(stage[1])
                    dve.wait_ge(p_done[b], 6 * n + s + 1)
                    if s < 5:
                        V.copy_predicated(t_inv[:, b, :, :], wide(level_masks[:, 0, s, :], 4), four(1))\
                            .then_inc(t_ready[b], 1)
                    else:
                        V.copy_predicated(q_inv[:, b, :, :], wide(level_masks[:, 1, s, :], 4), four(1))\
                            .then_inc(q_final[b], 1)
                elif stage == "rhs0":
                    dve.wait_ge(rec_pe, 5 * q + 1)
                    V.tensor_copy(rh[:], b4[:, 0:P]).then_inc(rec_dve, 1)
                elif stage == "u0":
                    dve.wait_ge(rec_pe, 5 * q + 2)
                    V.tensor_scalar(nu[:], b4[:, P:2 * P], -1.0, None, ALU.mult).then_inc(rec_dve, 1)
                elif stage == "st":
                    dve.wait_ge(rec_pe, 5 * q + 3)
                    for hh in range(2):
                        w = slice(64 * hh, 64 * hh + 64)
                        ins = V.tensor_scalar(s0[w, w], b4[w, 2 * P + 64 * hh:2 * P + 64 * hh + 64],
                                              state_scale[w, b:b + 1], None, ALU.mult)
                    ins.then_inc(rec_dve, 1)
                elif stage == "rhs1":
                    dve.wait_ge(rec_pe, 5 * q + 4)
                    V.tensor_copy(rh[:], b4[:, 3 * P:4 * P]).then_inc(rec_dve, 1)
                elif stage == "u1":
                    dve.wait_ge(rec_pe, 5 * q + 5)
                    V.tensor_scalar(nu[:], b4[:, 0:P], -1.0, None, ALU.mult).then_inc(rec_dve, 1)

            def attention(l):
                base = MIX_AT[2 + l]
                ng = (1, 3)[l]
                norm(8 + 3 * l)
                dve.wait_ge(small_loaded, 160 + 48 * (l + 1))
                if l:
                    two_pi = 2 * np.pi
                    c1 = 6.28125
                    c2 = float(np.float32(two_pi - c1))
                    c3 = float(two_pi - c1 - np.float64(np.float32(two_pi - c1)))
                    link(V.tensor_copy(ang[:], pos_i[:]))
                    link(V.tensor_scalar(ang[:], ang[:], col("inv_freq"), None, ALU.mult))
                    link(V.tensor_scalar(cos[:], ang[:], 1.0 / two_pi, 12582912.0, ALU.mult, ALU.add))
                    link(V.tensor_scalar(cos[:], cos[:], -12582912.0, None, ALU.add))
                    for part in (c1, c2, c3):
                        link(V.scalar_tensor_tensor(ang[:], cos[:], -part, ang[:], ALU.mult, ALU.add))
                    V.tensor_scalar(ang[:], ang[:], 3.1415925, -3.1415925, ALU.min, ALU.max).then_inc(angle_ready, 1)
                    dve.wait_ge(angle_ready, 1)
                    link(V.tensor_scalar(cos[:], ang[:], -1.0, None, ALU.mult))
                    link(V.tensor_tensor(cos[:], cos[:], ang[:], ALU.max))
                    V.tensor_scalar(cos[:], cos[:], -1.0, float(np.pi / 2), ALU.mult, ALU.add).then_inc(angle_ready, 1)
                    dve.wait_ge(rope_ready, 1)
                half = base

                def finish_qk(g, c):
                    n = DT * g + c
                    b = n % 2
                    bank = wait_filled(dve, ("ss", l, g, c))
                    V.tensor_scalar(ssr[:, b, :, :], pairs(bank), 1.0 / HD, NORM_EPS, ALU.mult, ALU.add)\
                        .then_inc(emptied["dve"], 1)
                    wait_emptied(dve, ("ss", l, g, c))
                    V.reciprocal(ssr[:, b, :, :], ssr[:, b, :, :]).then_inc(var_ready, 1)
                    roots[0] += 1
                    if l:
                        bank = wait_filled(dve, ("rot", l, g, c))
                        V.tensor_tensor(rot[:], pairs(bank), wide(sin[:], 2), ALU.mult).then_inc(emptied["dve"], 1)
                        link(V.tensor_tensor(qkg[:, b, :, :], qkg[:, b, :, :], wide(cos[:], 2), ALU.mult))
                        wait_emptied(dve, ("rot", l, g, c))
                        link(V.tensor_tensor(qkg[:, b, :, :], qkg[:, b, :, :], rot[:], ALU.add))
                    root_wait()
                    V.tensor_tensor(qk[:, g, 2 * c:2 * c + 2, :], qkg[:, b, :, :], ssr[:, b, :, :], ALU.mult)\
                        .then_inc(qk_ready, 1)
                    dve.wait_ge(qk_ready, DT * (g + l) + c + 1)

                for g in range(ng):
                    for c in range(DT):
                        keep_ahead(half + 1)
                        half += 2
                        b = (DT * g + c) % 2
                        bank = wait_filled(dve, ("qk", l, g, c))
                        dve.wait_ge(squared, PIECE["ss", l, g, c] + 1)
                        for i in range(2):
                            gc = COL["fox_g"] + i if l == 0 else COL["dil_g"] + 2 * g + i
                            ins = V.tensor_scalar(qkg[:, b, i, :], bank[:, i * T:(i + 1) * T], cols[:, gc:gc + 1],
                                                  None, ALU.mult)
                        ins.then_inc(emptied["dve"], 1)
                        wait_emptied(dve, ("qk", l, g, c))
                        if c:
                            finish_qk(g, c - 1)
                    finish_qk(g, DT - 1)
                    for s in range(4):
                        keep_ahead(half + 1)
                        half += 2
                if l == 0:
                    keep_ahead(half + 1)
                    bank = wait_filled(dve, ("f", 0))[:, 0:NCH * HEADS].rearrange("p (j n) -> p j n", j=NCH)
                    V.tensor_tensor(ls[:], bank, wide(bf_b[:], NCH), ALU.add).then_inc(emptied["dve"], 1)
                    wait_emptied(dve, ("f", 0))
                    link(V.tensor_scalar(ls_t[:], ls[:], -1.0, None, ALU.mult))
                    V.tensor_tensor(ls_t[:], ls_t[:], ls[:], ALU.min).then_inc(fexp, 1)
                    link(V.tensor_scalar(ls[:], ls[:], 0.0, None, ALU.min))
                    dve.wait_ge(fexp, 2)
                    link(V.tensor_tensor(ls[:], ls[:], ls_t[:], ALU.subtract))

                def gates_of(hd):
                    V.tensor_copy(ls_b[:], ls[:, :, hd:hd + 1].to_broadcast([P, NCH, P])).then_inc(lsb_ready, 1)

                def largest(hd):
                    n = HEADS * l + hd
                    dve.wait_ge(logits_done, n + 1)
                    if l == 0 and hd + 1 < HEADS:
                        gates_of(hd + 1)
                    if hd >= 2:
                        dve.wait_ge(pt_done, n - 1 if l == 0 else HEADS + GROUPS * (hd - 1))
                    lg = logits[hd % 2]
                    st = stat[:, hd % 2, :]
                    V.tensor_tensor(lg[:, 0:ng, :], sv[:, 0:ng, 0:3 * P], amask[:, 0:ng, :], ALU.add)\
                        .then_inc(logits_read, 1)
                    dve.wait_ge(logits_read, n + 1)
                    V.tensor_reduce(st[:, 0:1], lg[:, 0:ng, 0:P], AX.XY, ALU.max, negate=True)
                    link(V.tensor_reduce(st[:, 1:2], lg[:, 0:ng, P:3 * P], AX.XY, ALU.max, negate=True))
                    V.tensor_scalar(st[:, 2:4], st[:, 0:2], HD ** -0.5, None, ALU.mult).then_inc(max_ready, 1)

                def rest_of(c):
                    bank = wait_filled(dve, ("o", l, c))
                    dve.wait_ge(o_hi_ready, DT * l + c + 1)
                    V.tensor_tensor(o_lo[:, c, :], bank[:, 0:T], o_hi[:, c, :].bitcast(F32), ALU.subtract)\
                        .then_inc(emptied["dve"], 1)

                if l == 0:
                    gates_of(0)
                largest(0)
                for hd in range(HEADS):
                    if hd + 1 < HEADS:
                        largest(hd + 1)
                    dve.wait_ge(probs_ready, HEADS * l + hd + 1)
                    lg = logits[hd % 2]
                    st = stat[:, hd % 2, :]
                    link(V.reciprocal(st[:, 6:8], st[:, 4:6]))
                    V.tensor_scalar(lg[:, 0:ng, 0:P], lg[:, 0:ng, 0:P], st[:, 6:7], None, ALU.mult)
                    V.tensor_scalar(lg[:, 0:ng, P:3 * P], lg[:, 0:ng, P:3 * P], st[:, 7:8], None, ALU.mult)\
                        .then_inc(norm_ready, 1)
                    if hd % 2 and hd > 1:
                        rest_of(hd // 2 - 1)
                rest_of(DT - 1)
                for d in range(4):
                    keep_ahead(OUT_AT[2 + l] + 2 * d + 1)
                    residual(("out", 2 + l, d), 2 * d, None, 3 * l + 1)

            keep_ahead(-1)
            dve.wait_ge(consts_loaded, 64)
            dve.wait_ge(c_ready, 1)
            for l in range(2):
                ffn(2 * l)
                rwkv(l)
                ffn(2 * l + 1)
            for l in range(2):
                for sub in range(3):
                    w = 3 * l + sub
                    a = 72 * l + 24 * sub
                    g = COL["norm_g"] + 8 * w
                    link(V.tensor_scalar(gain2[:, w, :], mod[:, a + 8:a + 16], 1.0, None, ALU.add))
                    link(V.tensor_tensor(gain2[:, w, :], gain2[:, w, :], cols[:, g:g + 8], ALU.mult))
                    link(V.tensor_scalar(gate2[:, w, :], mod[:, a + 16:a + 24], 1.0 if sub == 1 else 0.5, None,
                                         ALU.mult))
            norm(6)
            for l in range(2):
                ffn(4 + 2 * l)
                attention(l)
                ffn(5 + 2 * l)

        @block.tensor
        def _(pe):
            M = nc.tensor.matmul

            def bank_for(key):
                n = PLAN.uses[key][0]
                if n >= 3:
                    wait_emptied(pe, PLAN.order[n - 3])
                return lin[:, n % 3, :]

            def half_ready(w):
                pe.wait_ge(lo_ready, w + 1)
                return split[:, w % SPLIT_SLOTS, :, :]

            def three(o, w_hi, w_lo, a_hi, a_lo, start, stop, skip=False):
                M(o, w_hi, a_hi, start=start, stop=False, skip_group_check=skip)
                M(o, w_hi, a_lo, start=False, stop=False, skip_group_check=skip)
                return M(o, w_lo, a_hi, start=False, stop=stop, skip_group_check=skip)

            def two_tiles(w, key, acts, ready=None):
                bank = bank_for(key)
                for i in range(2):
                    s = half_ready(w + i)
                    hi, lo = acts[i]
                    for k in range(DT):
                        if ready is not None and i == 0 and k % 2 == 0:
                            ready(k // 2)
                        t = slice(k * P, (k + 1) * P)
                        ins = three(bank[:, i * T:(i + 1) * T], s[:, 0, t], s[:, 1, t], hi[:, k, :], lo[:, k, :],
                                    k == 0, k == DT - 1)
                    if i == 0:
                        ins.then_inc(halves_used, 1)
                ins.then_inc(lin_filled, 1)

            HH = (h[:, 0, :, :], h[:, 1, :, :])

            def tokens_major(w, key, width):
                bank = bank_for(key)
                for i in range(2):
                    s = half_ready(w + i)
                    for j in range(NCH):
                        o = bank[:, j * width:(j + 1) * width]
                        for k in range(4):
                            m = slice(k * 2 * P, k * 2 * P + width)
                            kk_ = 4 * i + k
                            a_hi = h[:, 0, kk_, j * CH:(j + 1) * CH]
                            a_lo = h[:, 1, kk_, j * CH:(j + 1) * CH]
                            M(o, a_hi, s[:, 0, m], start=(kk_ == 0 and j == 0), stop=False, skip_group_check=True)
                            M(o, a_lo, s[:, 0, m], start=False, stop=False, skip_group_check=True)
                            ins = M(o, a_hi, s[:, 1, m], start=False, stop=(kk_ == DT - 1 and j == NCH - 1),
                                    skip_group_check=True)
                    if i == 0:
                        ins.then_inc(halves_used, 1)
                ins.then_inc(lin_filled, 1)

            def norm(n):
                bank = bank_for(("norm", n))
                sums(bank, [("norm", n, i) for i in range(4)])

            def sums(bank, keys):
                for i, key in enumerate(keys):
                    p = PIECE[key]
                    pe.wait_ge(squared, p + 1)
                    for t in range(2):
                        ins = M(bank[:, 0:T], mean_w, pieces[:, p % 2, t, :], start=(i == 0 and t == 0),
                                stop=(i == 3 and t == 1))
                    ins.then_inc(piece_used if i < 3 else lin_filled, 1)

            def h_wait(n):
                m = n if n < 6 else n - 1
                return lambda i: pe.wait_ge(h_ready, 4 * m + i + 1)

            def mod_columns(m):
                bank = bank_for(("mod", m))
                pe.wait_ge(mod_summed, m + 1)
                for i in range(2):
                    ins = M(bank[:, i:i + 1], mod_acc[:, m % 2, i * P:(i + 1) * P], c_("one"), start=True, stop=True)
                ins.then_inc(lin_filled, 1)

            def ffn(i):
                base = FFN_AT[i]
                norm(ffn_norm(i))
                for j in range(FT):
                    two_tiles(base + 2 * j, ("gu", i, j), (HH, HH), h_wait(ffn_norm(i)) if j == 0 else None)
                    if i < 4 and j - 1 in MOD_STEPS:
                        mod_columns(MOD_AT["ffn", i, j - 1])
                base += 2 * FT
                pe.wait_ge(hidden_ready, FT * (i + 1) - 2)
                for d in range(4):
                    bank = bank_for(("down", i, d))
                    for e in range(2):
                        for k in range(FT):
                            flat = (2 * d + e) * FT + k
                            w = base + flat // HALF
                            if flat % HALF == 0:
                                half_ready(w)
                            if d == 0 and e == 0 and k >= FT - 2:
                                pe.wait_ge(hidden_ready, FT * i + k + 1)
                            s = split[:, w % SPLIT_SLOTS, :, :]
                            t = slice(flat % HALF * P, (flat % HALF + 1) * P)
                            ins = three(bank[:, e * T:(e + 1) * T], s[:, 0, t], s[:, 1, t], hidden[:, 0, k, :],
                                        hidden[:, 1, k, :], k == 0, k == FT - 1)
                            last = e == 1 and k == FT - 1
                            if last:
                                ins.then_inc(lin_filled, 1)
                            elif flat % HALF == HALF - 1:
                                ins.then_inc(halves_used, 1)

            def transposes(key, t):
                bank = bank_for(key)
                s = key[-1]
                for i in range(4):
                    ins = nc.tensor.transpose(bank[:, i * P:(i + 1) * P],
                                              t[:, 2 * s + i // 2, (i % 2) * CH:(i % 2 + 1) * CH], ident)
                ins.then_inc(lin_filled, 1)

            def rwkv(l):
                base = MIX_AT[l]
                norm(3 * l + 1)
                for s in range(13):
                    two_tiles(base + 2 * s, ("shift", l, s), (HH, HH), h_wait(3 * l + 1) if s == 0 else None)
                pe.wait_ge(small_loaded, 80 * (l + 1))
                pe.wait_ge(tanh_ready, l + 1)
                for s in range(4):
                    bank = bank_for(("z", l, s))
                    j = s // 2
                    M(bank, lora[0:64, 0, j * CH:(j + 1) * CH], w2a2[0:64, (s % 2) * 512:(s % 2 + 1) * 512],
                      start=True, stop=True).then_inc(lin_filled, 1)
                for s in range(4):
                    bank = bank_for(("a", l, s))
                    for i in range(2):
                        c = 2 * s + i
                        ins = M(bank[:, i * T:(i + 1) * T], w2a2[64:128, c * P:(c + 1) * P], lora[64:128, 0, :],
                                start=True, stop=True)
                    ins.then_inc(lin_filled, 1)
                if l:
                    for s in range(4):
                        bank = bank_for(("vr", l, s))
                        for i in range(2):
                            c = 2 * s + i
                            ins = M(bank[:, i * T:(i + 1) * T], v2[0:32, c * P:(c + 1) * P], lora[0:32, 1, :],
                                    start=True, stop=True)
                        ins.then_inc(lin_filled, 1)
                for s in range(4):
                    two_tiles(base + 2 * (13 + s), ("va", l, s), (HH, HH))
                for s in range(4):
                    bank = bank_for(("kk", l, s))
                    p = PIECE["kk", l, s]
                    pe.wait_ge(squared, p + 1)
                    M(bank, head_w, pieces[:, p % 2, :, :], start=True, stop=True).then_inc(lin_filled, 1)
                for s in range(4):
                    two_tiles(base + 2 * (17 + s), ("u", l, s), (HH, HH))
                for s in range(4):
                    bank = bank_for(("bonus", l, s))
                    pe.wait_ge(rk_ready, 4 * l + s + 1)
                    M(bank, head_w, pair[:, s % 2, :, :], start=True, stop=True).then_inc(lin_filled, 1)
                for s in range(4):
                    transposes(("vt", l, s), v_)
                bank = bank_for(("vmean", l))
                wait_emptied(pe, ("va", l, 3))
                for k in range(DT):
                    ins = M(bank[:, 0:T], mean_w, va[:, k, :], start=(k == 0), stop=(k == DT - 1))
                ins.then_inc(lin_filled, 1)
                sums(bank_for(("vvar", l)), [("vvar", l, s) for s in range(4)])
                for s in range(4):
                    pe.wait_ge(va_ready, 4 * l + s + 1)
                    transposes(("vat", l, s), va)
                pe.wait_ge(zeroed, l + 1)
                for s in range(4):
                    bank = bank_for(("sgu", l, s))
                    wait_emptied(pe, ("vat", l, s))
                    for i in range(4):
                        g, j = 2 * s + i // 2, i % 2
                        ins = M(bank[:, i * P:(i + 1) * P], va[:, g, j * CH:(j + 1) * CH], ws_t[:, g, :],
                                start=True, stop=True)
                    ins.then_inc(lin_filled, 1)
                pe.wait_ge(decay_ready, 4 * l + 4)
                for c in range(-1, DT):
                    for a, b in zip(SECOND_HALF, FIRST_HALF):
                        if c >= 0:
                            solve(a, l, c)
                            if a in MOD_STAGES:
                                mod_columns(MOD_AT["solve", l, c, MOD_STAGES.index(a)])
                        if c < DT - 1:
                            solve(b, l, c + 1)
                for s in range(4):
                    bank = bank_for(("gmean", l, s))
                    wait_emptied(pe, ("y", l, 2 * s + 1))
                    M(bank, head_w, r_[:, 2 * s:2 * s + 2, :], start=True, stop=True).then_inc(lin_filled, 1)
                for s in range(4):
                    bank = bank_for(("gvar", l, s))
                    p = PIECE["gvar", l, s]
                    pe.wait_ge(squared, p + 1)
                    M(bank, head_w, pieces[:, p % 2, :, :], start=True, stop=True).then_inc(lin_filled, 1)
                if l == 0:
                    for s in range(4):
                        if s == 0:
                            pe.wait_ge(yb_temp, 4)
                        transposes(("vback", l, s), v_)
                YA, YB = (ya_hi, ya_lo), (yb_hi, yb_lo)
                for n in range(DT):
                    two_tiles(base + 2 * (21 + 2 * n), ("gate", l, n), (HH, HH))
                    if n == 0:
                        pe.wait_ge(ya_ready, 4 * l + 4)
                        pe.wait_ge(yb_ready, 4 * l + 4)
                    two_tiles(base + 2 * (22 + 2 * n), ("proj", l, n), (YA, YB))
                for d in range(4):
                    two_tiles(OUT_AT[l] + 2 * d, ("out", l, d), (HH, HH),
                              (lambda i: pe.wait_ge(merged_split, 4 * l + i + 1)) if d == 0 else None)

            def solve(stage, l, c):
                q, b = DT * l + c, c % 2
                n = q // 2
                zb, pb, b4 = sv[:, 2 * b, :], sv[:, 2 * b + 1, :], sv[:, 4, :]
                part = lambda i: slice(i * CH, (i + 1) * CH)
                lt, rbt, akt, rkt = (lambda i, a=a: gbk[b][:, i, part(a)] for a in range(4))
                v_tok = lambda j, hh: v_[:, c, j * CH + 64 * hh:j * CH + 64 * hh + 64]
                if stage == "cum":
                    bank = bank_for(("cum", l, c))
                    for j in range(NCH):
                        ins = M(bank[:, j * (CH + 1):(j + 1) * (CH + 1)], decay[:, j, c * P:(c + 1) * P], tri,
                                start=True, stop=True)
                    ins.then_inc(lin_filled, 1)
                elif stage[:5] == "score":
                    i = int(stage[5])
                    hh, j = i // 2, i % 2
                    if i == 0:
                        pe.wait_ge(scaled, q + 1)
                        bank = bank_for(("kbt", l, c))
                        for a in range(2):
                            ins = nc.tensor.transpose(bank[:, part(a)], kb0[:, a, :], ident)
                        ins.then_inc(lin_filled, 1)
                    bank = bank_for(("score", l, c, i))
                    M(bank[:, 0:2 * CH], beta[:, hh, j, :], ar[:, b, j, :], start=True, stop=True)
                    M(bank[:, 2 * CH:4 * CH], kappa[:, hh, j, :], ar[:, b, j, :], start=True, stop=True)\
                        .then_inc(lin_filled, 1)
                elif stage == "low":
                    bank = bank_for(("low", l, c))
                    for i in range(4):
                        ins = M(bank[:, part(i)], ar[:, b, i % 2, 0:CH], beta[:, i // 2, i % 2, :],
                                start=True, stop=True)
                    ins.then_inc(lin_filled, 1)
                elif stage[0] == "z":
                    s = int(stage[1])
                    pe.wait_ge(t_ready[b], 6 * n + s + 1)
                    if s:
                        pe.wait_ge(q_copied[b], 5 * n + s)
                    for i in range(4):
                        ins = M(zb[:, part(i)], lt(i), t_inv[:, b, i, :], start=True, stop=True)
                    ins.then_inc(z_done[b], 1)
                elif stage[0] == "p":
                    s = int(stage[1])
                    pe.wait_ge(z_ready[b], 6 * n + s + 1)
                    for i in range(4):
                        if s < 5:
                            ins = M(pb[:, part(i)], q_inv[:, b, i, :], z_neg[:, b, i, :], start=True, stop=True)
                        else:
                            ins = M(pb[:, part(i)], z_neg[:, b, i, :], q_inv[:, b, i, :], start=True, stop=True)
                    ins.then_inc(p_done[b], 1)
                elif stage[0] == "t":
                    s = int(stage[1])
                    pe.wait_ge(t_ready[b], 6 * n + s + 2)
                    for i in range(4):
                        ins = nc.tensor.transpose(zb[:, part(i)], t_inv[:, b, i, :], ident)
                    ins.then_inc(turned[b], 1)
                elif stage == "rhs0":
                    pe.wait_ge(q_final[b], n + 1)
                    for hh in range(2):
                        ins = M(b4[:, 64 * hh:64 * hh + 64], akt(2 * hh), v_tok(0, hh), start=True, stop=True)
                    ins.then_inc(rec_pe, 1)
                elif stage == "u0":
                    pe.wait_ge(rec_dve, 5 * q + 1)
                    for hh in range(2):
                        ins = M(b4[:, P + 64 * hh:P + 64 * hh + 64], q_inv[:, b, 2 * hh, :],
                                rh[:, 64 * hh:64 * hh + 64], start=True, stop=True)
                    ins.then_inc(rec_pe, 1)
                elif stage == "st":
                    pe.wait_ge(rec_dve, 5 * q + 2)
                    M(b4[:, 2 * P:3 * P], kbt[:, b, 0, :], v_[:, c, 0:P], start=True, stop=False)
                    M(b4[:, 2 * P:3 * P], kbt[:, b, 1, :], nu[:], start=False, stop=True).then_inc(rec_pe, 1)
                    y = bank_for(("y", l, c))
                    for hh in range(2):
                        w = slice(64 * hh, 64 * hh + 64)
                        M(y[w, 0:CH], v_tok(0, hh), rkt(2 * hh), start=True, stop=False)
                        M(y[w, 0:CH], nu[:, w], rbt(2 * hh), start=False, stop=True)
                elif stage == "rhs1":
                    pe.wait_ge(rec_dve, 5 * q + 3)
                    for hh in range(2):
                        M(b4[:, 3 * P + 64 * hh:3 * P + 64 * hh + 64], akt(2 * hh + 1), v_tok(1, hh),
                          start=(hh == 0), stop=False, skip_group_check=True)
                    M(b4[:, 3 * P:4 * P], ar[:, b, 1, 0:CH], s0[:], start=False, stop=True, skip_group_check=True)\
                        .then_inc(rec_pe, 1)
                elif stage == "u1":
                    pe.wait_ge(rec_dve, 5 * q + 4)
                    for hh in range(2):
                        ins = M(b4[:, 64 * hh:64 * hh + 64], q_inv[:, b, 2 * hh + 1, :], rh[:, 64 * hh:64 * hh + 64],
                                start=True, stop=True)
                    ins.then_inc(rec_pe, 1)
                elif stage == "y":
                    y = lin[:, PLAN.uses["y", l, c][0] % 3, :]
                    M(y[:, CH:2 * CH], s0[:], ar[:, b, 1, CH:2 * CH], start=True, stop=False, skip_group_check=True)
                    pe.wait_ge(rec_dve, 5 * q + 5)
                    for hh in range(2):
                        w = slice(64 * hh, 64 * hh + 64)
                        M(y[w, CH:2 * CH], v_tok(1, hh), rkt(2 * hh + 1), start=False, stop=False,
                          skip_group_check=True)
                        ins = M(y[w, CH:2 * CH], nu[:, w], rbt(2 * hh + 1), start=False, stop=(hh == 1),
                                skip_group_check=True)
                    ins.then_inc(lin_filled, 1)

            def attention(l):
                base = MIX_AT[2 + l]
                ng = (1, 3)[l]
                norm(8 + 3 * l)
                half = base

                def finish_qk(g, c):
                    bank = bank_for(("ss", l, g, c))
                    p = PIECE["ss", l, g, c]
                    pe.wait_ge(squared, p + 1)
                    M(bank, head_w, pieces[:, p % 2, :, :], start=True, stop=True).then_inc(lin_filled, 1)
                    if l:
                        bank = bank_for(("rot", l, g, c))
                        pe.wait_ge(small_loaded, 160 + 96)
                        wait_emptied(pe, ("qk", l, g, c))
                        M(bank, rope_m[:], qkg[:, (DT * g + c) % 2, :, :], start=True, stop=True).then_inc(lin_filled, 1)

                for g in range(ng):
                    for c in range(DT):
                        two_tiles(half, ("qk", l, g, c), (HH, HH), h_wait(8 + 3 * l) if g == 0 and c == 0 else None)
                        half += 2
                        if c:
                            finish_qk(g, c - 1)
                    finish_qk(g, DT - 1)
                    for s in range(4):
                        tokens_major(half, ("v", l, g, s), 2 * P)
                        half += 2
                if l == 0:
                    tokens_major(half, ("f", 0), HEADS)
                    pe.wait_ge(small_loaded, 160 + 48)
                pe.wait_ge(qk_ready, DT if l == 0 else 4 * DT)
                wait_emptied(pe, ("v", l, ng - 1, 3))

                def logits_of(hd):
                    c, w = hd // 2, slice(64 * (hd % 2), 64 * (hd % 2) + 64)
                    if hd:
                        pe.wait_ge(logits_read, HEADS * l + hd)
                    if l == 0:
                        pe.wait_ge(lsb_ready, hd + 1)
                    for g in range(ng):
                        b = sv[:, g, :]
                        q_, kx = qk[:, g, 2 * c, :], qk[:, g, 2 * c + 1, :]
                        more = l == 0
                        ins = M(b[:, 0:P], q_[w, 0:P], kx[w, 0:P], start=True, stop=not more)
                        if more:
                            M(b[:, 0:P], ls_b[:, 0, :], cum_rhs[:, 0:P], start=False, stop=True)
                        ins = M(b[:, P:3 * P], q_[w, P:2 * P], kx[w, :], start=True, stop=not more,
                                skip_group_check=True)
                        if more:
                            M(b[:, P:3 * P], ls_b[:, 0, :], cum_rhs[:], start=False, stop=False, skip_group_check=True)
                            ins = M(b[:, 2 * P:3 * P], ls_b[:, 1, :], cum_rhs[:, 0:P], start=False, stop=True,
                                    skip_group_check=True)
                    ins.then_inc(logits_done, 1)

                def turn(hd):
                    pe.wait_ge(norm_ready, HEADS * l + hd + 1)
                    for g in range(ng):
                        m = hd if l == 0 else HEADS + GROUPS * hd + g
                        b = sv[:, 3 + m % 2, :]
                        if m >= 2:
                            pe.wait_ge(pt_ready, m - 1)
                        for i in range(3):
                            ins = nc.tensor.transpose(b[:, i * P:(i + 1) * P], logits[hd % 2][:, g, i * P:(i + 1) * P],
                                                      ident)
                        ins.then_inc(pt_done, 1)

                def values_of(hd):
                    c, hh = hd // 2, hd % 2
                    w = slice(64 * hh, 64 * hh + 64)
                    o = lin[:, PLAN.uses["o", l, c][0] % 3, :] if hh else bank_for(("o", l, c))
                    pe.wait_ge(pt_ready, hd + 1 if l == 0 else HEADS + GROUPS * (hd + 1))
                    vt = lambda g, j: vtok[:, g, j, hd * HD:(hd + 1) * HD]
                    probs = pt[hd % 2]
                    for g in range(ng):
                        M(o[w, 0:P], vt(g, 0), probs[:, g, 0:P], start=(g == 0), stop=(g == ng - 1))
                    for g in range(ng):
                        M(o[w, P:2 * P], vt(g, 0), probs[:, g, P:2 * P], start=(g == 0), stop=False)
                        ins = M(o[w, P:2 * P], vt(g, 1), probs[:, g, 2 * P:3 * P], start=False, stop=(g == ng - 1))
                    if hh:
                        ins.then_inc(lin_filled, 1)

                logits_of(0)
                logits_of(1)
                for hd in range(HEADS):
                    if hd + 2 < HEADS:
                        logits_of(hd + 2)
                    turn(hd)
                    if hd:
                        values_of(hd - 1)
                values_of(HEADS - 1)
                wait_emptied(pe, ("o", l, DT - 1))
                OO = (o_hi, o_lo)
                for d in range(4):
                    two_tiles(OUT_AT[2 + l] + 2 * d, ("out", 2 + l, d), (OO, OO))

            pe.wait_ge(consts_loaded, 64)
            for l in range(2):
                ffn(2 * l)
                rwkv(l)
                ffn(2 * l + 1)
            norm(6)
            for l in range(2):
                ffn(4 + 2 * l)
                attention(l)
                ffn(5 + 2 * l)


def constants():
    i = np.arange(P)
    const = np.zeros((P, NCONST), np.float32)

    def put(name, value):
        a, n = CONST[name]
        const[:, a:a + n] = value

    put("ident", np.eye(P))
    put("mean", 1.0 / D)
    put("head", i[:, None] // HD == i[None, :] // HD)
    mid = CH // 2 - 1
    put("tri", -DECAY_SCALE * ((i[:, None] <= np.arange(CH + 1)[None, :] - 1).astype(np.float64)
                               - (i[:, None] <= mid)))
    put("mask", np.concatenate([i[:, None] < i[None, :], i[:, None] <= i[None, :]], 1))
    below = (i[:, None] % 2 == 1) & (i[None, :] == i[:, None] - 1)
    put("neg2", -1.0 * below)
    put("neg2t", -1.0 * below.T)
    put("one", 1.0)
    levels = np.zeros((P, 2, len(LEVELS), P), np.float32)
    for s, m in enumerate(LEVELS):
        b = (i[:, None] // m % 2 == 1) & (i[None, :] // m == i[:, None] // m - 1)
        levels[:, 0, s], levels[:, 1, s] = b, b.T
    rope = np.zeros((P, P), np.float32)
    for base in (0, HD):
        for f in range(8):
            rope[base + f + 8, base + f] = -1.0
            rope[base + f, base + f + 8] = 1.0
    cum = np.concatenate([i[:, None] <= i[None, :], np.ones((P, P), bool)], 1) * np.float32(-(HD ** 0.5))

    def allowed(window, dilation):
        t, s = np.arange(T)[:, None], np.arange(T)[None, :]
        ok = (s <= t) & ((t - s) % dilation == 0) & (t - s <= window)
        m = np.where(ok, 0.0, NEG).astype(np.float32)
        return np.concatenate([m[:P, :P], m[P:, :]], 1)

    fox = allowed(T, 1)
    dil = np.stack([allowed(w, d) for w, d in ((128, 1), (512, 4), (2048, 16))], 1)
    freq = np.float32(500000.0) ** (-(np.arange(8, dtype=np.float32) * np.float32(2.0) / np.float32(16)))
    inv = np.zeros((P, 1), np.float32)
    for base in (0, 8, HD, HD + 8):
        inv[base:base + 8, 0] = freq
    return {"const": const, "level_masks": levels, "rope_m": rope, "cum_rhs": cum.astype(np.float32),
            "fox_mask": fox, "dil_mask": np.ascontiguousarray(dil), "inv_freq": inv}


def kernel(**inputs):
    import concourse.bacc as bacc
    from concourse.bass_utils import run_bass_kernel_spmd

    a = {k: np.asarray(v) for k, v in inputs.items()}
    fixed = constants()

    def tiles(w):
        w = np.concatenate([w, np.zeros((D, -w.shape[1] % P), w.dtype)], 1)
        return w.reshape(DT, P, -1, P).transpose(2, 1, 0, 3)

    def units(pairs_):
        return [np.stack(p, 1).reshape(P, TPU * P) for p in pairs_]

    def down(w):
        w = w.reshape(FT, P, DT, P).transpose(1, 2, 0, 3).reshape(P, DOWN_UNITS, TPU * P)
        return list(w.transpose(1, 0, 2))

    def moving(w):
        w = np.concatenate([w, np.zeros((D, 2 * P - w.shape[1]), w.dtype)], 1)
        return w.reshape(DT, P, 2 * P).transpose(1, 0, 2).reshape(P, TPU * P)

    stream = []

    def ffn(gate, up, w_down):
        stream.extend(units(zip(tiles(gate), tiles(up))))
        stream.extend(down(w_down))

    for l in range(2):
        gu = a["ffn1_w_gu"][l]
        ffn(gu[:, :FF], gu[:, FF:], a["ffn1_w_down"][l])
        w = a["w_in_first"] if l == 0 else a["w_in_rest"][0]
        w = tiles(np.concatenate([w, np.zeros((D, 58 * P - w.shape[1]), w.dtype)], 1))
        pa, pb = tiles(a["w_proj_a"][l]), tiles(a["w_proj_b"][l])
        order = [(56, 57)] + [(32 + c, 40 + c) for c in range(8)] + [(48 + c, 49 + c) for c in range(0, 8, 2)]
        order += [(24 + c, 25 + c) for c in range(0, 8, 2)] + [(16 + c, 17 + c) for c in range(0, 8, 2)]
        stream.extend(units((w[m], w[n]) for m, n in order))
        for n in range(DT):
            stream.extend(units([(w[n], w[8 + n]), (pa[n], pb[n])]))
        wo = tiles(a["w_out"][l])
        stream.extend(units((wo[n], wo[n + 1]) for n in range(0, 8, 2)))
        gu = a["ffn2_w_gu"][l]
        ffn(gu[:, :FF], gu[:, FF:], a["ffn2_w_down"][l])
    for l in range(2):
        ffn(a["ffn_w_gate_2"][l, 0], a["ffn_w_up_2"][l, 0], a["ffn_w_down_2"][l, 0])
        w_in, w_o = (a["fox_w_in_2"][0], a["fox_w_out_2"][0]) if l == 0 else (a["dil_w_in_2"][0], a["dil_w_out_2"][0])
        for g in range((1, 3)[l]):
            w = w_in[:, 3 * D * g:3 * D * (g + 1)]
            t = tiles(w[:, :2 * D])
            stream.extend(units((t[c], t[8 + c]) for c in range(DT)))
            stream.extend(moving(w[:, 2 * D + 256 * s:2 * D + 256 * (s + 1)]) for s in range(4))
        if l == 0:
            stream.append(moving(w_in[:, 3 * D:]))
        wo = tiles(w_o)
        stream.extend(units((wo[n], wo[n + 1]) for n in range(0, 8, 2)))
        ffn(a["ffn_w_gate_2"][l, 1], a["ffn_w_up_2"][l, 1], a["ffn_w_down_2"][l, 1])

    column = lambda v: v.reshape(-1, P).T
    cols = np.zeros((P, NCOLS), np.float32)

    def put(key, v):
        n = v.shape[-1] // P
        cols[:, COL[key]:COL[key] + n] = column(v)

    for l in range(2):
        for name, key in (("ffn1_norm",) * 2, ("mix_norm",) * 2, ("ffn2_norm",) * 2, ("ln_g", "sgu_ln_g"),
                          ("ln_b", "sgu_ln_b"), ("a0", "rwkv_a0"), ("k_k", "rwkv_k_k"), ("k_a", "rwkv_k_a"),
                          ("gn_g", "rwkv_gn_g"), ("gn_b", "rwkv_gn_b")):
            put((name, l), a[key][l])
        put(("r_k", l), a["rwkv_r_k"][l].reshape(-1))
        mu = a["mu_first"] if l == 0 else a["mu_rest"][0]
        put(("mu", l), np.concatenate([mu, np.zeros(26 * P - mu.shape[0], mu.dtype)]))
    put(("v0", 1), a["rwkv_v0"][0])
    put("final_norm", a["final_norm"])
    put("norm_g", a["norm_g_2"].reshape(-1))
    put("c", a["c_2"][0])
    twice = lambda v: np.concatenate([v, v])
    put("fox_g", np.concatenate([twice(a["fox_q_g_2"][0]), twice(a["fox_k_g_2"][0])]))
    put("dil_g", np.concatenate([twice(a[n][0][g]) for g in range(3) for n in ("dil_q_g_2", "dil_k_g_2")]))
    cols[:, COL["inv_freq"]:COL["inv_freq"] + 1] = fixed.pop("inv_freq")

    v2 = a["rwkv_v2"][0]
    arrays = {
        "x": a["x"][0].T.reshape(DT, P, T).transpose(1, 0, 2),
        "stream": np.stack(stream),
        "mod_w": a["mod_w_2"].reshape(2, DT, P, 36, 2 * P).transpose(0, 3, 2, 1, 4).reshape(72, P, TPU * P),
        "mod_b": column(a["mod_b_2"].reshape(-1)),
        "cols": cols,
        "w2a2": np.concatenate([a["rwkv_w2"], a["rwkv_a2"]], 1),
        "v2": np.stack([v2, v2]),
        "w0": a["rwkv_w0"],
        "bs": a["sgu_b_s"].reshape(2, -1),
        "ws_t": a["sgu_w_s"].transpose(0, 3, 1, 2),
        "b_f": a["fox_b_f_2"][0],
        "positions": a["positions_2"][0],
        **fixed,
    }
    arrays = {k: np.ascontiguousarray(v) for k, v in arrays.items()}
    nc = bacc.Bacc("TRN2", target_bir_lowering=False, num_devices=1)
    src = {k: nc.dram_tensor(f"in_{k}", v.shape, mybir.dt.from_np(v.dtype), kind="ExternalInput").ap()
           for k, v in arrays.items()}
    out = nc.dram_tensor("out", (P, DT, T), F32, kind="ExternalOutput").ap()
    build_program(nc, src, out)
    r = run_bass_kernel_spmd(nc, [{f"in_{k}": v for k, v in arrays.items()}], core_ids=[0])
    y = r.results[0]["out"]
    return np.ascontiguousarray(y.transpose(1, 0, 2).reshape(D, T).T)[None]
```

```python
import numpy as np
import concourse.bass as bass
from concourse import mybir

F32 = mybir.dt.float32
F32R = mybir.dt.float32r
I32 = mybir.dt.int32
I8 = mybir.dt.int8
ALU = mybir.AluOpType
ACT = mybir.ActivationFunctionType
AX = mybir.AxisListType

P = 128
T = 256
D = 1024
DT = D // P
FF = 2816
FT = FF // P
HEADS = 16
HD = 64
CH = 128
NCH = T // CH
TPU = 16
HALF = TPU // 2
DOWN_UNITS = FT * DT // TPU
FFN_UNITS = FT + DOWN_UNITS
NORM_EPS = 1e-6
LN_EPS = 1e-5
GN_EPS = 64e-5
DECAY_SCALE = float(np.exp(-0.5))
NEG = -1e30
GROUPS = 3
LEVELS = (2, 4, 8, 16, 32, 64)
MOD_UNITS = 72
RAW_SLOTS = 3
SPLIT_SLOTS = 4
AHEAD = 3

COL = {}
_at = 0
for _l in range(2):
    for _name, _n in (("ffn1_norm", 8), ("mix_norm", 8), ("ffn2_norm", 8), ("ln_g", 8), ("ln_b", 8),
                      ("mu", 26), ("a0", 8), ("v0", 8), ("k_k", 8), ("k_a", 8), ("r_k", 8),
                      ("gn_g", 8), ("gn_b", 8)):
        COL[_name, _l] = _at
        _at += _n
for _name, _n in (("final_norm", 8), ("norm_g", 48), ("c", 8), ("fox_g", 2), ("dil_g", 6), ("inv_freq", 1)):
    COL[_name] = _at
    _at += _n
NCOLS = _at

CONST = {}
_at = 0
for _name, _n in (("ident", P), ("mean", P), ("head", P), ("tri", 129), ("mask", 2 * P), ("neg2", P), ("neg2t", P), ("one", 1), ("norm_eps", 1), ("ln_eps", 1)):
    CONST[_name] = (_at, _n)
    _at += _n
NCONST = _at


FIRST_HALF = ("score0", "score1", "score2", "score3", "low", "z0", "p0", "t0", "z1", "p1", "t1", "z2", "p2", "t2")
SECOND_HALF = ("z3", "p3", "t3", "z4", "p4", "t4", "z5", "p5", "rhs0", "u0", "st", "rhs1", "u1", "y")
CUM_STEP = 11
MOD_FFN = 6
MOD_SPREAD = ((0, 4), (4, 8), (8, 8))
MOD_STAGES = ("u0", "u1")
MOD_SUMS = [(0, i, i + 1) for i in range(8)] + [(1, 2 * i, 2 * i + 2) for i in range(4)]
MOD_AT = {}
GATE_STEPS = range(5, 10)
GATE_TAKEN = 10
SPLIT_STEPS = (6, 7)
GROUP_STEPS = {0: "mean", 1: "square", 3: "var", 5: "invert0", 6: "invert1", 7: "root", 8: "scale", 9: "affine",
               10: "bonus", 11: "high", 12: "rest"}
SOLVE = [(c, i, SECOND_HALF[i] if c >= 0 else None, FIRST_HALF[i] if c < DT - 1 else None)
         for c in range(-1, DT) for i in range(len(FIRST_HALF))]


def group_norm_at(c, i):
    return (GROUP_STEPS[i], c // 2 - 1) if c >= 2 and c % 2 == 0 and i in GROUP_STEPS else (None, None)


def mod_done(j):
    return (j - 4) // 3 if j >= 4 and (j - 4) % 3 == 0 and (j - 4) // 3 < MOD_FFN else None


def down_halves(d):
    ends = [(2 * FT * e - 1) // HALF + 1 if e else 0 for e in (d, d + 1)]
    return range(*ends)


class Plan:

    def __init__(self):
        self.uses = {}
        self.filled = {}
        self.emptied = {"act": 0, "dve": 0}
        self.order = []
        self.unit = {}
        self.units = 0
        self.items = []
        self.item_of = {}
        self.mods = 0

    def use(self, key, engine, at_once=True):
        self.uses[key] = (len(self.order), engine)
        self.order.append(key)
        if at_once:
            self.fill(key)
            self.empty(key)

    def empty(self, key):
        engine = self.uses[key][1]
        self.emptied[engine] += 1
        self.uses[key] += (self.emptied[engine],)

    def fill(self, key):
        self.filled[key] = len(self.filled) + 1

    def stream(self, key, count=1):
        self.unit[key] = self.units
        self.units += count

    def load_units(self, count=1):
        for _ in range(count):
            n = sum(kind == "unit" for kind, _ in self.items)
            self.item_of["unit", n] = len(self.items)
            self.items.append(("unit", n))

    def load_mod(self):
        self.item_of["mod", self.mods] = len(self.items)
        self.items.append(("mod", self.mods))
        self.mods += 1


def make_plan():
    p = Plan()

    def ffn(i):
        p.stream(("ffn", i), FFN_UNITS)
        for j in range(FT):
            p.use(("gu", i, j), "dve")
            if i < 4 and mod_done(j) is not None:
                MOD_AT["ffn", i, mod_done(j)] = len(MOD_AT)
                p.use(("mod", MOD_AT["ffn", i, mod_done(j)]), "dve")
        for d in range(DT // 2):
            p.use(("down", i, d), "dve")
            if i < 4:
                MOD_AT["ffn", i, MOD_FFN + d] = len(MOD_AT)
                p.use(("mod", MOD_AT["ffn", i, MOD_FFN + d]), "dve")

    for l in range(2):
        ffn(2 * l)
        p.stream(("mix", l), 37)
        for s in range(13):
            p.use(("shift", l, s), "act")
        for s in range(4):
            p.use(("z", l, s), "dve")
        for s in range(4):
            p.use(("a", l, s), "act")
        if l:
            for s in range(4):
                p.use(("vr", l, s), "act")
        for s in range(4):
            p.use(("va", l, s), "act")
        for s in range(4):
            p.use(("kk", l, s), "dve")
        p.use(("vmean", l), "dve")
        for s in range(4):
            p.use(("u", l, s), "act")
        for s in range(4):
            p.use(("vat", l, s), "act")
        for s in range(4):
            p.use(("sgu", l, s), "dve")
        for s in range(4):
            p.use(("bonus", l, s), "dve")
        for s in range(4):
            p.use(("vt", l, s), "act")
        p.use(("cum", l, 0), "act")
        for c, i, a, b in SOLVE:
            if i == 0 and c >= 0:
                for n in range(2):
                    MOD_AT["solve", l, c, n] = len(MOD_AT)
            if b and i == GATE_TAKEN:
                p.empty(("gate", l, c + 1))
            if a in MOD_STAGES:
                p.use(("mod", MOD_AT["solve", l, c, MOD_STAGES.index(a)]), "dve")
            if a == "st":
                p.use(("y", l, c), "act", at_once=False)
            if a == "y":
                p.fill(("y", l, c))
                p.empty(("y", l, c))
            if b == "score0":
                p.use(("kbt", l, c + 1), "act")
            if b and b[:5] == "score":
                p.use(("score", l, c + 1, int(b[5])), "dve")
            elif b == "low":
                p.use(("low", l, c + 1), "dve")
            stage, s = group_norm_at(c, i)
            if stage in ("mean", "var"):
                p.use(("g" + stage, l, s), "dve")
            if b and i == GATE_STEPS[0]:
                p.use(("gate", l, c + 1), "act", at_once=False)
            if b and i == GATE_STEPS[-1]:
                p.fill(("gate", l, c + 1))
            if i == CUM_STEP and c + 2 < DT:
                p.use(("cum", l, c + 2), "act")
        p.use(("gmean", l, 3), "dve")
        p.use(("pa", l, 0), "dve")
        p.use(("gvar", l, 3), "dve")
        p.use(("pa", l, 1), "dve")
        p.use(("pa", l, 2), "dve")
        if l == 0:
            for s in range(4):
                p.use(("vback", l, s), "act")
        p.use(("pa", l, 3), "dve")
        for s in range(4):
            p.use(("pb", l, s), "dve")
        p.stream(("out", l), 4)
        for d in range(4):
            p.use(("out", l, d), "dve")
        ffn(2 * l + 1)
    for l in range(2):
        ffn(4 + 2 * l)
        p.stream(("mix", 2 + l), (13, 36)[l])
        for g in range((1, 3)[l]):
            for c in range(DT):
                p.use(("qk", l, g, c), "act")
                if c:
                    p.use(("ss", l, g, c - 1), "act")
                    if l:
                        p.use(("rot", l, g, c - 1), "dve")
                if c % 2:
                    p.use(("v", l, g, c // 2), "act")
            p.use(("ss", l, g, DT - 1), "act")
            if l:
                p.use(("rot", l, g, DT - 1), "dve")
        if l == 0:
            p.use(("f", 0), "dve")
        for c in range(DT):
            p.use(("o", l, c), "dve")
        p.stream(("out", 2 + l), 4)
        for d in range(4):
            p.use(("out", 2 + l, d), "dve")
        ffn(5 + 2 * l)
    for l in range(2):
        for i in (2 * l, 2 * l + 1):
            done = 0
            at = [3 * m + 4 for m in range(MOD_FFN)]
            at += [FT + (down_halves(d)[0] + AHEAD) // 2 + 1 for d in range(DT // 2)]
            for n in at:
                p.load_units(n - done)
                done = n
                p.load_mod()
            p.load_units(FFN_UNITS - done)
            if i == 2 * l:
                p.load_units(22)
                for c in range(-1, DT):
                    if c >= 0:
                        p.load_mod()
                    if c < DT - 1:
                        p.load_units()
                    if c >= 0:
                        p.load_mod()
                p.load_units(37 - 30 + 4)
    p.load_units(p.units - sum(kind == "unit" for kind, _ in p.items))
    assert p.mods == MOD_UNITS == len(MOD_AT)
    return p


def ffn_norm(i):
    return (0, 2, 3, 5, 7, 9, 10, 12)[i]


PLAN = make_plan()


def build_program(nc, src, out):
    sem = {}

    def signal(name):
        sem[name] = nc.alloc_semaphore(name)
        return sem[name]

    at = [nc.sbuf_base + (-nc.sbuf_base) % 64]

    def place(name, shape, dt=F32, where=None):
        size = int(np.prod(shape[1:])) * (1 if dt == I8 else 4)
        size += -size % 32
        if where is None:
            where = at[0]
            at[0] += size
        return nc.alloc_sbuf_tensor_at(name, list(shape), dt, offset=where)

    raw = place("raw_units", [P, RAW_SLOTS, TPU * P])
    split = place("split_halves", [P, SPLIT_SLOTS, 2, HALF * P], F32R)
    x = place("x", [P, DT, T])
    h = place("h_split", [P, 2, DT, T], F32R)
    pieces_at = at[0]
    pieces = place("squares", [P, 2, 2, T])
    v_first = place("v_first", [P, DT, T])
    const = place("constants", [P, NCONST])
    level_masks = place("level_masks", [P, 2, len(LEVELS), P], I8)
    cols = place("columns", [P, NCOLS])
    mod = place("modulation", [P, 144])
    mod_b = place("modulation_bias", [P, 144])
    gain2 = place("modulated_gain", [P, 6, DT])
    gate2 = place("residual_gate", [P, 6, DT])
    one_less_ka = place("one_less_ka", [P, 2, DT])
    rstd = place("rstd", [P, T])
    state_scale = nc.alloc_sbuf_tensor_at("state_scale", [P, 2], F32, offset=pieces_at + 2112)
    arena = at[0] + (-at[0]) % 32
    KB = 1024

    def over(name, shape, kb, dt=F32):
        return place(name, shape, dt, where=arena + int(kb * KB))

    hidden = over("hidden_split", [P, 2, FT, T], 0, F32R)
    mod_acc = over("modulation_sums", [P, 2, 2 * P], 104.5)
    silu = over("silu", [P, 3, T], 62)
    product = over("gated", [P, 3, T], 65)
    r_ = over("r", [P, DT, T], 0)
    k_ = over("k", [P, DT, T], 8)
    v_ = over("v", [P, DT, T], 16)
    decay = over("decay", [P, NCH, D], 24)
    a_ = over("a", [P, DT, T], 32)
    kk = over("kk", [P, DT, T], 40)
    va = over("va", [P, DT, T], 48)
    u_ = over("u", [P, DT, T], 56)
    bonus = v_first
    lora = over("lora", [P, 2, T], 72)
    ws_t = over("spatial_t", [P, DT, CH], 74)
    B = 78
    raw_shift = over("raw_shift", [P, 2, 2, T + 1], B)
    diff = over("diff", [P, 2, T], B + 4.25)
    w2a2 = over("w2a2", [P, D], B + 6.25)
    v2 = over("v2", [32, D], B + 10.25)
    w0_b = over("w0_rows", [P, D], B + 14.25)
    bs_b = over("bs_rows", [P, D], B + 18.25)
    pair = over("pair", [P, 2, 2, T], B + 22.25)
    e_pos = nc.alloc_sbuf_tensor_at("exp_pos", [P, NCH, CH + 1], F32, offset=pieces_at)
    e_neg = nc.alloc_sbuf_tensor_at("exp_neg", [P, NCH, CH + 1], F32, offset=pieces_at + 1056)
    gbk = (over("scores_0", [P, 4, 4 * CH], 64), over("scores_1", [P, 4, 4 * CH], 72))
    t_inv = over("inverse", [P, 2, 4, CH], 80)
    q_inv = over("inverse_t", [P, 2, 4, CH], 84)
    z_neg = over("z_neg", [P, 2, 4, CH], 88)
    ar = over("alpha_rho", [P, 2, NCH, 2 * CH], 92)
    beta = over("beta", [P, 2, NCH, CH], 96)
    kappa = over("kappa", [P, 2, NCH, CH], 98)
    kbt = over("kappa_beta_tok", [P, 2, 2, P], 100)
    kb0 = over("kappa_beta_0", [P, 2, CH], 102)
    rh = over("rhs", [P, P], 103)
    nu = over("neg_u", [P, P], 103.5)
    s0 = over("state", [P, P], 104)
    ya_hi = over("ya_hi", [P, DT, T], 48, F32R)
    ya_lo = over("ya_lo", [P, DT, T], 56, F32R)
    yb_hi = over("yb_hi", [P, DT, T], 8, F32R)
    yb_lo = over("yb_lo", [P, DT, T], 0, F32R)
    gate_sig = over("gate_sigmoids", [P, 2, DT, T], 32)
    merged = over("merged", [P, DT, T], 32)
    level_floats = over("level_floats", [P, 2, len(LEVELS), P], 98)
    qk = over("qk", [P, GROUPS, 2 * DT, T], 0)
    vtok = over("v_tokens", [P, GROUPS, NCH, D], 48)
    amask = over("attention_mask", [P, GROUPS, 3 * P], 72)
    logits = (over("logits_0", [P, GROUPS, 3 * P], 76.5), over("logits_1", [P, GROUPS, 3 * P], 87.5))
    pt = (over("probs_t_0", [P, GROUPS, 3 * P], 81), over("probs_t_1", [P, GROUPS, 3 * P], 92))
    cos = over("cos", [P, T], 85.5)
    sin = over("sin", [P, T], 86.5)
    qkg = over("qk_gained", [P, 2, 2, T], 87.5)
    ssr = over("qk_rstd", [P, 2, 2, T], 91.5)
    rot = over("rotated", [P, 2, T], 95.5)
    rope_m = over("rope_matrix", [P, P], 97.5)
    cum_rhs = over("cum_rhs", [P, 2 * P], 98)
    ls = over("log_sigmoid", [P, NCH, HEADS], 99)
    ls_t = over("log_sigmoid_t", [P, NCH, HEADS], 99.125)
    bf_b = over("b_f_rows", [P, HEADS], 99.25)
    ls_b = over("log_sigmoid_b", [P, NCH, P], 99.5)
    stat = over("attention_stats", [P, 2, 8], 100.5)
    pos_i = over("positions", [P, T], 100.625, I32)
    ang = over("angle", [P, T], 101.625)
    o_hi = over("o_hi", [P, DT, T], 0, F32R)
    o_lo = over("o_lo", [P, DT, T], 16, F32R)

    lin = nc.alloc_psum_tensor("linear_banks", [P, 3, 512], F32)
    sv = nc.alloc_psum_tensor("solve_banks", [P, 5, 512], F32)

    def c_(name):
        a, n = CONST[name]
        return const[:, a:a + n]

    ident, mean_w, head_w, tri, mask = (c_(n) for n in ("ident", "mean", "head", "tri", "mask"))

    def col(name, i=0, l=None):
        a = COL[name if l is None else (name, l)] + i
        return cols[:, a:a + 1]

    def wide(ap, n, dim=1):
        return ap.unsqueeze(dim).to_broadcast([P, n, ap.shape[-1]])

    consts_loaded = signal("consts_loaded")
    x_loaded = [signal(f"x_loaded_{i}") for i in range(4)]
    masks_loaded = signal("masks_loaded")
    raw_loaded = [signal(f"raw_loaded_{s}") for s in range(RAW_SLOTS)]
    small_loaded = signal("small_loaded")
    hi_ready = signal("hi_ready")
    lo_ready = signal("lo_ready")
    halves_used = signal("halves_used")
    lin_filled = signal("lin_filled")
    emptied = {"act": signal("emptied_by_act"), "dve": signal("emptied_by_dve")}
    x_normed = signal("x_normed")
    squared = signal("squared")
    piece_used = signal("piece_used")
    norm_summed = signal("norm_summed")
    dve_step = signal("dve_step")
    act_step = signal("act_step")
    var_ready = signal("var_ready")
    root_ready = signal("root_ready")
    h_temp_ready = signal("h_temp_ready")
    h_hi_ready = signal("h_hi_ready")
    h_ready = signal("h_ready")
    silu_ready = signal("silu_ready")
    hidden_hi = signal("hidden_hi")
    hidden_ready = signal("hidden_ready")
    mod_summed = signal("mod_summed")
    c_ready = signal("c_ready")
    mixed = signal("mixed")
    tanh_ready = signal("tanh_ready")
    decay_ready = signal("decay_ready")
    v_done = signal("v_done")
    kk_scaled = signal("kk_scaled")
    rk_ready = signal("rk_ready")
    rk_used = signal("rk_used")
    va_centred = signal("va_centred")
    va_ready = signal("va_ready")
    ya_temp = signal("ya_temp")
    ya_hi_ready = signal("ya_hi_ready")
    ya_ready = signal("ya_ready")
    scaled = signal("scaled")
    group_squared = signal("group_squared")
    t_ready = [signal(f"t_ready_{b}") for b in range(2)]
    q_copied = [signal(f"q_copied_{b}") for b in range(2)]
    q_started = [signal(f"q_started_{b}") for b in range(2)]
    q_final = [signal(f"q_final_{b}") for b in range(2)]
    z_done = [signal(f"z_done_{b}") for b in range(2)]
    z_ready = [signal(f"z_ready_{b}") for b in range(2)]
    p_done = [signal(f"p_done_{b}") for b in range(2)]
    turned = [signal(f"turned_{b}") for b in range(2)]
    rec_pe = signal("recurrence_products")
    rec_dve = signal("recurrence_kept")
    yb_temp = signal("yb_temp")
    yb_hi_ready = signal("yb_hi_ready")
    yb_ready = signal("yb_ready")
    merged_ready = signal("merged_ready")
    merged_hi = signal("merged_hi")
    merged_split = signal("merged_split")
    qk_ready = signal("qk_ready")
    lsb_ready = signal("lsb_ready")
    fexp = signal("fexp")
    logits_done = signal("logits_done")
    logits_read = signal("logits_read")
    max_ready = signal("max_ready")
    probs_ready = signal("probs_ready")
    norm_ready = signal("norm_ready")
    pt_done = signal("pt_done")
    pt_ready = signal("pt_ready")
    o_hi_ready = signal("o_hi_ready")
    o_ready = signal("o_ready")
    angle_ready = signal("angle_ready")
    rope_ready = signal("rope_ready")
    stored = signal("stored")
    masks_ready = signal("masks_ready")
    zeroed = signal("zeroed")

    piece_free = []
    used_pieces = [0]

    def add_piece(last_of=None):
        if last_of is None:
            used_pieces[0] += 1
            piece_free.append((piece_used, used_pieces[0]))
        elif last_of[0] == "norm":
            piece_free.append((norm_summed, last_of[1] + 1))
        else:
            piece_free.append((lin_filled, PLAN.filled[last_of]))
        return len(piece_free) - 1

    half_free = []
    used_halves = [0]

    def add_half(last_of=None):
        if last_of is None:
            used_halves[0] += 1
            half_free.append((halves_used, used_halves[0]))
        else:
            half_free.append((lin_filled, PLAN.filled[last_of]))

    def add_units(keys):
        for key in keys:
            add_half()
            add_half(key)

    def add_ffn(i):
        add_units(("gu", i, j) for j in range(FT))
        for w in range(2 * DOWN_UNITS):
            last = (w + 1) * HALF - 1
            add_half(("down", i, last // (2 * FT)) if (last + 1) % (2 * FT) == 0 else None)

    for l in range(2):
        add_ffn(2 * l)
        add_units([("shift", l, s) for s in range(13)] + [("va", l, s) for s in range(4)]
                  + [("u", l, s) for s in range(4)])
        add_units(("gate", l, n) for n in range(DT))
        add_units((k, l, s) for k in ("pa", "pb") for s in range(4))
        add_units(("out", l, d) for d in range(4))
        add_ffn(2 * l + 1)
    for l in range(2):
        add_ffn(4 + 2 * l)
        for g in range((1, 3)[l]):
            for s in range(4):
                add_units([("qk", l, g, 2 * s), ("qk", l, g, 2 * s + 1), ("v", l, g, s)])
        if l == 0:
            add_units([("f", 0)])
        add_units(("out", 2 + l, d) for d in range(4))
        add_ffn(5 + 2 * l)
    assert len(half_free) == 2 * PLAN.units

    PIECE = {}

    def norm_pieces(n):
        for i in range(4):
            PIECE["norm", n, i] = add_piece(("norm", n) if i == 3 else None)

    for b in range(2):
        for l in range(2):
            if b == 0:
                norm_pieces(3 * l)
                norm_pieces(3 * l + 1)
                for s in range(4):
                    PIECE["kk", l, s] = add_piece(("kk", l, s))
                for s in range(4):
                    PIECE["vvar", l, s] = add_piece()
                norm_pieces(3 * l + 2)
            else:
                norm_pieces(7 + 3 * l)
                norm_pieces(8 + 3 * l)
                for g in range((1, 3)[l]):
                    for c in range(DT):
                        PIECE["ss", l, g, c] = add_piece(("ss", l, g, c))
                norm_pieces(9 + 3 * l)
        if b == 0:
            norm_pieces(6)

    PIECE_USED = {("vvar", l): piece_free[PIECE["vvar", l, 3]][1] for l in range(2)}

    def gu_key(n):
        return "gu", n // FT, n % FT

    def wait_filled(eng, key):
        eng.wait_ge(lin_filled, PLAN.filled[key])
        return lin[:, PLAN.uses[key][0] % 3, :]

    def wait_emptied(eng, key):
        _, engine, count = PLAN.uses[key]
        eng.wait_ge(emptied[engine], count)

    def pairs(bank):
        return bank.rearrange("p (a t) -> p a t", a=2)

    FFN_AT = {}
    for i in range(8):
        FFN_AT[i] = 2 * PLAN.unit["ffn", i]
    MIX_AT = {m: 2 * PLAN.unit["mix", m] for m in range(4)}
    OUT_AT = {m: 2 * PLAN.unit["out", m] for m in range(4)}
    HALVES = 2 * PLAN.units
    X_FROM = {1: ("down", 0), 2: ("out", 0), 3: ("down", 1), 4: ("down", 2), 5: ("out", 1), 6: ("down", 3),
              8: ("down", 4), 9: ("out", 2), 10: ("down", 5), 11: ("down", 6), 12: ("out", 3), 13: ("down", 7)}

    NORM_OF = {key: n for n, key in X_FROM.items() if n < 13}
    norm_bank = sv[:, 4, 0:T]

    def shift_of(n, c):
        l, sub = divmod(n - 7, 3)
        at_ = 72 * l + 24 * sub + c
        return mod[:, at_:at_ + 1]

    def pairs_left(n):
        return range({0: 4, 7: 0}.get(n, 3), 4)

    def x_wait(eng, n, i):
        if n == 0:
            eng.wait_ge(x_loaded[i], 16)
        elif n == 7:
            eng.wait_ge(x_normed, i + 1)
        else:
            wait_emptied(eng, (*X_FROM[n], i))

    with nc.Block() as block:

        @block.sync
        def _(sp):
            for i in range(4):
                sp.dma_start(x[:, 2 * i:2 * i + 2, :], src["x"][:, 2 * i:2 * i + 2, :]).then_inc(x_loaded[i], 16)
                if i == 0:
                    sp.dma_start(const[:], src["const"]).then_inc(consts_loaded, 16)
            sp.dma_start(cols[:], src["cols"]).then_inc(consts_loaded, 16)
            sp.dma_start(mod_b[:], src["mod_b"]).then_inc(consts_loaded, 16)

            issued = [0]

            def load(count):
                for n in range(issued[0], issued[0] + count):
                    if n >= RAW_SLOTS:
                        kind, m = PLAN.items[n - RAW_SLOTS]
                        if kind == "unit":
                            sp.wait_ge(lo_ready, 2 * m + 2)
                        else:
                            sp.wait_ge(mod_summed, m + 1)
                    kind, m = PLAN.items[n]
                    sp.dma_start(raw[:, n % RAW_SLOTS, :], src["stream" if kind == "unit" else "mod_w"][m])\
                        .then_inc(raw_loaded[n % RAW_SLOTS], 16)
                issued[0] += count

            def load_to(u):
                load((PLAN.item_of["unit", u] if u < PLAN.units else len(PLAN.items)) - issued[0])

            def small(l):
                sp.wait_ge(masks_ready, 1)
                if l:
                    x_wait(sp, 2, 3)
                sp.dma_start(w2a2[:], src["w2a2"][l]).then_inc(small_loaded, 16)
                sp.dma_start(v2[:], src["v2"][l]).then_inc(small_loaded, 16)
                sp.dma_start(w0_b[:], src["w0"][l].partition_broadcast(P)).then_inc(small_loaded, 16)
                sp.dma_start(bs_b[:], src["bs"][l].partition_broadcast(P)).then_inc(small_loaded, 16)
                sp.dma_start(ws_t[:], src["ws_t"][l]).then_inc(small_loaded, 16)

            load(RAW_SLOTS)
            sp.dma_start(level_floats[:], src["level_masks"]).then_inc(masks_loaded, 16)
            for l in range(2):
                load_to(PLAN.unit["mix", l])
                small(l)
            load_to(PLAN.unit["mix", 2])
            x_wait(sp, 5, 3)
            sp.dma_start(amask[:, 0, :], src["fox_mask"]).then_inc(small_loaded, 16)
            sp.dma_start(cum_rhs[:], src["cum_rhs"]).then_inc(small_loaded, 16)
            sp.dma_start(bf_b[:], src["b_f"].partition_broadcast(P)).then_inc(small_loaded, 16)
            load_to(PLAN.unit["mix", 3])
            x_wait(sp, 9, 3)
            sp.dma_start(amask[:], src["dil_mask"]).then_inc(small_loaded, 16)
            sp.dma_start(pos_i[:], src["positions"].partition_broadcast(P)).then_inc(small_loaded, 16)
            sp.dma_start(rope_m[:], src["rope_m"]).then_inc(small_loaded, 16)
            load_to(PLAN.units)
            for i in range(4):
                x_wait(sp, 13, i)
                sp.dma_start(out[:, 2 * i:2 * i + 2, :], x[:, 2 * i:2 * i + 2, :]).then_inc(stored, 16)
            sp.wait_ge(stored, 4 * 16)

        @block.gpsimd
        def _(pool):
            pool.wait_ge(masks_loaded, 16)
            nc.gpsimd.tensor_copy(level_masks[:], level_floats[:]).then_inc(masks_ready, 1)
            for l in range(2):
                pool.wait_ge(small_loaded, 80 * (l + 1))
                nc.gpsimd.affine_select(out=ws_t[:], in_=ws_t[:], compare_op=ALU.is_ge, fill=0.0, base=0,
                                        pattern=[[0, DT], [1, CH]], channel_multiplier=-1).then_inc(zeroed, 1)

        @block.scalar
        def _(act):
            steps = [0]
            next_half = [0]

            def link(ins):
                steps[0] += 1
                ins.then_inc(act_step, 1)
                act.wait_ge(act_step, steps[0])

            def keep_ahead(w, ahead=AHEAD):
                while next_half[0] <= min(w + ahead, HALVES - 1):
                    n = next_half[0]
                    item = PLAN.item_of["unit", n // 2]
                    act.wait_ge(raw_loaded[item % RAW_SLOTS], 16 * (item // RAW_SLOTS + 1))
                    if n >= SPLIT_SLOTS:
                        act.wait_ge(*half_free[n - SPLIT_SLOTS])
                    nc.scalar.activation(split[:, n % SPLIT_SLOTS, 0, :],
                                         raw[:, item % RAW_SLOTS, (n % 2) * HALF * P:(n % 2 + 1) * HALF * P],
                                         ACT.Copy).then_inc(hi_ready, 1)
                    next_half[0] += 1

            def square(key, in_):
                n = PIECE[key]
                if n >= 2:
                    act.wait_ge(*piece_free[n - 2])
                nc.scalar.activation(pieces[:, n % 2, :, :], in_, ACT.Square).then_inc(squared, 1)

            roots = [0]

            def root(out_, in_):
                roots[0] += 1
                act.wait_ge(var_ready, roots[0])
                nc.scalar.activation(out_, in_, ACT.Sqrt).then_inc(root_ready, 1)

            def norm(n):
                for i in pairs_left(n):
                    norm_square(n, i)
                act.wait_ge(norm_summed, n + 1)
                nc.scalar.activation(rstd[:], norm_bank, ACT.Sqrt, bias=c_("norm_eps")).then_inc(root_ready, 1)
                if n != 6:
                    split_h(n)

            def norm_square(n, i):
                x_wait(act, n, i)
                square(("norm", n, i), x[:, 2 * i:2 * i + 2, :])

            def early_square(key, d):
                if d and key in NORM_OF:
                    norm_square(NORM_OF[key], d - 1)

            def split_h(n):
                m = n if n < 6 else n - 1
                for i in range(4):
                    act.wait_ge(h_temp_ready, 4 * m + i + 1)
                    if n < 6:
                        nc.scalar.activation(h[:, 0, 2 * i:2 * i + 2, :], pieces[:, i % 2, :, :], ACT.Copy)\
                            .then_inc(h_hi_ready, 1)
                    else:
                        for c in (2 * i, 2 * i + 1):
                            ins = nc.scalar.activation(h[:, 0, c, :], pieces[:, i % 2, c % 2, :], ACT.Identity,
                                                       bias=shift_of(n, c))
                        ins.then_inc(h_hi_ready, 1)

            def ffn(i):
                base = FFN_AT[i]
                norm(ffn_norm(i))
                for j in range(FT):
                    keep_ahead(base + 2 * j + 1)
                    bank = wait_filled(act, ("gu", i, j))
                    n = FT * i + j
                    if n >= 3:
                        wait_emptied(act, gu_key(n - 3))
                    nc.scalar.activation(silu[:, n % 3, :], bank[:, 0:T], ACT.Silu).then_inc(silu_ready, 1)
                    if j:
                        hidden_high(i, j - 1)
                hidden_high(i, FT - 1)
                for d in range(4):
                    halves = down_halves(d)
                    keep_ahead(base + 2 * FT + halves[1])
                    early_square(("down", i), d)
                    keep_ahead(base + 2 * FT + halves[-1])

            def hidden_high(i, j):
                n = FT * i + j
                wait_emptied(act, ("gu", i, j))
                nc.scalar.activation(hidden[:, 0, j, :], product[:, n % 3, :], ACT.Copy).then_inc(hidden_hi, 1)

            def rwkv(l):
                base = MIX_AT[l]
                norm(3 * l + 1)
                for s in range(13):
                    keep_ahead(base + 2 * s + 1)
                    bank = wait_filled(act, ("shift", l, s))
                    n = 13 * l + s
                    if n >= 2:
                        act.wait_ge(mixed, n - 1)
                    nc.scalar.activation(raw_shift[:, n % 2, :, 1:T + 1], pairs(bank), ACT.Copy)\
                        .then_inc(emptied["act"], 1)
                    if s == 1:
                        act.wait_ge(mixed, 13 * l + 1)
                        nc.scalar.activation(lora[0:64, 0, :], lora[0:64, 0, :], ACT.Tanh).then_inc(tanh_ready, 1)
                keep_ahead(base + 2 * 13 - 1)
                for s in range(4):
                    wait_emptied(act, ("z", l, s))
                    part = decay[:, s // 2, (s % 2) * 512:(s % 2 + 1) * 512]
                    nc.scalar.activation(part, part, ACT.Sigmoid).then_inc(decay_ready, 1)
                for s in range(4):
                    bank = wait_filled(act, ("a", l, s))
                    for i in range(2):
                        ins = nc.scalar.activation(a_[:, 2 * s + i, :], bank[:, i * T:(i + 1) * T], ACT.Sigmoid,
                                                   bias=col("a0", 2 * s + i, l))
                    ins.then_inc(emptied["act"], 1)
                if l:
                    for s in range(4):
                        bank = wait_filled(act, ("vr", l, s))
                        if s >= 2:
                            act.wait_ge(v_done, s - 1)
                        for i in range(2):
                            ins = nc.scalar.activation(pair[:, s % 2, i, :], bank[:, i * T:(i + 1) * T],
                                                       ACT.Sigmoid, bias=col("v0", 2 * s + i, l))
                        ins.then_inc(emptied["act"], 1)
                for s in range(4):
                    keep_ahead(base + 2 * (13 + s) + 1)
                    bank = wait_filled(act, ("va", l, s))
                    nc.scalar.activation(va[:, 2 * s:2 * s + 2, :], pairs(bank), ACT.Gelu_apprx_tanh)\
                        .then_inc(emptied["act"], 1)
                for s in range(4):
                    act.wait_ge(kk_scaled, 4 * l + s + 1)
                    square(("kk", l, s), kk[:, 2 * s:2 * s + 2, :])
                for s in range(4):
                    if s % 2 == 0:
                        for i in (s, s + 1):
                            act.wait_ge(va_centred, 4 * l + i + 1)
                            square(("vvar", l, i), va[:, 2 * i:2 * i + 2, :])
                    keep_ahead(base + 2 * (17 + s) + 1, 2 if s == 3 else AHEAD)
                    if s == 3:
                        act.wait_ge(piece_used, PIECE_USED["vvar", l])
                        act.wait_ge(va_centred, 4 * l + 4)
                        nc.scalar.activation(rstd[:], norm_bank, ACT.Sqrt, bias=c_("ln_eps")).then_inc(root_ready, 1)
                    bank = wait_filled(act, ("u", l, s))
                    nc.scalar.activation(u_[:, 2 * s:2 * s + 2, :], pairs(bank), ACT.Gelu_apprx_tanh)\
                        .then_inc(emptied["act"], 1)
                for s in range(4):
                    root(bonus[:, 2 * s:2 * s + 2, :], bonus[:, 2 * s:2 * s + 2, :])
                for s in range(4):
                    bank = wait_filled(act, ("vat", l, s))
                    nc.scalar.activation(va[:, 2 * s:2 * s + 2, :], pairs(bank), ACT.Copy)\
                        .then_inc(emptied["act"], 1)
                for s in range(4):
                    act.wait_ge(ya_temp, 4 * l + s + 1)
                    nc.scalar.activation(ya_hi[:, 2 * s:2 * s + 2, :], u_[:, 2 * s:2 * s + 2, :], ACT.Copy)\
                        .then_inc(ya_hi_ready, 1)
                wait_emptied(act, ("bonus", l, 3))
                for s in range(4):
                    bank = wait_filled(act, ("vt", l, s))
                    nc.scalar.activation(v_[:, 2 * s:2 * s + 2, :], pairs(bank), ACT.Copy)\
                        .then_inc(emptied["act"], 1)
                gates = base + 2 * 21
                solve("cum", l, 0)
                for c, i, a, b in SOLVE:
                    if b and i == GATE_TAKEN:
                        bank = wait_filled(act, ("gate", l, c + 1))
                        act.wait_ge(scaled, DT * l + c + 2)
                        nc.scalar.activation(gate_sig[:, :, c + 1, :], pairs(bank), ACT.Sigmoid)\
                            .then_inc(emptied["act"], 1)
                    if a:
                        solve(a, l, c)
                    if b:
                        solve(b, l, c + 1)
                    stage, s = group_norm_at(c, i)
                    if stage:
                        group_norm(stage, l, s)
                    if b and i in SPLIT_STEPS:
                        keep_ahead(gates + 2 * (c + 1) + 1, 1 + SPLIT_STEPS.index(i))
                    if i == CUM_STEP and c + 2 < DT:
                        solve("cum", l, c + 2)
                proj = gates + 2 * DT
                group_norm("square", l, 3)
                keep_ahead(proj + 1)
                group_norm("root", l, 3)
                keep_ahead(proj + 3)
                group_norm("high", l, 3)
                keep_ahead(proj + 5)
                if l == 0:
                    for s in range(4):
                        bank = wait_filled(act, ("vback", l, s))
                        nc.scalar.activation(v_first[:, 2 * s:2 * s + 2, :], pairs(bank), ACT.Copy)\
                            .then_inc(emptied["act"], 1)
                keep_ahead(proj + 7)
                wait_filled(act, ("gate", l, DT - 1))
                for s in range(4):
                    keep_ahead(proj + 8 + 2 * s + 1)
                    act.wait_ge(merged_ready, 4 * l + s + 1)
                    nc.scalar.activation(h[:, 0, 2 * s:2 * s + 2, :], merged[:, 2 * s:2 * s + 2, :], ACT.Copy)\
                        .then_inc(merged_hi, 1)
                for d in range(4):
                    keep_ahead(OUT_AT[l] + 2 * d + 1)
                    early_square(("out", l), d)

            def group_norm(stage, l, s):
                w = slice(2 * s, 2 * s + 2)
                if stage == "square":
                    wait_emptied(act, ("gmean", l, s))
                    nc.scalar.activation(k_[:, w, :], r_[:, w, :], ACT.Square).then_inc(group_squared, 1)
                elif stage == "root":
                    root(k_[:, w, :], k_[:, w, :])
                elif stage == "high":
                    act.wait_ge(yb_temp, 4 * l + s + 1)
                    nc.scalar.activation(yb_hi[:, w, :], r_[:, w, :], ACT.Copy).then_inc(yb_hi_ready, 1)

            def solve(stage, l, c):
                q, b = DT * l + c, c % 2
                n = q // 2
                four = lambda i: sv[:, 2 * b + i, :].rearrange("p (a t) -> p a t", a=4)
                if stage == "cum":
                    bank = wait_filled(act, ("cum", l, c))
                    cum = bank[:, 0:NCH * (CH + 1)].rearrange("p (j t) -> p j t", j=NCH)
                    if q:
                        act.wait_ge(scaled, q)
                    nc.scalar.activation(e_pos[:], cum, ACT.Exp)
                    nc.scalar.activation(e_neg[:], cum, ACT.Exp, scale=-1.0).then_inc(emptied["act"], 1)
                elif stage == "score0":
                    bank = wait_filled(act, ("kbt", l, c))
                    nc.scalar.activation(kbt[:, b, :, :], bank[:, 0:2 * P].rearrange("p (a t) -> p a t", a=2),
                                         ACT.Copy).then_inc(emptied["act"], 1)
                elif stage[0] == "z":
                    act.wait_ge(z_done[b], 6 * n + int(stage[1]) + 1)
                    nc.scalar.activation(z_neg[:, b, :, :], four(0), ACT.Copy, scale=-1.0).then_inc(z_ready[b], 1)
                elif stage[0] == "t":
                    act.wait_ge(turned[b], 5 * n + int(stage[1]) + 1)
                    nc.scalar.activation(q_inv[:, b, :, :], four(0), ACT.Copy).then_inc(q_copied[b], 1)
                elif stage == "y":
                    bank = wait_filled(act, ("y", l, c))
                    nc.scalar.activation(r_[:, c, :], bank[:, 0:T], ACT.Copy).then_inc(emptied["act"], 1)

            def attention(l):
                base = MIX_AT[2 + l]
                ng = (1, 3)[l]
                norm(8 + 3 * l)
                if l:
                    act.wait_ge(angle_ready, 1)
                    nc.scalar.activation(sin[:], ang[:], ACT.Sin)
                    act.wait_ge(angle_ready, 2)
                    nc.scalar.activation(cos[:], cos[:], ACT.Sin).then_inc(rope_ready, 1)
                half = base

                def qk_root(g, c):
                    bank = wait_filled(act, ("ss", l, g, c))
                    nc.scalar.activation(ssr[:, (DT * g + c) % 2, :, :], pairs(bank), ACT.Sqrt, scale=1.0 / HD,
                                         bias=c_("norm_eps")).then_inc(emptied["act"], 1)

                for g in range(ng):
                    for c in range(DT):
                        keep_ahead(half + 1)
                        half += 2
                        bank = wait_filled(act, ("qk", l, g, c))
                        square(("ss", l, g, c), pairs(bank))
                        n = DT * (g + l) + c
                        if n >= 2:
                            act.wait_ge(qk_ready, n - 1)
                        for i in range(2):
                            gain = col("fox_g", i) if l == 0 else col("dil_g", 2 * g + i)
                            ins = nc.scalar.activation(qkg[:, (DT * g + c) % 2, i, :], bank[:, i * T:(i + 1) * T],
                                                       ACT.Copy, scale=gain)
                        ins.then_inc(emptied["act"], 1)
                        if c:
                            qk_root(g, c - 1)
                        if c % 2:
                            s = c // 2
                            keep_ahead(half + 1)
                            half += 2
                            bank = wait_filled(act, ("v", l, g, s))
                            nc.scalar.activation(vtok[:, g, :, s * 2 * P:(s + 1) * 2 * P], pairs(bank), ACT.Copy)\
                                .then_inc(emptied["act"], 1)
                    qk_root(g, DT - 1)
                if l == 0:
                    keep_ahead(half + 1)
                    act.wait_ge(fexp, 1)
                    link(nc.scalar.activation(ls_t[:], ls_t[:], ACT.Exp))
                    nc.scalar.activation(ls_t[:], ls_t[:], ACT.Ln, bias=1.0).then_inc(fexp, 1)

                def exponentials(hd):
                    act.wait_ge(max_ready, HEADS * l + hd + 1)
                    st = stat[:, hd % 2, :]
                    lg0 = logits[hd % 2][:, 0:ng, 0:P]
                    lg1 = logits[hd % 2][:, 0:ng, P:3 * P]
                    nc.scalar.activation(lg0, lg0, ACT.Exp, scale=HD ** -0.5, bias=st[:, 2:3], accum_out=st[:, 4:5])
                    nc.scalar.activation(lg1, lg1, ACT.Exp, scale=HD ** -0.5, bias=st[:, 3:4], accum_out=st[:, 5:6])\
                        .then_inc(probs_ready, 1)

                def high_of(c):
                    bank = wait_filled(act, ("o", l, c))
                    nc.scalar.activation(o_hi[:, c, :], bank[:, 0:T], ACT.Copy).then_inc(o_hi_ready, 1)

                exponentials(0)
                for hd in range(HEADS):
                    if hd + 1 < HEADS:
                        exponentials(hd + 1)
                    for g in range(ng):
                        m = HEADS * g + hd if l == 0 else HEADS + GROUPS * hd + g
                        act.wait_ge(pt_done, m + 1)
                        nc.scalar.activation(pt[hd % 2][:, g, :], sv[:, 3 + m % 2, 0:3 * P], ACT.Copy).then_inc(pt_ready, 1)
                    if hd % 2 and hd > 1:
                        high_of(hd // 2 - 1)
                high_of(DT - 1)
                for d in range(4):
                    keep_ahead(OUT_AT[2 + l] + 2 * d + 1)
                    early_square(("out", 2 + l), d)

            for i in range(4):
                norm_square(0, i)
            keep_ahead(-1, 2)
            act.wait_ge(consts_loaded, 48)
            nc.scalar.activation(cols[:, COL["c"]:COL["c"] + DT], cols[:, COL["c"]:COL["c"] + DT], ACT.Silu)\
                .then_inc(c_ready, 1)
            for l in range(2):
                ffn(2 * l)
                rwkv(l)
                ffn(2 * l + 1)
            norm(6)
            for l in range(2):
                ffn(4 + 2 * l)
                attention(l)
                ffn(5 + 2 * l)

        @block.vector
        def _(dve):
            steps = [0]
            next_half = [0]
            V = nc.vector

            def link(ins):
                steps[0] += 1
                ins.then_inc(dve_step, 1)
                dve.wait_ge(dve_step, steps[0])

            def keep_ahead(w, ahead=AHEAD):
                while next_half[0] <= min(w + ahead, HALVES - 1):
                    n = next_half[0]
                    item = PLAN.item_of["unit", n // 2]
                    dve.wait_ge(hi_ready, n + 1)
                    V.tensor_tensor(split[:, n % SPLIT_SLOTS, 1, :],
                                    raw[:, item % RAW_SLOTS, (n % 2) * HALF * P:(n % 2 + 1) * HALF * P],
                                    split[:, n % SPLIT_SLOTS, 0, :].bitcast(F32), ALU.subtract).then_inc(lo_ready, 1)
                    next_half[0] += 1

            roots = [0]

            def root_wait():
                dve.wait_ge(root_ready, roots[0])

            def norm(n):
                roots[0] += 1
                root_wait()
                link(V.reciprocal(rstd[:], rstd[:]))
                if n == 6:
                    for i in range(4):
                        for c in (2 * i, 2 * i + 1):
                            ins = V.scalar_tensor_tensor(x[:, c, :], x[:, c, :], col("final_norm", c), rstd[:],
                                                         ALU.mult, ALU.mult)
                        ins.then_inc(x_normed, 1)
                    return
                m = n if n < 6 else n - 1
                normed_pair(n, m, 0)
                for i in range(4):
                    if i < 3:
                        normed_pair(n, m, i + 1)
                    dve.wait_ge(h_hi_ready, 4 * m + i + 1)
                    if n < 6:
                        V.tensor_tensor(h[:, 1, 2 * i:2 * i + 2, :], pieces[:, i % 2, :, :],
                                        h[:, 0, 2 * i:2 * i + 2, :].bitcast(F32), ALU.subtract).then_inc(h_ready, 1)
                    else:
                        for c in (2 * i, 2 * i + 1):
                            ins = V.scalar_tensor_tensor(h[:, 1, c, :], pieces[:, i % 2, c % 2, :], shift_of(n, c),
                                                         h[:, 0, c, :].bitcast(F32), ALU.add, ALU.subtract)
                        ins.then_inc(h_ready, 1)

            def normed_pair(n, m, i):
                if i >= 2:
                    dve.wait_ge(h_ready, 4 * m + i - 1)
                for c in (2 * i, 2 * i + 1):
                    o = pieces[:, i % 2, c % 2, :]
                    if n < 6:
                        l, w = divmod(n, 3)
                        name = ("ffn1_norm", "mix_norm", "ffn2_norm")[w]
                        ins = V.scalar_tensor_tensor(o, x[:, c, :], col(name, c, l), rstd[:], ALU.mult, ALU.mult)
                    else:
                        ins = V.scalar_tensor_tensor(o, x[:, c, :], gain2[:, n - 7, c:c + 1], rstd[:],
                                                     ALU.mult, ALU.mult)
                ins.then_inc(h_temp_ready, 1)

            def mod_sum(m, first=0, last=DT):
                item = PLAN.item_of["mod", m]
                if first == 0:
                    dve.wait_ge(raw_loaded[item % RAW_SLOTS], 16 * (item // RAW_SLOTS + 1))
                    if m >= 2:
                        wait_emptied(dve, ("mod", m - 2))
                acc = mod_acc[:, m % 2, :]
                w = raw[:, item % RAW_SLOTS, :].rearrange("p (k n) -> p k n", k=DT)
                for k in range(first, last):
                    if k == 0:
                        ins = V.tensor_scalar(acc, w[:, 0, :], col("c", 0), None, ALU.mult)
                    else:
                        ins = V.scalar_tensor_tensor(acc, w[:, k, :], col("c", k), acc, ALU.mult, ALU.add)
                    if k < DT - 1:
                        link(ins)
                    else:
                        ins.then_inc(mod_summed, 1)

            def mod_keep(m):
                bank = wait_filled(dve, ("mod", m))
                V.tensor_tensor(mod[:, 2 * m:2 * m + 2], bank[:, 0:2], mod_b[:, 2 * m:2 * m + 2], ALU.add)\
                    .then_inc(emptied["dve"], 1)

            def hidden_rest(i, j):
                n = FT * i + j
                dve.wait_ge(hidden_hi, n + 1)
                V.tensor_tensor(hidden[:, 1, j, :], product[:, n % 3, :], hidden[:, 0, j, :].bitcast(F32),
                                ALU.subtract).then_inc(hidden_ready, 1)

            def ffn(i):
                base = FFN_AT[i]
                norm(ffn_norm(i))
                for j in range(FT):
                    keep_ahead(base + 2 * j + 1)
                    n = FT * i + j
                    bank = wait_filled(dve, ("gu", i, j))
                    dve.wait_ge(silu_ready, n + 1)
                    if n >= 3:
                        dve.wait_ge(hidden_ready, n - 2)
                    V.tensor_tensor(product[:, n % 3, :], silu[:, n % 3, :], bank[:, T:2 * T], ALU.mult)\
                        .then_inc(emptied["dve"], 1)
                    if i < 4 and 0 < j <= 3 * MOD_FFN:
                        mod_sum(MOD_AT["ffn", i, (j - 1) // 3], *MOD_SPREAD[(j - 1) % 3])
                    if i < 4 and mod_done(j) is not None:
                        mod_keep(MOD_AT["ffn", i, mod_done(j)])
                    if j:
                        hidden_rest(i, j - 1)
                hidden_rest(i, FT - 1)
                for d in range(4):
                    for n, w in enumerate(down_halves(d)):
                        keep_ahead(base + 2 * FT + w)
                        if i < 4 and n < 2:
                            mod_sum(MOD_AT["ffn", i, MOD_FFN + d], 4 * n, 4 * n + 4)
                    residual(("down", i, d), 2 * d, 0.5 if i < 4 else None, (i - 4) // 2 * 3 + (i - 4) % 2 * 2)
                    if i < 4:
                        mod_keep(MOD_AT["ffn", i, MOD_FFN + d])

            def residual(key, c, factor, which):
                bank = pairs(wait_filled(dve, key))
                if factor is not None:
                    V.scalar_tensor_tensor(x[:, c:c + 2, :], bank, factor, x[:, c:c + 2, :], ALU.mult, ALU.add)\
                        .then_inc(emptied["dve"], 1)
                else:
                    V.scalar_tensor_tensor(x[:, c, :], bank[:, 0, :], gate2[:, which, c:c + 1], x[:, c, :],
                                           ALU.mult, ALU.add)
                    V.scalar_tensor_tensor(x[:, c + 1, :], bank[:, 1, :], gate2[:, which, c + 1:c + 2],
                                           x[:, c + 1, :], ALU.mult, ALU.add).then_inc(emptied["dve"], 1)

            def rwkv(l):
                base = MIX_AT[l]
                norm(3 * l + 1)
                link(V.memset(raw_shift[:, :, :, 0:1], 0.0))
                for s in range(13):
                    keep_ahead(base + 2 * s + 1)
                    n = 13 * l + s
                    wait_emptied(dve, ("shift", l, s))
                    if n:
                        dve.wait_ge(mixed, n)
                    b = raw_shift[:, n % 2, :, :]
                    link(V.tensor_tensor(diff[:], b[:, :, 0:T], b[:, :, 1:T + 1], ALU.subtract))
                    if s == 0:
                        dst = [(lora[:, 0, :], 24), (lora[:, 1, :], 25)]
                    elif s < 9:
                        dst = [(r_[:, s - 1, :], s - 1), (k_[:, s - 1, :], 8 + s - 1)]
                    else:
                        c = 2 * (s - 9)
                        dst = [(v_[:, c, :], 16 + c), (v_[:, c + 1, :], 17 + c)]
                    for i, (o, m) in enumerate(dst):
                        ins = V.scalar_tensor_tensor(o, diff[:, i, :], col("mu", m, l), b[:, i, 1:T + 1],
                                                     ALU.mult, ALU.add)
                    ins.then_inc(mixed, 1)
                dve.wait_ge(mixed, 13 * l + 13)
                dve.wait_ge(small_loaded, 80 * (l + 1))
                for s in range(4):
                    bank = wait_filled(dve, ("z", l, s))
                    V.tensor_tensor(decay[:, s // 2, (s % 2) * 512:(s % 2 + 1) * 512], bank,
                                    w0_b[:, (s % 2) * 512:(s % 2 + 1) * 512], ALU.add).then_inc(emptied["dve"], 1)
                if l:
                    for s in range(4):
                        wait_emptied(dve, ("vr", l, s))
                        vs = v_[:, 2 * s:2 * s + 2, :]
                        link(V.tensor_tensor(diff[:], v_first[:, 2 * s:2 * s + 2, :], vs, ALU.subtract))
                        link(V.tensor_tensor(diff[:], diff[:], pair[:, s % 2, :, :], ALU.mult))
                        V.tensor_tensor(vs, vs, diff[:], ALU.add).then_inc(v_done, 1)
                        dve.wait_ge(v_done, s + 1)
                for s in range(4):
                    keep_ahead(base + 2 * (13 + s) + 1)
                    for c in (2 * s, 2 * s + 1):
                        ins = V.tensor_scalar(kk[:, c, :], k_[:, c, :], col("k_k", c, l), None, ALU.mult)
                    ins.then_inc(kk_scaled, 1)
                for s in range(4):
                    bank = wait_filled(dve, ("kk", l, s))
                    V.tensor_scalar(bonus[:, 2 * s:2 * s + 2, :], pairs(bank), 1e-24, None, ALU.max)\
                        .then_inc(emptied["dve"], 1)
                bank = wait_filled(dve, ("vmean", l))
                V.tensor_copy(rstd[:], bank[:, 0:T]).then_inc(emptied["dve"], 1)
                wait_emptied(dve, ("vmean", l))
                for s in range(4):
                    w = slice(2 * s, 2 * s + 2)
                    V.tensor_tensor(va[:, w, :], va[:, w, :], wide(rstd[:], 2), ALU.subtract).then_inc(va_centred, 1)
                wait_emptied(dve, ("a", l, 3))
                a0 = COL["k_a", l]
                link(V.tensor_scalar(one_less_ka[:, l, :], cols[:, a0:a0 + DT], -1.0, 1.0, ALU.mult, ALU.add))
                for s in range(4):
                    keep_ahead(base + 2 * (17 + s) + 1, 2 if s == 3 else AHEAD)
                    if s < 2:
                        keys_of(l, s)
                roots[0] += 1
                root_wait()
                link(V.reciprocal(rstd[:], rstd[:]))
                for s in range(4):
                    w = slice(2 * s, 2 * s + 2)
                    link(V.tensor_tensor(va[:, w, :], va[:, w, :], wide(rstd[:], 2), ALU.mult))
                    for c in (2 * s, 2 * s + 1):
                        ins = V.tensor_scalar(va[:, c, :], va[:, c, :], col("ln_g", c, l), col("ln_b", c, l),
                                              ALU.mult, ALU.add)
                    ins.then_inc(va_ready, 1)
                keys_of(l, 2)
                keys_of(l, 3)
                for s in range(4):
                    roots[0] += 1
                    root_wait()
                    w = slice(2 * s, 2 * s + 2)
                    link(V.tensor_tensor(kk[:, w, :], kk[:, w, :], bonus[:, w, :], ALU.mult))
                    link(V.tensor_tensor(a_[:, w, :], kk[:, w, :], a_[:, w, :], ALU.mult))
                for s in range(4):
                    bank = wait_filled(dve, ("sgu", l, s))
                    w = slice(2 * s, 2 * s + 2)
                    bs = bs_b[:, 2 * s * CH:(2 * s + 2) * CH].rearrange("p (g t) -> p g t", g=2)
                    bank4 = bank.rearrange("p (g j t) -> p g j t", g=2, j=NCH)
                    d4 = diff[:].rearrange("p g (j t) -> p g j t", j=NCH)
                    for j in range(NCH):
                        ins = V.tensor_tensor(d4[:, :, j, :], bank4[:, :, j, :], bs, ALU.add)
                    ins.then_inc(emptied["dve"], 1)
                    wait_emptied(dve, ("sgu", l, s))
                    V.tensor_tensor(u_[:, w, :], u_[:, w, :], diff[:], ALU.mult).then_inc(ya_temp, 1)
                    dve.wait_ge(ya_temp, 4 * l + s + 1)
                    if s:
                        spatial_rest(l, s - 1)
                spatial_rest(l, 3)
                for s in range(4):
                    n = 4 * l + s
                    if s >= 2:
                        wait_filled(dve, ("bonus", l, s - 2))
                    for c in (2 * s, 2 * s + 1):
                        ins = V.scalar_tensor_tensor(pair[:, s % 2, c % 2, :], r_[:, c, :], col("r_k", c, l),
                                                     k_[:, c, :], ALU.mult, ALU.mult)
                    ins.then_inc(rk_ready, 1)
                    if s:
                        bonus_of(l, s - 1)
                bonus_of(l, 3)
                for b in (beta, kappa):
                    V.memset(b[0:64, 1, :, :], 0.0)
                    V.memset(b[64:128, 0, :, :], 0.0)
                link(V.memset(s0[:], 0.0))
                if l == 0:
                    dve.wait_ge(masks_ready, 1)
                gates = base + 2 * 21
                solve("cum", l, 0)
                for c, i, a, b in SOLVE:
                    if a:
                        solve(a, l, c)
                        if a in MOD_STAGES:
                            mod_keep(MOD_AT["solve", l, c, MOD_STAGES.index(a)])
                    if b:
                        solve(b, l, c + 1)
                    stage, s = group_norm_at(c, i)
                    if stage:
                        group_norm(stage, l, s)
                    if a and i < len(MOD_SUMS):
                        which, first, last = MOD_SUMS[i]
                        mod_sum(MOD_AT["solve", l, c, which], first, last)
                    if b and i in SPLIT_STEPS:
                        keep_ahead(gates + 2 * (c + 1) + 1, 1 + SPLIT_STEPS.index(i))
                    if i == len(SECOND_HALF) - 1 and c + 2 < DT:
                        solve("cum", l, c + 2)
                proj = gates + 2 * DT
                group_norm("mean", l, 3)
                keep_ahead(proj + 1)
                first_product(l, 0)
                for stage in ("var", "invert0", "invert1"):
                    group_norm(stage, l, 3)
                keep_ahead(proj + 3)
                first_product(l, 1)
                for stage in ("scale", "affine", "bonus"):
                    group_norm(stage, l, 3)
                keep_ahead(proj + 5)
                first_product(l, 2)
                group_norm("rest", l, 3)
                keep_ahead(proj + 7)
                first_product(l, 3)
                for s in range(4):
                    keep_ahead(proj + 8 + 2 * s + 1)
                    w = slice(2 * s, 2 * s + 2)
                    bank = wait_filled(dve, ("pb", l, s))
                    V.tensor_tensor(diff[:], pairs(bank), gate_sig[:, 1, w, :], ALU.mult).then_inc(emptied["dve"], 1)
                    wait_emptied(dve, ("pb", l, s))
                    V.tensor_tensor(merged[:, w, :], merged[:, w, :], diff[:], ALU.add).then_inc(merged_ready, 1)
                    dve.wait_ge(merged_hi, 4 * l + s + 1)
                    V.tensor_tensor(h[:, 1, w, :], merged[:, w, :], h[:, 0, w, :].bitcast(F32), ALU.subtract)\
                        .then_inc(merged_split, 1)
                for d in range(4):
                    keep_ahead(OUT_AT[l] + 2 * d + 1)
                    residual(("out", l, d), 2 * d, 1.0, None)

            def first_product(l, s):
                w = slice(2 * s, 2 * s + 2)
                bank = wait_filled(dve, ("pa", l, s))
                wait_emptied(dve, ("gate", l, DT - 1))
                V.tensor_tensor(merged[:, w, :], pairs(bank), gate_sig[:, 0, w, :], ALU.mult)\
                    .then_inc(emptied["dve"], 1)

            def group_norm(stage, l, s):
                w = slice(2 * s, 2 * s + 2)
                o = k_[:, w, :]
                if stage == "mean":
                    wait_emptied(dve, ("y", l, 2 * s + 1))
                    bank = wait_filled(dve, ("gmean", l, s))
                    V.scalar_tensor_tensor(r_[:, w, :], pairs(bank), -1.0 / HD, r_[:, w, :], ALU.mult, ALU.add)\
                        .then_inc(emptied["dve"], 1)
                elif stage == "var":
                    bank = wait_filled(dve, ("gvar", l, s))
                    V.tensor_scalar(o, pairs(bank), 1.0 / HD, GN_EPS, ALU.mult, ALU.add).then_inc(emptied["dve"], 1)
                elif stage == "invert0":
                    wait_emptied(dve, ("gvar", l, s))
                    V.reciprocal(k_[:, 2 * s, :], k_[:, 2 * s, :])
                elif stage == "invert1":
                    V.reciprocal(k_[:, 2 * s + 1, :], k_[:, 2 * s + 1, :]).then_inc(var_ready, 1)
                    roots[0] += 1
                elif stage == "scale":
                    root_wait()
                    link(V.tensor_tensor(r_[:, w, :], r_[:, w, :], o, ALU.mult))
                elif stage == "affine":
                    for c in (2 * s, 2 * s + 1):
                        link(V.tensor_scalar(r_[:, c, :], r_[:, c, :], col("gn_g", c, l), col("gn_b", c, l),
                                             ALU.mult, ALU.add))
                elif stage == "bonus":
                    V.tensor_tensor(r_[:, w, :], r_[:, w, :], bonus[:, w, :], ALU.add).then_inc(yb_temp, 1)
                elif stage == "rest":
                    dve.wait_ge(yb_hi_ready, 4 * l + s + 1)
                    V.tensor_tensor(yb_lo[:, w, :], r_[:, w, :], yb_hi[:, w, :].bitcast(F32), ALU.subtract)\
                        .then_inc(yb_ready, 1)

            def keys_of(l, s):
                o = bonus[:, 2 * s:2 * s + 2, :]
                V.reciprocal(o, o).then_inc(var_ready, 1)
                for c in (2 * s, 2 * s + 1):
                    link(V.tensor_scalar(diff[:, c % 2, :], a_[:, c, :], col("k_a", c, l),
                                         one_less_ka[:, l, c:c + 1], ALU.mult, ALU.add))
                    link(V.tensor_tensor(k_[:, c, :], k_[:, c, :], diff[:, c % 2, :], ALU.mult))

            def spatial_rest(l, s):
                w = slice(2 * s, 2 * s + 2)
                dve.wait_ge(ya_hi_ready, 4 * l + s + 1)
                V.tensor_tensor(ya_lo[:, w, :], u_[:, w, :], ya_hi[:, w, :].bitcast(F32), ALU.subtract)\
                    .then_inc(ya_ready, 1)

            def bonus_of(l, s):
                bank = wait_filled(dve, ("bonus", l, s))
                w = slice(2 * s, 2 * s + 2)
                V.tensor_tensor(bonus[:, w, :], pairs(bank), v_[:, w, :], ALU.mult).then_inc(emptied["dve"], 1)

            def solve(stage, l, c):
                q, b = DT * l + c, c % 2
                n = q // 2
                four = lambda i: sv[:, 2 * b + i, :].rearrange("p (a t) -> p a t", a=4)
                b4 = sv[:, 4, :]
                if stage == "cum":
                    wait_emptied(dve, ("cum", l, c))
                    if c >= 2:
                        wait_filled(dve, ("y", l, c - 2))
                    in_chunks = lambda t: t[:, c, :].rearrange("p (j t) -> p j t", j=NCH)
                    neg_incl = e_neg[:, :, 1:CH + 1]
                    V.tensor_tensor(ar[:, b, :, 0:CH], in_chunks(kk), e_pos[:, :, 0:CH], ALU.mult)
                    V.tensor_tensor(ar[:, b, :, CH:2 * CH], in_chunks(r_), e_pos[:, :, 1:CH + 1], ALU.mult)
                    for o, t in ((kappa, k_), (beta, a_)):
                        for hh in range(2):
                            w = slice(64 * hh, 64 * hh + 64)
                            V.tensor_tensor(o[w, hh, :, :], in_chunks(t)[w], neg_incl[w], ALU.mult)
                    for i, t in enumerate((k_, a_)):
                        V.tensor_tensor(kb0[:, i, :], t[:, c, 0:CH], e_neg[:, 0, 1:CH + 1], ALU.mult)
                    V.tensor_tensor(state_scale[:, b:b + 1], e_pos[:, 0, CH:CH + 1], e_neg[:, 1, 0:1], ALU.mult)\
                        .then_inc(scaled, 1)
                elif stage[:5] == "score":
                    i = int(stage[5])
                    bank = wait_filled(dve, ("score", l, c, i))
                    V.tensor_tensor(gbk[b][:, i, :].rearrange("p (a t) -> p a t", a=2),
                                    bank.rearrange("p (a t) -> p a t", a=2), wide(mask, 2), ALU.mult)\
                        .then_inc(emptied["dve"], 1)
                elif stage == "low":
                    bank = wait_filled(dve, ("low", l, c))
                    V.tensor_tensor(t_inv[:, b, :, :], bank.rearrange("p (a t) -> p a t", a=4),
                                    wide(c_("neg2"), 4), ALU.mult).then_inc(emptied["dve"], 1)
                    wait_emptied(dve, ("low", l, c))
                    V.tensor_tensor(t_inv[:, b, :, :], t_inv[:, b, :, :], wide(ident, 4), ALU.add)\
                        .then_inc(t_ready[b], 1)
                    link(V.tensor_tensor(q_inv[:, b, :, :], gbk[b][:, :, 0:CH], wide(c_("neg2t"), 4), ALU.mult))
                    V.tensor_tensor(q_inv[:, b, :, :], q_inv[:, b, :, :], wide(ident, 4), ALU.add)\
                        .then_inc(q_started[b], 1)
                elif stage[0] == "p":
                    s = int(stage[1])
                    dve.wait_ge(p_done[b], 6 * n + s + 1)
                    if s < 5:
                        V.copy_predicated(t_inv[:, b, :, :], wide(level_masks[:, 0, s, :], 4), four(1))\
                            .then_inc(t_ready[b], 1)
                    else:
                        V.copy_predicated(q_inv[:, b, :, :], wide(level_masks[:, 1, s, :], 4), four(1))\
                            .then_inc(q_final[b], 1)
                elif stage == "rhs0":
                    dve.wait_ge(rec_pe, 5 * q + 1)
                    V.tensor_copy(rh[:], b4[:, 0:P]).then_inc(rec_dve, 1)
                elif stage == "u0":
                    dve.wait_ge(rec_pe, 5 * q + 2)
                    V.tensor_scalar(nu[:], b4[:, P:2 * P], -1.0, None, ALU.mult).then_inc(rec_dve, 1)
                elif stage == "st":
                    dve.wait_ge(rec_pe, 5 * q + 3)
                    for hh in range(2):
                        w = slice(64 * hh, 64 * hh + 64)
                        ins = V.tensor_scalar(s0[w, w], b4[w, 2 * P + 64 * hh:2 * P + 64 * hh + 64],
                                              state_scale[w, b:b + 1], None, ALU.mult)
                    ins.then_inc(rec_dve, 1)
                elif stage == "rhs1":
                    dve.wait_ge(rec_pe, 5 * q + 4)
                    V.tensor_copy(rh[:], b4[:, 3 * P:4 * P]).then_inc(rec_dve, 1)
                elif stage == "u1":
                    dve.wait_ge(rec_pe, 5 * q + 5)
                    V.tensor_scalar(nu[:], b4[:, 0:P], -1.0, None, ALU.mult).then_inc(rec_dve, 1)

            def attention(l):
                base = MIX_AT[2 + l]
                ng = (1, 3)[l]
                norm(8 + 3 * l)
                dve.wait_ge(small_loaded, 160 + 48 * (l + 1))
                if l:
                    two_pi = 2 * np.pi
                    c1 = 6.28125
                    c2 = float(np.float32(two_pi - c1))
                    c3 = float(two_pi - c1 - np.float64(np.float32(two_pi - c1)))
                    link(V.tensor_copy(ang[:], pos_i[:]))
                    link(V.tensor_scalar(ang[:], ang[:], col("inv_freq"), None, ALU.mult))
                    link(V.tensor_scalar(cos[:], ang[:], 1.0 / two_pi, 12582912.0, ALU.mult, ALU.add))
                    link(V.tensor_scalar(cos[:], cos[:], -12582912.0, None, ALU.add))
                    for part in (c1, c2, c3):
                        link(V.scalar_tensor_tensor(ang[:], cos[:], -part, ang[:], ALU.mult, ALU.add))
                    V.tensor_scalar(ang[:], ang[:], 3.1415925, -3.1415925, ALU.min, ALU.max).then_inc(angle_ready, 1)
                    dve.wait_ge(angle_ready, 1)
                    link(V.tensor_scalar(cos[:], ang[:], -1.0, None, ALU.mult))
                    link(V.tensor_tensor(cos[:], cos[:], ang[:], ALU.max))
                    V.tensor_scalar(cos[:], cos[:], -1.0, float(np.pi / 2), ALU.mult, ALU.add).then_inc(angle_ready, 1)
                    dve.wait_ge(rope_ready, 1)
                half = base

                def finish_qk(g, c):
                    n = DT * g + c
                    b = n % 2
                    wait_emptied(dve, ("ss", l, g, c))
                    link(V.reciprocal(ssr[:, b, :, :], ssr[:, b, :, :]))
                    if l:
                        bank = wait_filled(dve, ("rot", l, g, c))
                        V.tensor_tensor(rot[:], pairs(bank), wide(sin[:], 2), ALU.mult).then_inc(emptied["dve"], 1)
                        link(V.tensor_tensor(qkg[:, b, :, :], qkg[:, b, :, :], wide(cos[:], 2), ALU.mult))
                        wait_emptied(dve, ("rot", l, g, c))
                        link(V.tensor_tensor(qkg[:, b, :, :], qkg[:, b, :, :], rot[:], ALU.add))
                    V.tensor_tensor(qk[:, g, 2 * c:2 * c + 2, :], qkg[:, b, :, :], ssr[:, b, :, :], ALU.mult)\
                        .then_inc(qk_ready, 1)
                    dve.wait_ge(qk_ready, DT * (g + l) + c + 1)

                for g in range(ng):
                    for c in range(DT):
                        keep_ahead(half + 1)
                        half += 2
                        if c:
                            finish_qk(g, c - 1)
                        if c % 2:
                            keep_ahead(half + 1)
                            half += 2
                    finish_qk(g, DT - 1)
                if l == 0:
                    keep_ahead(half + 1)
                    bank = wait_filled(dve, ("f", 0))[:, 0:NCH * HEADS].rearrange("p (j n) -> p j n", j=NCH)
                    V.tensor_tensor(ls[:], bank, wide(bf_b[:], NCH), ALU.add).then_inc(emptied["dve"], 1)
                    wait_emptied(dve, ("f", 0))
                    link(V.tensor_scalar(ls_t[:], ls[:], -1.0, None, ALU.mult))
                    V.tensor_tensor(ls_t[:], ls_t[:], ls[:], ALU.min).then_inc(fexp, 1)
                    link(V.tensor_scalar(ls[:], ls[:], 0.0, None, ALU.min))
                    dve.wait_ge(fexp, 2)
                    link(V.tensor_tensor(ls[:], ls[:], ls_t[:], ALU.subtract))

                def gates_of(hd):
                    V.tensor_copy(ls_b[:], ls[:, :, hd:hd + 1].to_broadcast([P, NCH, P])).then_inc(lsb_ready, 1)

                def largest(hd):
                    n = HEADS * l + hd
                    dve.wait_ge(logits_done, n + 1)
                    if l == 0 and hd + 1 < HEADS:
                        gates_of(hd + 1)
                    if hd >= 2:
                        dve.wait_ge(pt_done, n - 1 if l == 0 else HEADS + GROUPS * (hd - 1))
                    lg = logits[hd % 2]
                    st = stat[:, hd % 2, :]
                    V.tensor_tensor(lg[:, 0:ng, :], sv[:, 0:ng, 0:3 * P], amask[:, 0:ng, :], ALU.add)\
                        .then_inc(logits_read, 1)
                    dve.wait_ge(logits_read, n + 1)
                    V.tensor_reduce(st[:, 0:1], lg[:, 0:ng, 0:P], AX.XY, ALU.max, negate=True)
                    link(V.tensor_reduce(st[:, 1:2], lg[:, 0:ng, P:3 * P], AX.XY, ALU.max, negate=True))
                    V.tensor_scalar(st[:, 2:4], st[:, 0:2], HD ** -0.5, None, ALU.mult).then_inc(max_ready, 1)

                def rest_of(c):
                    bank = wait_filled(dve, ("o", l, c))
                    dve.wait_ge(o_hi_ready, DT * l + c + 1)
                    V.tensor_tensor(o_lo[:, c, :], bank[:, 0:T], o_hi[:, c, :].bitcast(F32), ALU.subtract)\
                        .then_inc(emptied["dve"], 1)

                if l == 0:
                    gates_of(0)
                largest(0)
                largest(1)
                for hd in range(HEADS):
                    dve.wait_ge(probs_ready, HEADS * l + hd + 1)
                    lg = logits[hd % 2]
                    st = stat[:, hd % 2, :]
                    link(V.reciprocal(st[:, 6:8], st[:, 4:6]))
                    V.tensor_scalar(lg[:, 0:ng, 0:P], lg[:, 0:ng, 0:P], st[:, 6:7], None, ALU.mult)
                    V.tensor_scalar(lg[:, 0:ng, P:3 * P], lg[:, 0:ng, P:3 * P], st[:, 7:8], None, ALU.mult)\
                        .then_inc(norm_ready, 1)
                    if hd + 2 < HEADS:
                        largest(hd + 2)
                    if hd % 2 and hd > 1:
                        rest_of(hd // 2 - 1)
                rest_of(DT - 1)
                for d in range(4):
                    keep_ahead(OUT_AT[2 + l] + 2 * d + 1)
                    residual(("out", 2 + l, d), 2 * d, None, 3 * l + 1)

            keep_ahead(-1, 2)
            dve.wait_ge(consts_loaded, 48)
            dve.wait_ge(c_ready, 1)
            for l in range(2):
                ffn(2 * l)
                rwkv(l)
                ffn(2 * l + 1)
            for l in range(2):
                for sub in range(3):
                    w = 3 * l + sub
                    a = 72 * l + 24 * sub
                    g = COL["norm_g"] + 8 * w
                    link(V.tensor_scalar(gain2[:, w, :], mod[:, a + 8:a + 16], 1.0, None, ALU.add))
                    link(V.tensor_tensor(gain2[:, w, :], gain2[:, w, :], cols[:, g:g + 8], ALU.mult))
                    link(V.tensor_scalar(gate2[:, w, :], mod[:, a + 16:a + 24], 1.0 if sub == 1 else 0.5, None,
                                         ALU.mult))
            norm(6)
            for l in range(2):
                ffn(4 + 2 * l)
                attention(l)
                ffn(5 + 2 * l)

        @block.tensor
        def _(pe):
            M = nc.tensor.matmul

            def bank_for(key):
                n = PLAN.uses[key][0]
                if n >= 3:
                    wait_emptied(pe, PLAN.order[n - 3])
                return lin[:, n % 3, :]

            def half_ready(w):
                pe.wait_ge(lo_ready, w + 1)
                return split[:, w % SPLIT_SLOTS, :, :]

            def three(o, w_hi, w_lo, a_hi, a_lo, start, stop, skip=False):
                M(o, w_hi, a_hi, start=start, stop=False, skip_group_check=skip)
                M(o, w_hi, a_lo, start=False, stop=False, skip_group_check=skip)
                return M(o, w_lo, a_hi, start=False, stop=stop, skip_group_check=skip)

            def two_tiles(w, key, acts, ready=None):
                bank = bank_for(key)
                if ready is not None:
                    halves = [half_ready(w), half_ready(w + 1)]
                    for k in range(DT):
                        if k % 2 == 0:
                            ready(k // 2)
                        for i in range(2):
                            s = halves[i]
                            hi, lo = acts[i]
                            t = slice(k * P, (k + 1) * P)
                            ins = three(bank[:, i * T:(i + 1) * T], s[:, 0, t], s[:, 1, t], hi[:, k, :], lo[:, k, :],
                                        k == 0 and i == 0, k == DT - 1 and i == 1, skip=True)
                            if k == DT - 1:
                                ins.then_inc(halves_used if i == 0 else lin_filled, 1)
                    return
                for i in range(2):
                    s = half_ready(w + i)
                    hi, lo = acts[i]
                    for k in range(DT):
                        t = slice(k * P, (k + 1) * P)
                        ins = three(bank[:, i * T:(i + 1) * T], s[:, 0, t], s[:, 1, t], hi[:, k, :], lo[:, k, :],
                                    k == 0, k == DT - 1)
                    if i == 0:
                        ins.then_inc(halves_used, 1)
                ins.then_inc(lin_filled, 1)

            HH = (h[:, 0, :, :], h[:, 1, :, :])

            def tokens_major(w, key, width):
                bank = bank_for(key)
                for i in range(2):
                    s = half_ready(w + i)
                    for j in range(NCH):
                        o = bank[:, j * width:(j + 1) * width]
                        for k in range(4):
                            m = slice(k * 2 * P, k * 2 * P + width)
                            kk_ = 4 * i + k
                            a_hi = h[:, 0, kk_, j * CH:(j + 1) * CH]
                            a_lo = h[:, 1, kk_, j * CH:(j + 1) * CH]
                            M(o, a_hi, s[:, 0, m], start=(kk_ == 0 and j == 0), stop=False, skip_group_check=True)
                            M(o, a_lo, s[:, 0, m], start=False, stop=False, skip_group_check=True)
                            ins = M(o, a_hi, s[:, 1, m], start=False, stop=(kk_ == DT - 1 and j == NCH - 1),
                                    skip_group_check=True)
                    if i == 0:
                        ins.then_inc(halves_used, 1)
                ins.then_inc(lin_filled, 1)

            def norm(n):
                for i in pairs_left(n):
                    norm_sums(n, i)

            def norm_sums(n, i):
                p = PIECE["norm", n, i]
                pe.wait_ge(squared, p + 1)
                for t in range(2):
                    ins = M(norm_bank, mean_w, pieces[:, p % 2, t, :], start=(i == 0 and t == 0),
                            stop=(i == 3 and t == 1), skip_group_check=True)
                ins.then_inc(piece_used if i < 3 else norm_summed, 1)

            def early_sums(key, d):
                if d and key in NORM_OF:
                    norm_sums(NORM_OF[key], d - 1)

            def h_wait(n):
                m = n if n < 6 else n - 1
                return lambda i: pe.wait_ge(h_ready, 4 * m + i + 1)

            def mod_columns(m):
                bank = bank_for(("mod", m))
                pe.wait_ge(mod_summed, m + 1)
                for i in range(2):
                    ins = M(bank[:, i:i + 1], mod_acc[:, m % 2, i * P:(i + 1) * P], c_("one"), start=True, stop=True)
                ins.then_inc(lin_filled, 1)

            def ffn(i):
                base = FFN_AT[i]
                norm(ffn_norm(i))
                for j in range(FT):
                    two_tiles(base + 2 * j, ("gu", i, j), (HH, HH), h_wait(ffn_norm(i)) if j == 0 else None)
                    if i < 4 and mod_done(j) is not None:
                        mod_columns(MOD_AT["ffn", i, mod_done(j)])
                base += 2 * FT
                pe.wait_ge(hidden_ready, FT * (i + 1) - 2)
                for d in range(4):
                    bank = bank_for(("down", i, d))
                    for e in range(2):
                        for k in range(FT):
                            flat = (2 * d + e) * FT + k
                            w = base + flat // HALF
                            if flat % HALF == 0:
                                half_ready(w)
                            if d == 0 and e == 0 and k >= FT - 2:
                                pe.wait_ge(hidden_ready, FT * i + k + 1)
                            s = split[:, w % SPLIT_SLOTS, :, :]
                            t = slice(flat % HALF * P, (flat % HALF + 1) * P)
                            ins = three(bank[:, e * T:(e + 1) * T], s[:, 0, t], s[:, 1, t], hidden[:, 0, k, :],
                                        hidden[:, 1, k, :], k == 0, k == FT - 1)
                            last = e == 1 and k == FT - 1
                            if last:
                                ins.then_inc(lin_filled, 1)
                            elif flat % HALF == HALF - 1:
                                ins.then_inc(halves_used, 1)
                    if i < 4:
                        mod_columns(MOD_AT["ffn", i, MOD_FFN + d])
                    early_sums(("down", i), d)

            def transposes(key, t):
                bank = bank_for(key)
                s = key[-1]
                for i in range(4):
                    ins = nc.tensor.transpose(bank[:, i * P:(i + 1) * P],
                                              t[:, 2 * s + i // 2, (i % 2) * CH:(i % 2 + 1) * CH], ident)
                ins.then_inc(lin_filled, 1)

            def rwkv(l):
                base = MIX_AT[l]
                norm(3 * l + 1)
                for s in range(13):
                    two_tiles(base + 2 * s, ("shift", l, s), (HH, HH), h_wait(3 * l + 1) if s == 0 else None)
                pe.wait_ge(small_loaded, 80 * (l + 1))
                pe.wait_ge(tanh_ready, l + 1)
                for s in range(4):
                    bank = bank_for(("z", l, s))
                    j = s // 2
                    M(bank, lora[0:64, 0, j * CH:(j + 1) * CH], w2a2[0:64, (s % 2) * 512:(s % 2 + 1) * 512],
                      start=True, stop=True).then_inc(lin_filled, 1)
                for s in range(4):
                    bank = bank_for(("a", l, s))
                    for i in range(2):
                        c = 2 * s + i
                        ins = M(bank[:, i * T:(i + 1) * T], w2a2[64:128, c * P:(c + 1) * P], lora[64:128, 0, :],
                                start=True, stop=True)
                    ins.then_inc(lin_filled, 1)
                if l:
                    for s in range(4):
                        bank = bank_for(("vr", l, s))
                        for i in range(2):
                            c = 2 * s + i
                            ins = M(bank[:, i * T:(i + 1) * T], v2[0:32, c * P:(c + 1) * P], lora[0:32, 1, :],
                                    start=True, stop=True)
                        ins.then_inc(lin_filled, 1)
                for s in range(4):
                    two_tiles(base + 2 * (13 + s), ("va", l, s), (HH, HH))
                for s in range(4):
                    bank = bank_for(("kk", l, s))
                    p = PIECE["kk", l, s]
                    pe.wait_ge(squared, p + 1)
                    M(bank, head_w, pieces[:, p % 2, :, :], start=True, stop=True).then_inc(lin_filled, 1)
                bank = bank_for(("vmean", l))
                wait_emptied(pe, ("va", l, 3))
                for k in range(DT):
                    ins = M(bank[:, 0:T], mean_w, va[:, k, :], start=(k == 0), stop=(k == DT - 1))
                ins.then_inc(lin_filled, 1)
                for s in range(4):
                    two_tiles(base + 2 * (17 + s), ("u", l, s), (HH, HH))
                    if s in (1, 2):
                        for i in (2 * s - 2, 2 * s - 1):
                            p = PIECE["vvar", l, i]
                            pe.wait_ge(squared, p + 1)
                            for t in range(2):
                                ins = M(norm_bank, mean_w, pieces[:, p % 2, t, :], start=(i == 0 and t == 0),
                                        stop=(i == 3 and t == 1), skip_group_check=True)
                            ins.then_inc(piece_used, 1)
                for s in range(4):
                    pe.wait_ge(va_ready, 4 * l + s + 1)
                    transposes(("vat", l, s), va)
                pe.wait_ge(zeroed, l + 1)
                for s in range(4):
                    bank = bank_for(("sgu", l, s))
                    wait_emptied(pe, ("vat", l, s))
                    for i in range(4):
                        g, j = 2 * s + i // 2, i % 2
                        ins = M(bank[:, i * P:(i + 1) * P], va[:, g, j * CH:(j + 1) * CH], ws_t[:, g, :],
                                start=True, stop=True)
                    ins.then_inc(lin_filled, 1)
                for s in range(4):
                    bank = bank_for(("bonus", l, s))
                    pe.wait_ge(rk_ready, 4 * l + s + 1)
                    M(bank, head_w, pair[:, s % 2, :, :], start=True, stop=True).then_inc(lin_filled, 1)
                for s in range(4):
                    transposes(("vt", l, s), v_)
                pe.wait_ge(decay_ready, 4 * l + 4)
                gates = base + 2 * 21
                solve("cum", l, 0)
                for c, i, a, b in SOLVE:
                    if a:
                        solve(a, l, c)
                        if a in MOD_STAGES:
                            mod_columns(MOD_AT["solve", l, c, MOD_STAGES.index(a)])
                    if b:
                        solve(b, l, c + 1)
                    stage, s = group_norm_at(c, i)
                    if stage:
                        group_norm(stage, l, s)
                    if b and i in GATE_STEPS:
                        n = i - GATE_STEPS[0]
                        gate_products(l, c + 1, gates + 2 * (c + 1), TPU * n // len(GATE_STEPS),
                                      TPU * (n + 1) // len(GATE_STEPS))
                    if i == CUM_STEP and c + 2 < DT:
                        solve("cum", l, c + 2)
                YA, YB = (ya_hi, ya_lo), (yb_hi, yb_lo)
                proj = gates + 2 * DT
                group_norm("mean", l, 3)
                pe.wait_ge(ya_ready, 4 * l + 4)
                two_tiles(proj, ("pa", l, 0), (YA, YA))
                group_norm("var", l, 3)
                two_tiles(proj + 2, ("pa", l, 1), (YA, YA))
                two_tiles(proj + 4, ("pa", l, 2), (YA, YA))
                if l == 0:
                    pe.wait_ge(yb_temp, 4)
                    for s in range(4):
                        transposes(("vback", l, s), v_)
                two_tiles(proj + 6, ("pa", l, 3), (YA, YA))
                pe.wait_ge(yb_ready, 4 * l + 4)
                for s in range(4):
                    two_tiles(proj + 8 + 2 * s, ("pb", l, s), (YB, YB))
                for d in range(4):
                    two_tiles(OUT_AT[l] + 2 * d, ("out", l, d), (HH, HH),
                              (lambda i: pe.wait_ge(merged_split, 4 * l + i + 1)) if d == 0 else None)
                    early_sums(("out", l), d)

            def gate_products(l, c, w, first, last):
                bank = bank_for(("gate", l, c)) if first == 0 else lin[:, PLAN.uses["gate", l, c][0] % 3, :]
                for f in range(first, last):
                    i, k = divmod(f, DT)
                    s = half_ready(w + i)
                    t = slice(k * P, (k + 1) * P)
                    ins = three(bank[:, i * T:(i + 1) * T], s[:, 0, t], s[:, 1, t], h[:, 0, k, :], h[:, 1, k, :],
                                k == 0, k == DT - 1)
                    if f == DT - 1:
                        ins.then_inc(halves_used, 1)
                if last == TPU:
                    ins.then_inc(lin_filled, 1)

            def group_norm(stage, l, s):
                w = slice(2 * s, 2 * s + 2)
                if stage == "mean":
                    bank = bank_for(("gmean", l, s))
                    wait_emptied(pe, ("y", l, 2 * s + 1))
                    M(bank, head_w, r_[:, w, :], start=True, stop=True).then_inc(lin_filled, 1)
                elif stage == "var":
                    bank = bank_for(("gvar", l, s))
                    pe.wait_ge(group_squared, 4 * l + s + 1)
                    M(bank, head_w, k_[:, w, :], start=True, stop=True).then_inc(lin_filled, 1)

            def solve(stage, l, c):
                q, b = DT * l + c, c % 2
                n = q // 2
                zb, pb, b4 = sv[:, 2 * b, :], sv[:, 2 * b + 1, :], sv[:, 4, :]
                part = lambda i: slice(i * CH, (i + 1) * CH)
                lt, rbt, akt, rkt = (lambda i, a=a: gbk[b][:, i, part(a)] for a in range(4))
                v_tok = lambda j, hh: v_[:, c, j * CH + 64 * hh:j * CH + 64 * hh + 64]
                if stage == "cum":
                    bank = bank_for(("cum", l, c))
                    for j in range(NCH):
                        ins = M(bank[:, j * (CH + 1):(j + 1) * (CH + 1)], decay[:, j, c * P:(c + 1) * P], tri,
                                start=True, stop=True)
                    ins.then_inc(lin_filled, 1)
                elif stage[:5] == "score":
                    i = int(stage[5])
                    hh, j = i // 2, i % 2
                    if i == 0:
                        pe.wait_ge(scaled, q + 1)
                        bank = bank_for(("kbt", l, c))
                        for a in range(2):
                            ins = nc.tensor.transpose(bank[:, part(a)], kb0[:, a, :], ident)
                        ins.then_inc(lin_filled, 1)
                    bank = bank_for(("score", l, c, i))
                    M(bank[:, 0:2 * CH], beta[:, hh, j, :], ar[:, b, j, :], start=True, stop=True)
                    M(bank[:, 2 * CH:4 * CH], kappa[:, hh, j, :], ar[:, b, j, :], start=True, stop=True)\
                        .then_inc(lin_filled, 1)
                elif stage == "low":
                    bank = bank_for(("low", l, c))
                    for i in range(4):
                        ins = M(bank[:, part(i)], ar[:, b, i % 2, 0:CH], beta[:, i // 2, i % 2, :],
                                start=True, stop=True)
                    ins.then_inc(lin_filled, 1)
                elif stage[0] == "z":
                    s = int(stage[1])
                    pe.wait_ge(t_ready[b], 6 * n + s + 1)
                    if s:
                        pe.wait_ge(q_copied[b], 5 * n + s)
                    for i in range(4):
                        ins = M(zb[:, part(i)], lt(i), t_inv[:, b, i, :], start=True, stop=True)
                    ins.then_inc(z_done[b], 1)
                elif stage[0] == "p":
                    s = int(stage[1])
                    if s == 0:
                        pe.wait_ge(q_started[b], n + 1)
                    pe.wait_ge(z_ready[b], 6 * n + s + 1)
                    for i in range(4):
                        if s < 5:
                            ins = M(pb[:, part(i)], q_inv[:, b, i, :], z_neg[:, b, i, :], start=True, stop=True)
                        else:
                            ins = M(pb[:, part(i)], z_neg[:, b, i, :], q_inv[:, b, i, :], start=True, stop=True)
                    ins.then_inc(p_done[b], 1)
                elif stage[0] == "t":
                    s = int(stage[1])
                    pe.wait_ge(t_ready[b], 6 * n + s + 2)
                    for i in range(4):
                        ins = nc.tensor.transpose(zb[:, part(i)], t_inv[:, b, i, :], ident)
                    ins.then_inc(turned[b], 1)
                elif stage == "rhs0":
                    pe.wait_ge(q_final[b], n + 1)
                    for hh in range(2):
                        ins = M(b4[:, 64 * hh:64 * hh + 64], akt(2 * hh), v_tok(0, hh), start=True, stop=True)
                    ins.then_inc(rec_pe, 1)
                elif stage == "u0":
                    pe.wait_ge(rec_dve, 5 * q + 1)
                    for hh in range(2):
                        ins = M(b4[:, P + 64 * hh:P + 64 * hh + 64], q_inv[:, b, 2 * hh, :],
                                rh[:, 64 * hh:64 * hh + 64], start=True, stop=True)
                    ins.then_inc(rec_pe, 1)
                elif stage == "st":
                    pe.wait_ge(rec_dve, 5 * q + 2)
                    M(b4[:, 2 * P:3 * P], kbt[:, b, 0, :], v_[:, c, 0:P], start=True, stop=False)
                    M(b4[:, 2 * P:3 * P], kbt[:, b, 1, :], nu[:], start=False, stop=True).then_inc(rec_pe, 1)
                    y = bank_for(("y", l, c))
                    for hh in range(2):
                        w = slice(64 * hh, 64 * hh + 64)
                        M(y[w, 0:CH], v_tok(0, hh), rkt(2 * hh), start=True, stop=False)
                        M(y[w, 0:CH], nu[:, w], rbt(2 * hh), start=False, stop=True)
                elif stage == "rhs1":
                    pe.wait_ge(rec_dve, 5 * q + 3)
                    for hh in range(2):
                        M(b4[:, 3 * P + 64 * hh:3 * P + 64 * hh + 64], akt(2 * hh + 1), v_tok(1, hh),
                          start=(hh == 0), stop=False, skip_group_check=True)
                    M(b4[:, 3 * P:4 * P], ar[:, b, 1, 0:CH], s0[:], start=False, stop=True, skip_group_check=True)\
                        .then_inc(rec_pe, 1)
                elif stage == "u1":
                    pe.wait_ge(rec_dve, 5 * q + 4)
                    for hh in range(2):
                        ins = M(b4[:, 64 * hh:64 * hh + 64], q_inv[:, b, 2 * hh + 1, :], rh[:, 64 * hh:64 * hh + 64],
                                start=True, stop=True)
                    ins.then_inc(rec_pe, 1)
                elif stage == "y":
                    y = lin[:, PLAN.uses["y", l, c][0] % 3, :]
                    M(y[:, CH:2 * CH], s0[:], ar[:, b, 1, CH:2 * CH], start=True, stop=False, skip_group_check=True)
                    pe.wait_ge(rec_dve, 5 * q + 5)
                    for hh in range(2):
                        w = slice(64 * hh, 64 * hh + 64)
                        M(y[w, CH:2 * CH], v_tok(1, hh), rkt(2 * hh + 1), start=False, stop=False,
                          skip_group_check=True)
                        ins = M(y[w, CH:2 * CH], nu[:, w], rbt(2 * hh + 1), start=False, stop=(hh == 1),
                                skip_group_check=True)
                    ins.then_inc(lin_filled, 1)

            def attention(l):
                base = MIX_AT[2 + l]
                ng = (1, 3)[l]
                norm(8 + 3 * l)
                half = base

                def finish_qk(g, c):
                    bank = bank_for(("ss", l, g, c))
                    p = PIECE["ss", l, g, c]
                    pe.wait_ge(squared, p + 1)
                    M(bank, head_w, pieces[:, p % 2, :, :], start=True, stop=True).then_inc(lin_filled, 1)
                    if l:
                        bank = bank_for(("rot", l, g, c))
                        pe.wait_ge(small_loaded, 160 + 96)
                        wait_emptied(pe, ("qk", l, g, c))
                        M(bank, rope_m[:], qkg[:, (DT * g + c) % 2, :, :], start=True, stop=True).then_inc(lin_filled, 1)

                for g in range(ng):
                    for c in range(DT):
                        two_tiles(half, ("qk", l, g, c), (HH, HH), h_wait(8 + 3 * l) if g == 0 and c == 0 else None)
                        half += 2
                        if c:
                            finish_qk(g, c - 1)
                        if c % 2:
                            tokens_major(half, ("v", l, g, c // 2), 2 * P)
                            half += 2
                    finish_qk(g, DT - 1)
                if l == 0:
                    tokens_major(half, ("f", 0), HEADS)
                    pe.wait_ge(small_loaded, 160 + 48)
                wait_emptied(pe, ("v", l, ng - 1, 3))

                def logits_of(hd):
                    c, w = hd // 2, slice(64 * (hd % 2), 64 * (hd % 2) + 64)
                    pe.wait_ge(qk_ready, DT * (ng - 1 + l) + c + 1)
                    if hd:
                        pe.wait_ge(logits_read, HEADS * l + hd)
                    if l == 0:
                        pe.wait_ge(lsb_ready, hd + 1)
                    for g in range(ng):
                        b = sv[:, g, :]
                        q_, kx = qk[:, g, 2 * c, :], qk[:, g, 2 * c + 1, :]
                        more = l == 0
                        ins = M(b[:, 0:P], q_[w, 0:P], kx[w, 0:P], start=True, stop=not more)
                        if more:
                            M(b[:, 0:P], ls_b[:, 0, :], cum_rhs[:, 0:P], start=False, stop=True)
                        ins = M(b[:, P:3 * P], q_[w, P:2 * P], kx[w, :], start=True, stop=not more,
                                skip_group_check=True)
                        if more:
                            M(b[:, P:3 * P], ls_b[:, 0, :], cum_rhs[:], start=False, stop=False, skip_group_check=True)
                            ins = M(b[:, 2 * P:3 * P], ls_b[:, 1, :], cum_rhs[:, 0:P], start=False, stop=True,
                                    skip_group_check=True)
                    ins.then_inc(logits_done, 1)

                def turn(hd):
                    pe.wait_ge(norm_ready, HEADS * l + hd + 1)
                    for g in range(ng):
                        m = hd if l == 0 else HEADS + GROUPS * hd + g
                        b = sv[:, 3 + m % 2, :]
                        if m >= 2:
                            pe.wait_ge(pt_ready, m - 1)
                        for i in range(3):
                            ins = nc.tensor.transpose(b[:, i * P:(i + 1) * P], logits[hd % 2][:, g, i * P:(i + 1) * P],
                                                      ident)
                        ins.then_inc(pt_done, 1)

                def values_of(hd):
                    c, hh = hd // 2, hd % 2
                    w = slice(64 * hh, 64 * hh + 64)
                    o = lin[:, PLAN.uses["o", l, c][0] % 3, :] if hh else bank_for(("o", l, c))
                    pe.wait_ge(pt_ready, hd + 1 if l == 0 else HEADS + GROUPS * (hd + 1))
                    vt = lambda g, j: vtok[:, g, j, hd * HD:(hd + 1) * HD]
                    probs = pt[hd % 2]
                    for g in range(ng):
                        M(o[w, 0:P], vt(g, 0), probs[:, g, 0:P], start=(g == 0), stop=(g == ng - 1))
                    for g in range(ng):
                        M(o[w, P:2 * P], vt(g, 0), probs[:, g, P:2 * P], start=(g == 0), stop=False)
                        ins = M(o[w, P:2 * P], vt(g, 1), probs[:, g, 2 * P:3 * P], start=False, stop=(g == ng - 1))
                    if hh:
                        ins.then_inc(lin_filled, 1)

                logits_of(0)
                logits_of(1)
                for hd in range(HEADS):
                    if hd + 2 < HEADS:
                        logits_of(hd + 2)
                    turn(hd)
                    if hd:
                        values_of(hd - 1)
                values_of(HEADS - 1)
                wait_emptied(pe, ("o", l, DT - 1))
                OO = (o_hi, o_lo)
                for d in range(4):
                    two_tiles(OUT_AT[2 + l] + 2 * d, ("out", 2 + l, d), (OO, OO))
                    early_sums(("out", 2 + l), d)

            pe.wait_ge(consts_loaded, 48)
            for i in range(4):
                norm_sums(0, i)
            for l in range(2):
                ffn(2 * l)
                rwkv(l)
                ffn(2 * l + 1)
            norm(6)
            for l in range(2):
                ffn(4 + 2 * l)
                attention(l)
                ffn(5 + 2 * l)


def constants():
    i = np.arange(P)
    const = np.zeros((P, NCONST), np.float32)

    def put(name, value):
        a, n = CONST[name]
        const[:, a:a + n] = value

    put("ident", np.eye(P))
    put("mean", 1.0 / D)
    put("head", i[:, None] // HD == i[None, :] // HD)
    mid = CH // 2 - 1
    put("tri", -DECAY_SCALE * ((i[:, None] <= np.arange(CH + 1)[None, :] - 1).astype(np.float64)
                               - (i[:, None] <= mid)))
    put("mask", np.concatenate([i[:, None] < i[None, :], i[:, None] <= i[None, :]], 1))
    below = (i[:, None] % 2 == 1) & (i[None, :] == i[:, None] - 1)
    put("neg2", -1.0 * below)
    put("neg2t", -1.0 * below.T)
    put("one", 1.0)
    put("norm_eps", NORM_EPS)
    put("ln_eps", LN_EPS)
    levels = np.zeros((P, 2, len(LEVELS), P), np.float32)
    for s, m in enumerate(LEVELS):
        b = (i[:, None] // m % 2 == 1) & (i[None, :] // m == i[:, None] // m - 1)
        levels[:, 0, s], levels[:, 1, s] = b, b.T
    rope = np.zeros((P, P), np.float32)
    for base in (0, HD):
        for f in range(8):
            rope[base + f + 8, base + f] = -1.0
            rope[base + f, base + f + 8] = 1.0
    cum = np.concatenate([i[:, None] <= i[None, :], np.ones((P, P), bool)], 1) * np.float32(-(HD ** 0.5))

    def allowed(window, dilation):
        t, s = np.arange(T)[:, None], np.arange(T)[None, :]
        ok = (s <= t) & ((t - s) % dilation == 0) & (t - s <= window)
        m = np.where(ok, 0.0, NEG).astype(np.float32)
        return np.concatenate([m[:P, :P], m[P:, :]], 1)

    fox = allowed(T, 1)
    dil = np.stack([allowed(w, d) for w, d in ((128, 1), (512, 4), (2048, 16))], 1)
    freq = np.float32(500000.0) ** (-(np.arange(8, dtype=np.float32) * np.float32(2.0) / np.float32(16)))
    inv = np.zeros((P, 1), np.float32)
    for base in (0, 8, HD, HD + 8):
        inv[base:base + 8, 0] = freq
    return {"const": const, "level_masks": levels, "rope_m": rope, "cum_rhs": cum.astype(np.float32),
            "fox_mask": fox, "dil_mask": np.ascontiguousarray(dil), "inv_freq": inv}


def kernel(**inputs):
    import concourse.bacc as bacc
    from concourse.bass_utils import run_bass_kernel_spmd

    a = {k: np.asarray(v) for k, v in inputs.items()}
    fixed = constants()

    def tiles(w):
        w = np.concatenate([w, np.zeros((D, -w.shape[1] % P), w.dtype)], 1)
        return w.reshape(DT, P, -1, P).transpose(2, 1, 0, 3)

    def units(pairs_):
        return [np.stack(p, 1).reshape(P, TPU * P) for p in pairs_]

    def down(w):
        w = w.reshape(FT, P, DT, P).transpose(1, 2, 0, 3).reshape(P, DOWN_UNITS, TPU * P)
        return list(w.transpose(1, 0, 2))

    def moving(w):
        w = np.concatenate([w, np.zeros((D, 2 * P - w.shape[1]), w.dtype)], 1)
        return w.reshape(DT, P, 2 * P).transpose(1, 0, 2).reshape(P, TPU * P)

    stream = []

    def ffn(gate, up, w_down):
        stream.extend(units(zip(tiles(gate), tiles(up))))
        stream.extend(down(w_down))

    for l in range(2):
        gu = a["ffn1_w_gu"][l]
        ffn(gu[:, :FF], gu[:, FF:], a["ffn1_w_down"][l])
        w = a["w_in_first"] if l == 0 else a["w_in_rest"][0]
        w = tiles(np.concatenate([w, np.zeros((D, 58 * P - w.shape[1]), w.dtype)], 1))
        pa, pb = tiles(a["w_proj_a"][l]), tiles(a["w_proj_b"][l])
        order = [(56, 57)] + [(32 + c, 40 + c) for c in range(8)] + [(48 + c, 49 + c) for c in range(0, 8, 2)]
        order += [(24 + c, 25 + c) for c in range(0, 8, 2)] + [(16 + c, 17 + c) for c in range(0, 8, 2)]
        stream.extend(units((w[m], w[n]) for m, n in order))
        stream.extend(units((w[n], w[8 + n]) for n in range(DT)))
        for t in (pa, pb):
            stream.extend(units((t[n], t[n + 1]) for n in range(0, DT, 2)))
        wo = tiles(a["w_out"][l])
        stream.extend(units((wo[n], wo[n + 1]) for n in range(0, 8, 2)))
        gu = a["ffn2_w_gu"][l]
        ffn(gu[:, :FF], gu[:, FF:], a["ffn2_w_down"][l])
    for l in range(2):
        ffn(a["ffn_w_gate_2"][l, 0], a["ffn_w_up_2"][l, 0], a["ffn_w_down_2"][l, 0])
        w_in, w_o = (a["fox_w_in_2"][0], a["fox_w_out_2"][0]) if l == 0 else (a["dil_w_in_2"][0], a["dil_w_out_2"][0])
        for g in range((1, 3)[l]):
            w = w_in[:, 3 * D * g:3 * D * (g + 1)]
            t = tiles(w[:, :2 * D])
            for s in range(4):
                stream.extend(units((t[c], t[8 + c]) for c in (2 * s, 2 * s + 1)))
                stream.append(moving(w[:, 2 * D + 256 * s:2 * D + 256 * (s + 1)]))
        if l == 0:
            stream.append(moving(w_in[:, 3 * D:]))
        wo = tiles(w_o)
        stream.extend(units((wo[n], wo[n + 1]) for n in range(0, 8, 2)))
        ffn(a["ffn_w_gate_2"][l, 1], a["ffn_w_up_2"][l, 1], a["ffn_w_down_2"][l, 1])

    column = lambda v: v.reshape(-1, P).T
    cols = np.zeros((P, NCOLS), np.float32)

    def put(key, v):
        n = v.shape[-1] // P
        cols[:, COL[key]:COL[key] + n] = column(v)

    for l in range(2):
        for name, key in (("ffn1_norm",) * 2, ("mix_norm",) * 2, ("ffn2_norm",) * 2, ("ln_g", "sgu_ln_g"),
                          ("ln_b", "sgu_ln_b"), ("a0", "rwkv_a0"), ("k_k", "rwkv_k_k"), ("k_a", "rwkv_k_a"),
                          ("gn_g", "rwkv_gn_g"), ("gn_b", "rwkv_gn_b")):
            put((name, l), a[key][l])
        put(("r_k", l), a["rwkv_r_k"][l].reshape(-1))
        mu = a["mu_first"] if l == 0 else a["mu_rest"][0]
        put(("mu", l), np.concatenate([mu, np.zeros(26 * P - mu.shape[0], mu.dtype)]))
    put(("v0", 1), a["rwkv_v0"][0])
    put("final_norm", a["final_norm"])
    put("norm_g", a["norm_g_2"].reshape(-1))
    put("c", a["c_2"][0])
    twice = lambda v: np.concatenate([v, v])
    put("fox_g", np.concatenate([twice(a["fox_q_g_2"][0]), twice(a["fox_k_g_2"][0])]))
    put("dil_g", np.concatenate([twice(a[n][0][g]) for g in range(3) for n in ("dil_q_g_2", "dil_k_g_2")]))
    cols[:, COL["inv_freq"]:COL["inv_freq"] + 1] = fixed.pop("inv_freq")

    v2 = a["rwkv_v2"][0]
    arrays = {
        "x": a["x"][0].T.reshape(DT, P, T).transpose(1, 0, 2),
        "stream": np.stack(stream),
        "mod_w": a["mod_w_2"].reshape(2, DT, P, 36, 2 * P).transpose(0, 3, 2, 1, 4).reshape(72, P, TPU * P),
        "mod_b": column(a["mod_b_2"].reshape(-1)),
        "cols": cols,
        "w2a2": np.concatenate([a["rwkv_w2"], a["rwkv_a2"]], 1),
        "v2": np.stack([v2, v2]),
        "w0": a["rwkv_w0"],
        "bs": a["sgu_b_s"].reshape(2, -1),
        "ws_t": a["sgu_w_s"].transpose(0, 3, 1, 2),
        "b_f": a["fox_b_f_2"][0],
        "positions": a["positions_2"][0],
        **fixed,
    }
    arrays = {k: np.ascontiguousarray(v) for k, v in arrays.items()}
    nc = bacc.Bacc("TRN2", target_bir_lowering=False, num_devices=1)
    src = {k: nc.dram_tensor(f"in_{k}", v.shape, mybir.dt.from_np(v.dtype), kind="ExternalInput").ap()
           for k, v in arrays.items()}
    out = nc.dram_tensor("out", (P, DT, T), F32, kind="ExternalOutput").ap()
    build_program(nc, src, out)
    r = run_bass_kernel_spmd(nc, [{f"in_{k}": v for k, v in arrays.items()}], core_ids=[0])
    y = r.results[0]["out"]
    return np.ascontiguousarray(y.transpose(1, 0, 2).reshape(D, T).T)[None]
```
